# Optimizing a Trainium2 kernel written in Bass

```python
import jax, jax.numpy as jnp
from jax import lax
import numpy as np

D_MODEL = 2048
BATCH = 1
SEQ = 512
DEPTH = 1
DEC_BATCH = 1
DEC_SEQ = 32
PAST_LEN = 512

CHUNK = 64
CONV_DIM = D_MODEL // 2
CONV_WIDTH = 31
GLA_HEADS = 4
GLA_DK = D_MODEL // 16
GLA_DV = D_MODEL // 8
GLA_RANK = 16
GLA_TAU = 16.0
QK_DIM = GLA_HEADS * GLA_DK
V_DIM = GLA_HEADS * GLA_DV
IN_COLS = 2 * CONV_DIM + 2 * QK_DIM + 2 * V_DIM + GLA_RANK
PEER_HEADS = 8
PEER_NKEYS = 128
PEER_TOPK = 16
PEER_DKEY = 256
PEER_BLOCK = 128
N_EXPERTS = PEER_NKEYS * PEER_NKEYS
LN_EPS = 1e-5
ALPHA = (2.0 * DEPTH) ** 0.25
BETA = (8.0 * DEPTH) ** -0.25

kernel_name = 'hymba_conformer_gla_peer_stream'

def layer_norm(x, g, b):
    xf = x.astype(jnp.float32)
    mu = jnp.mean(xf, axis=-1, keepdims=True)
    var = jnp.mean(jnp.square(xf - mu), axis=-1, keepdims=True)
    return ((xf - mu) * lax.rsqrt(var + LN_EPS) * g + b).astype(x.dtype)

def split_in(z):
    sizes = (CONV_DIM, CONV_DIM, QK_DIM, QK_DIM, V_DIM, V_DIM, GLA_RANK)
    offs = [int(o) for o in np.cumsum(sizes)[:-1]]
    return jnp.split(z, offs, axis=-1)

def conv_mixer(a, gate, conv_buf, conv_w, conv_b, ln_g, ln_b):
    u = a * jax.nn.sigmoid(gate)
    ext = jnp.concatenate([conv_buf.astype(u.dtype), u], axis=1)
    y = lax.conv_general_dilated(ext, conv_w[:, None, :].astype(u.dtype), window_strides=(1,),
                                 padding='VALID', dimension_numbers=('NWC', 'WIO', 'NWC'),
                                 feature_group_count=CONV_DIM) + conv_b
    y = jax.nn.silu(layer_norm(y, ln_g, ln_b))
    return y, ext[:, -(CONV_WIDTH - 1):]

def gla_scan(q, k, v, log_a, s0):
    B, H, L, _ = q.shape
    n = -(-L // CHUNK)
    pad = n * CHUNK - L
    padf = lambda t: jnp.pad(t, ((0, 0), (0, 0), (0, pad), (0, 0)))
    to_chunks = lambda t: jnp.moveaxis(padf(t).reshape(B, H, n, CHUNK, t.shape[-1]), 2, 0)
    qc, kc, vc, ac = to_chunks(q), to_chunks(k), to_chunks(v), to_chunks(log_a)
    causal = jnp.tril(jnp.ones((CHUNK, CHUNK), dtype=bool))

    def step(S, inp):
        qb, kb, vb, ab = inp
        bcum = jnp.cumsum(ab, axis=2)
        diff = bcum[:, :, :, None, :] - bcum[:, :, None, :, :]
        decay = jnp.exp(jnp.where(causal[:, :, None], diff, -jnp.inf))
        scores = jnp.einsum('bhtk,bhsk,bhtsk->bhts', qb, kb, decay)
        o = (jnp.einsum('bhts,bhsv->bhtv', scores, vb)
             + jnp.einsum('bhtk,bhkv->bhtv', qb * jnp.exp(bcum), S))
        b_last = bcum[:, :, -1:, :]
        S_new = (jnp.exp(b_last[:, :, 0, :])[..., None] * S
                 + jnp.einsum('bhsk,bhsv->bhkv', kb * jnp.exp(b_last - bcum), vb))
        return S_new, o

    S, o = lax.scan(step, s0, (qc, kc, vc, ac))
    o = jnp.moveaxis(o, 0, 2).reshape(B, H, n * CHUNK, -1)[:, :, :L]
    return o, S

def gla_mixer(q, k, v, g, f_lr, s0, gate_w, gate_b, norm_g):
    B, L, _ = q.shape
    heads = lambda t, d: t.reshape(B, L, GLA_HEADS, d).transpose(0, 2, 1, 3).astype(jnp.float32)
    log_a = jax.nn.log_sigmoid((f_lr @ gate_w + gate_b).astype(jnp.float32)) / GLA_TAU
    o, S = gla_scan(heads(q, GLA_DK) * (GLA_DK ** -0.5), heads(k, GLA_DK), heads(v, GLA_DV),
                    heads(log_a, GLA_DK), s0.astype(jnp.float32))
    o = o * lax.rsqrt(jnp.mean(o * o, axis=-1, keepdims=True) + LN_EPS)
    o = o.transpose(0, 2, 1, 3).reshape(B, L, V_DIM) * norm_g
    return (o * jax.nn.silu(g.astype(jnp.float32))).astype(q.dtype), S.astype(s0.dtype)

def peer(x, w_query, sub_keys, u_table, v_table):
    B, L, D = x.shape
    T = B * L
    n = -(-T // PEER_BLOCK)
    tp = n * PEER_BLOCK
    xt = jnp.pad(x.reshape(T, D), ((0, tp - T), (0, 0)))
    q = (xt @ w_query).reshape(tp, PEER_HEADS, 2, PEER_DKEY // 2)
    s = jnp.einsum('thpc,hpnc->thpn', q, sub_keys).astype(jnp.float32)
    sv, si = lax.top_k(s, PEER_TOPK)
    cand = sv[:, :, 0, :, None] + sv[:, :, 1, None, :]
    cid = si[:, :, 0, :, None] * PEER_NKEYS + si[:, :, 1, None, :]
    best, pos = lax.top_k(cand.reshape(tp, PEER_HEADS, PEER_TOPK * PEER_TOPK), PEER_TOPK)
    ids = jnp.take_along_axis(cid.reshape(tp, PEER_HEADS, PEER_TOPK * PEER_TOPK), pos, axis=-1)
    gates = jax.nn.softmax(best, axis=-1)

    def block(args):
        xb, idb, gb = args
        h = jax.nn.gelu(jnp.einsum('td,thkd->thk', xb, u_table[idb]), approximate=False)
        w = (gb * h).astype(xb.dtype)
        return jnp.einsum('thk,thkd->td', w, v_table[idb]).astype(xb.dtype)

    out = lax.map(block, (xt.reshape(n, PEER_BLOCK, D),
                          ids.reshape(n, PEER_BLOCK, PEER_HEADS, PEER_TOPK),
                          gates.reshape(n, PEER_BLOCK, PEER_HEADS, PEER_TOPK)))
    return out.reshape(tp, D)[:T].reshape(B, L, D)

def trunk_layer(x, conv_buf, gla_state, w_in, conv_w, conv_b, conv_ln_g, conv_ln_b,
                gla_gate_w, gla_gate_b, gla_norm_g, w_out, ln1_g, ln1_b,
                peer_w_query, peer_sub_keys, peer_u, peer_v, ln2_g, ln2_b):
    z = x @ w_in
    c_val, c_gate, q, k, v, g, f_lr = split_in(z)
    y_conv, conv_new = conv_mixer(c_val, c_gate, conv_buf, conv_w, conv_b, conv_ln_g, conv_ln_b)
    y_gla, gla_new = gla_mixer(q, k, v, g, f_lr, gla_state, gla_gate_w, gla_gate_b, gla_norm_g)
    mix = jnp.concatenate([y_conv, y_gla.astype(y_conv.dtype)], axis=-1) @ w_out
    x = layer_norm(ALPHA * x + mix, ln1_g, ln1_b)
    x = layer_norm(ALPHA * x + peer(x, peer_w_query, peer_sub_keys, peer_u, peer_v), ln2_g, ln2_b)
    return x, conv_new, gla_new

def setup_inputs(seed: int = 0) -> dict:
    key = jax.random.key(seed)
    ks = jax.random.split(key, 24)
    nrm = lambda i, shape, s: jax.random.normal(ks[i], shape, jnp.float32) * s
    dsc = D_MODEL ** -0.5
    w_in = jnp.concatenate([
        nrm(0, (DEPTH, D_MODEL, CONV_DIM), dsc * BETA),
        nrm(1, (DEPTH, D_MODEL, CONV_DIM), dsc),
        nrm(2, (DEPTH, D_MODEL, 2 * QK_DIM), dsc),
        nrm(3, (DEPTH, D_MODEL, V_DIM), dsc * BETA),
        nrm(4, (DEPTH, D_MODEL, V_DIM + GLA_RANK), dsc),
    ], axis=-1)
    return {
        'x_prompt': nrm(5, (BATCH, SEQ, D_MODEL), 1.0),
        'x_sample': nrm(6, (DEC_BATCH, DEC_SEQ, D_MODEL), 1.0),
        'state_conv': nrm(7, (DEPTH, DEC_BATCH, CONV_WIDTH - 1, CONV_DIM), 0.5),
        'state_gla': nrm(8, (DEPTH, DEC_BATCH, GLA_HEADS, GLA_DK, GLA_DV), 0.5),
        'w_in': w_in,
        'conv_w': nrm(9, (DEPTH, CONV_WIDTH, CONV_DIM), CONV_WIDTH ** -0.5),
        'conv_b': nrm(10, (DEPTH, CONV_DIM), 0.02),
        'conv_ln_g': 1.0 + nrm(11, (DEPTH, CONV_DIM), 0.02),
        'conv_ln_b': nrm(12, (DEPTH, CONV_DIM), 0.02),
        'gla_gate_w': nrm(13, (DEPTH, GLA_RANK, QK_DIM), GLA_RANK ** -0.5),
        'gla_gate_b': 1.0 + nrm(14, (DEPTH, QK_DIM), 0.1),
        'gla_norm_g': 1.0 + nrm(15, (DEPTH, V_DIM), 0.02),
        'w_out': nrm(16, (DEPTH, D_MODEL, D_MODEL), dsc * BETA),
        'ln1_g': 1.0 + nrm(17, (DEPTH, D_MODEL), 0.02),
        'ln1_b': nrm(18, (DEPTH, D_MODEL), 0.02),
        'peer_w_query': nrm(19, (DEPTH, D_MODEL, PEER_HEADS * PEER_DKEY), dsc),
        'peer_sub_keys': nrm(20, (DEPTH, PEER_HEADS, 2, PEER_NKEYS, PEER_DKEY // 2), (PEER_DKEY // 2) ** -0.5),
        'peer_u': nrm(21, (DEPTH, N_EXPERTS, D_MODEL), dsc),
        'peer_v': nrm(22, (DEPTH, N_EXPERTS, D_MODEL), BETA),
        'ln2_g': 1.0 + nrm(23, (DEPTH, D_MODEL), 0.02),
        'ln2_b': jax.random.normal(jax.random.fold_in(key, 99), (DEPTH, D_MODEL), jnp.float32) * 0.02,
    }

def reference(x_prompt, x_sample, state_conv, state_gla, w_in, conv_w, conv_b, conv_ln_g, conv_ln_b,
              gla_gate_w, gla_gate_b, gla_norm_g, w_out, ln1_g, ln1_b,
              peer_w_query, peer_sub_keys, peer_u, peer_v, ln2_g, ln2_b):
    yp, ys = x_prompt, x_sample
    conv_p, gla_p, conv_s, gla_s = [], [], [], []
    for i in range(DEPTH):
        lp = (w_in[i], conv_w[i], conv_b[i], conv_ln_g[i], conv_ln_b[i],
              gla_gate_w[i], gla_gate_b[i], gla_norm_g[i], w_out[i], ln1_g[i], ln1_b[i],
              peer_w_query[i], peer_sub_keys[i], peer_u[i], peer_v[i], ln2_g[i], ln2_b[i])
        zero_conv = jnp.zeros((x_prompt.shape[0], CONV_WIDTH - 1, CONV_DIM), x_prompt.dtype)
        zero_gla = jnp.zeros((x_prompt.shape[0], GLA_HEADS, GLA_DK, GLA_DV), state_gla.dtype)
        yp, cp, gp = trunk_layer(yp, zero_conv, zero_gla, *lp)
        ys, cs, gs = trunk_layer(ys, state_conv[i], state_gla[i], *lp)
        conv_p.append(cp)
        gla_p.append(gp)
        conv_s.append(cs)
        gla_s.append(gs)
    return (yp, ys, jnp.stack(conv_p), jnp.stack(gla_p), jnp.stack(conv_s), jnp.stack(gla_s))


_drawn_inputs = setup_inputs


def setup_inputs(seed=0):
    import zlib

    import numpy as np

    out = dict(_drawn_inputs(seed))
    spreads = {}
    factors = {'conv_ln_g': 3.089,
     'conv_ln_b': 3.152,
     'gla_norm_g': 3.164,
     'ln2_g': 2.882,
     'ln2_b': 2.846}
    for name, (base, spread) in spreads.items():
        noise = np.random.default_rng([zlib.crc32(name.encode()), seed]).standard_normal(out[name].shape)
        drawn = base * np.exp(spread * noise) if base else spread * noise
        out[name] = __import__('jax').numpy.asarray(drawn.astype(out[name].dtype))
    for name, factor in factors.items():
        out[name] = (out[name] * factor).astype(out[name].dtype)
    return out
```

```python
from contextlib import ExitStack

import numpy as np

import concourse.bass as bass
from concourse import mybir
from concourse.alu_op_type import AluOpType as ALU

F32 = mybir.dt.float32
F32R = mybir.dt.float32r
U32 = mybir.dt.uint32
I32 = mybir.dt.int32
ACT = mybir.ActivationFunctionType
AX = mybir.AxisListType.X

P = 128
TP, TS = 512, 32
T = TP + TS
TH = T // 2
D = 2048
KT = D // P
CONV, CW = 1024, 31
CT = CONV // P
NPAD = CW - 1
EXT = NPAD + TP + NPAD + TS
YL = EXT - NPAD
HEADS, DK, DV, RANK = 4, 128, 256, 16
TAU = 16.0
CH = 64
NC = TP // CH
PH, NKEY, TOPK = 8, 128, 16
TT = 5
EG = 8
NG = NKEY // EG
GC = 32
NGC = T // GC
EPS = 1e-5
ALPHA = 2.0 ** 0.25
AHEAD = 2
LEVELS = (32, 16, 8, 4, 2, 1)


class Counts:

    def __init__(self, eng):
        self.eng, self.base, self.loops = eng, {}, []

    def value(self, sem):
        v = self.base.get(sem.name, 0)
        for reg, per in self.loops:
            if per.get(sem.name, 0):
                v = reg * per[sem.name] + v
        return v

    def inc(self, ins, sem):
        ins.then_inc(sem, 1)
        self.base[sem.name] = self.base.get(sem.name, 0) + 1

    def done(self, ins, sem):
        self.inc(ins, sem)
        self.eng.wait_ge(sem, self.value(sem))

    def loop(self, n, per):
        return _Loop(self, n, per)


class _Loop:
    def __init__(self, c, n, per):
        self.c, self.n, self.per = c, n, {s.name: k for s, k in per.items()}

    def __enter__(self):
        self.fori = self.c.eng.Fori(0, self.n)
        reg = self.fori.__enter__()
        self.before = dict(self.c.base)
        self.c.loops.append((reg, self.per))
        return reg

    def __exit__(self, *e):
        self.c.loops.pop()
        if e[0] is None:
            for name in set(self.c.base) | set(self.per):
                got = self.c.base.get(name, 0) - self.before.get(name, 0)
                assert got == self.per.get(name, 0), (name, got, self.per.get(name, 0))
                self.c.base[name] = self.before.get(name, 0) + self.n * got
        return self.fori.__exit__(*e)


def program(nc, xT, w_in, w_f, w_out, w_q, u_t, v_t, conv_state, conv_w, conv_vec, gla_state,
            gate_w, gate_b, norm_g, ln_vec, sub_keys, ident_in, iota_in, masks_in,
            y_out, conv_p, conv_s, gla_p, gla_s, g_dram):
    ctx = ExitStack()
    with ctx:
        lo0 = -(-nc.sbuf_base // 32) * 32

        def at(name, shape, dt, off):
            return nc.alloc_sbuf_tensor_at(name, shape, dt, offset=lo0 + off)

        def sem(name):
            return ctx.enter_context(nc.semaphore(name))

        ROW = T * 4
        X0, X1 = 0, KT * ROW
        M0, M1 = 2 * KT * ROW, 3 * KT * ROW
        R0 = 4 * KT * ROW
        TILE = KT * P * 4
        C0 = R0 + 6 * TILE
        S0 = C0 + 2656
        xh = at("xh", [P, KT, T], F32R, X0)
        xl = at("xl", [P, KT, T], F32R, X1)
        r1 = at("r1", [P, KT, T], F32, X0)
        mh = at("mh", [P, KT, T], F32R, M0)
        ml = at("ml", [P, KT, T], F32R, M1)
        x_raw = at("x_raw", [P, KT, T], F32, M0)
        wraw = at("wraw", [P, 2, KT, P], F32, R0)
        wh = at("wh", [P, 2, KT, P], F32R, R0 + 2 * TILE)
        wl = at("wl", [P, 2, KT, P], F32R, R0 + 4 * TILE)
        ident = at("ident", [P, P], F32, C0)
        ones = at("ones", [P, P], F32, C0 + 512)
        iota = at("iota", [P, P], F32, C0 + 1024)
        cvec = at("cvec", [P, 3, CT], F32, C0 + 1536)
        gb = at("gb", [P, HEADS], F32, C0 + 1632)
        ng = at("ng", [P, HEADS * 2], F32, C0 + 1664)
        lvec = at("lvec", [P, 4, KT], F32, C0 + 1696)
        wf_raw = at("wf_raw", [P, KT, RANK], F32, M1)
        z = at("z", [P, 6, T], F32, M0)
        bcum = at("bcum", [P, T], F32, M0 + 6 * ROW)
        keep = at("keep", [P, T], F32, M0 + 7 * ROW)
        state = at("state", [P, NC + 1, DV], F32, M1)
        kdN = at("kdN", [CH, NC + 1, P], F32, M1 + 9216)
        dist0 = at("dist0", [P, T], F32, M1 + 9216 + 4608)
        qe = [at(f"qe{u}", [P, T], F32, M0 + (14 + u) * ROW) for u in range(2)]
        ke = [at(f"ke{u}", [P, T], F32, M1 + (14 + u) * ROW) for u in range(2)]
        masks = at("masks", [CH, 7, CH], F32, S0)
        gw = at("gw", [RANK, HEADS, P], F32, S0 + 1792)
        flr = at("flr", [RANK, T], F32, S0 + 3840)
        vN = at("vN", [CH, NC + 1, DV], F32, S0 + 6016)
        scT = at("scT", [CH, NC + 1, CH], F32, S0 + 15232)
        dist1 = at("dist1", [P, T], F32, S0 + 17536)
        s_new = at("s_new", [P, DV], F32, S0 + 19712)
        cwt = at("cwt", [P, CT, CW], F32, S0 + 20768)
        dist = [dist0, dist1]
        stmp = at("stmp", [CH, NC + 1, CH], F32, M1 + 9216)
        cst = at("cst", [P, CT, NPAD], F32, M0)
        cpo = at("cpo", [P, 2, CT, NPAD], F32, M0 + 960)
        ext = at("ext", [P, EXT], F32, S0)
        sg = at("sg", [P, T], F32, S0 + 4864)
        yb = at("yb", [P, YL], F32, S0 + 7040)
        sum1 = at("sum1", [P, T], F32, S0 + 9344)
        sum2 = at("sum2", [P, T], F32, S0 + 11520)
        sq = at("sq", [P, T], F32, S0 + 13696)
        yf = at("yf", [P, CT, T], F32, M1)
        tmp = [at(f"tmp{u}", [P, T], F32, S0 + 15872 + u * ROW) for u in range(2)]
        qT = at("qT", [P, 2, T], F32, M0)
        skT = at("skT", [P, 2 * PH, P], F32, M0 + 2 * ROW)
        o = M1
        sc = at("sc", [P, 2, TT, P], F32, o); o += 2 * TT * P * 4
        scw = at("scw", [P, TT, P], F32, o); o += TT * P * 4
        cand = at("cand", [P, TT, 256], F32, o); o += TT * 1024
        candw = at("candw", [P, TT, 256], F32, o); o += TT * 1024
        oh = at("oh", [P, TT, 16, 16], F32, o); o += TT * 1024
        sv = at("sv", [P, 2, TT, 16], F32, o); o += 640
        si = at("si", [P, 2, TT, 16], U32, o); o += 640
        sif = at("sif", [P, 2, TT, 16], F32, o); o += 640
        bs = at("bs", [P, TT, 16], F32, o); o += 320
        pos = at("pos", [P, TT, 16], U32, o); o += 320
        pab = at("pab", [P, 2, TT, 16], U32, o); o += 640
        pabf = at("pabf", [P, 2, TT, 16], F32, o); o += 640
        assert o <= M1 + KT * ROW, o - M1
        picks = at("picks", [P, 3, TT, PH, 16], F32, S0)
        gsum = at("gsum", [P, TT * PH], F32, S0 + 7680)
        picksT = at("picksT", [P, 3, T], F32, S0 + 7840)
        oneA = at("oneA", [P, 2, 4, P], F32, S0 + 14368)
        oneB = at("oneB", [P, 2, 4, P], F32, M1)
        gst = at("gst", [P, 2, P, GC], F32, M0)
        W0h = at("W0h", [P, EG, T], F32R, M0)
        W0l = at("W0l", [P, EG, T], F32R, M0 + EG * ROW)
        acc = at("acc", [P, KT, T], F32, M1)
        gt = at("gt", [P, NGC, EG, GC], F32, S0)
        hb = [at(f"hb{u}", [P, T], F32, S0 + EG * ROW + u * ROW) for u in range(2)]
        fsum1 = at("fsum1", [P, T], F32, M0)
        fsum2 = at("fsum2", [P, T], F32, M0 + ROW)
        fsq = [at(f"fsq{u}", [P, T], F32, M0 + (2 + u) * ROW) for u in range(2)]

        ps = ctx.enter_context(nc.psum_tensor("ps", [P, 8, 512], F32))

        x_in = [sem(f"x_in{i}") for i in range(4)]
        consts_in, wf_in, keys_in = sem("consts_in"), sem("wf_in"), sem("sub_keys_in")
        w_in_s = [sem("w_slot0_in"), sem("w_slot1_in")]
        whi, wlo = sem("w_hi_split"), sem("w_lo_split")
        mm = sem("tile_mm_done")
        x_hi, x_lo = sem("x_hi_split"), sem("x_lo_split")
        f_mm, f_out, z_out, ones_set = sem("f_mm"), sem("f_out"), sem("z_out"), sem("ones_set")
        dve, act = sem("dve_step"), sem("act_step")
        gz_mm, soft, gz_ra, gz_rd = sem("gate_mm"), sem("softplus"), sem("gate_read_act"), sem("gate_read_dve")
        vt_mm, vt_out, kt_mm, kt_out = sem("v_turned"), sem("v_out"), sem("k_turned"), sem("k_out")
        dist_s, decay_s, qke, sc_mm, sc_out = (
            sem("distances"), sem("decays"), sem("qk_decayed"), sem("score_mm"), sem("score_out"))
        qb_s, kd_s, p_mm, p_out, o_mm, o_out, rs_mm, head_out = (
            sem("q_from_start"), sem("k_to_end"), sem("kv_mm"), sem("states"), sem("o_mm"), sem("o_out"),
            sem("rms_mm"), sem("head_done"))
        gs_in, st_out = sem("gla_state_in"), sem("gla_state_out")
        cst_in, cst_out = sem("conv_state_in"), sem("conv_state_out")
        sg_s, glu_s, yf_s, csq_s, csq_u, cst_s, cmean_mm, ycn_s, ysilu_s, mix_s = (
            sem("gate_sigmoid"), sem("glu_done"), sem("conv_done"), sem("conv_square"), sem("conv_square_used"),
            sem("conv_sums"), sem("conv_mean_mm"), sem("conv_normed"), sem("conv_silu"), sem("mix_ready"))
        r_s, rsq_s, rsq_u, rst_s, rmean_mm, x2_s, sc_set = (
            sem("residual_ready"), sem("residual_square"), sem("residual_square_used"), sem("norm1_sums"),
            sem("norm1_mean_mm"), sem("x2_ready"), sem("score_pad_set"))
        inv_s, root_s = sem("inverse_variance"), sem("inverse_deviation")
        q_out, s_mm, s_out, topk_s, gd_s, ge_s, picks_s, pt_mm, pt_out = (
            sem("q_out"), sem("key_scores"), sem("key_scores_out"), sem("head_picked"), sem("gate_diff"),
            sem("gate_exp"), sem("picks_ready"), sem("picks_turned"), sem("picks_turned_out"))
        oneh, g_mm, g_out = sem("one_hots"), sem("g_mm"), sem("g_out")
        g_st = [sem("g_stored0"), sem("g_stored1")]
        g_in = sem("g_group_in")
        h_out, w_s, y_add, acc_set = sem("gelu_out"), sem("w_ready"), sem("y_added"), sem("acc_set")
        n2_sq, n2_used, n2_st, n2_mm, n2_out, y_st = (
            sem("norm2_square"), sem("norm2_square_used"), sem("norm2_sums"), sem("norm2_mean_mm"),
            sem("norm2_out"), sem("y_stored"))

        NZ, NCV, NO, NQ = 6 * HEADS, 2 * CT, KT, 2 * PH
        A_CONV, A_OUT, A_Q, A_DENSE = NZ, NZ + NCV, NZ + NCV + NO, NZ + NCV + NO + NQ
        PER_G = EG + KT

        halves = [slice(h * TH, (h + 1) * TH) for h in range(2)]
        chunks = [(c, c * CH, CH) for c in range(NC)] + [(NC, TP, TS)]

        def parts(a):
            return a.rearrange("p (h t) -> p h t", h=2)

        def zr(u):
            return ps[:, 2 * u:2 * u + 2, 0:TH]

        def yr(u):
            return ps[:, 4 + 2 * u:6 + 2 * u, 0:TH]

        def f(ap):
            return ap.bitcast(F32)

        block = ctx.enter_context(nc.Block())

        @block.sync
        def _(sp):
            def load(dst, src, s):
                sp.dma_start(dst, src).then_inc(s, 16)

            def tile(src, u):
                load(wraw[:, u], src, w_in_s[u])

            def pairs(w):
                return w.rearrange("(n u) p k c -> n u p k c", u=2)

            load(x_raw[:, 0:4], xT[:, 0:4], x_in[0])
            load(wf_raw[:], w_f, wf_in)
            tile(pairs(w_in)[0, 0], 0)
            for i in range(1, 4):
                load(x_raw[:, 4 * i:4 * i + 4], xT[:, 4 * i:4 * i + 4], x_in[i])
            tile(pairs(w_in)[0, 1], 1)
            for dst, src in ((ident, ident_in), (iota, iota_in), (cvec, conv_vec), (gb, gate_b), (ng, norm_g),
                             (lvec, ln_vec), (masks, masks_in), (gw, gate_w), (cwt, conv_w)):
                load(dst[:], src, consts_in)

            def stream(src, n0, i0, i1):
                s = pairs(src)
                with sp.Fori(0, i1 - i0) as i:
                    for u in range(2):
                        sp.wait_ge(wlo, i * 2 + (n0 + u - 1))
                        tile(s[bass.ds(i + i0, 1), u].rearrange("o p k c -> (o p) k c"), u)

            stream(w_in, 2, 1, (NZ + NCV) // 2)
            stream(w_out, A_OUT, 0, NO // 2)
            s = pairs(w_q)
            for u in range(2):
                sp.wait_ge(wlo, A_Q + u - 1)
                tile(s[0, u], u)
            sp.wait_ge(mm, A_Q)
            load(skT[:], sub_keys, keys_in)
            stream(w_q, A_Q + 2, 1, NQ // 2)
            us = u_t.rearrange("(g n u) p k c -> g n u p k c", u=2, n=EG // 2)
            vs = v_t.rearrange("(g n u) p k c -> g n u p k c", u=2, n=EG // 2)
            gsrc = g_dram.rearrange("c j (g e) t -> g j c (e t)", e=EG)
            sp.wait_ge(g_st[0], 16 * ((NGC + 1) // 2))
            sp.wait_ge(g_st[1], 16 * (NGC // 2))
            with sp.Fori(0, NG) as g:
                sp.wait_ge(w_s, g * EG + AHEAD)
                load(gt[:].rearrange("p c e t -> p c (e t)"),
                     gsrc[bass.ds(g, 1)].rearrange("o j c q -> (o j) c q"), g_in)
                for a, src in enumerate((us, vs)):
                    with sp.Fori(0, EG // 2) as i:
                        for u in range(2):
                            sp.wait_ge(wlo, g * (2 * EG) + (i * 2 + (A_DENSE + a * EG + u - 1)))
                            t = src[bass.ds(g, 1), bass.ds(i, 1), u]
                            tile(t.rearrange("o q p k c -> (o q p) k c"), u)

        @block.gpsimd
        def _(pool):
            nc.gpsimd.memset(ones[:], 1.0).then_inc(ones_set, 1)

            def lo(n, u, freed):
                pool.wait_ge(whi, n + 1)
                if freed is not None:
                    pool.wait_ge(mm, freed)
                nc.gpsimd.tensor_tensor(wl[:, u], wraw[:, u], f(wh[:, u]), ALU.subtract).then_inc(wlo, 1)

            for u in range(2):
                lo(u, u, None)
            with pool.Fori(1, A_DENSE // 2) as i:
                for u in range(2):
                    lo(i * 2 + u, u, i * 2 + (u - 1))
            with pool.Fori(0, NG) as g:
                n0, m0 = g * (2 * EG) + A_DENSE, g * PER_G + A_DENSE
                for u in range(2):
                    lo(n0 + u, u, m0 - 1 + u)
                with pool.Fori(1, EG // 2) as i:
                    for u in range(2):
                        lo(i * 2 + (n0 + u), u, i * 2 + (m0 + (u - 1)))
                for u in range(2):
                    lo(n0 + (EG + u), u, m0 + (EG - 1 + u))
                with pool.Fori(1, EG // 2) as i:
                    for u in range(2):
                        lo(i * 2 + (n0 + (EG + u)), u, i * 4 + (m0 + (EG + 2 * u - 2)))

        @block.tensor
        def _(pe):
            mat = nc.tensor.matmul

            def job(u, n, a, ah, al, out, waits, first_k=None):
                pe.wait_ge(wlo, n + 1)
                for s, v in waits:
                    pe.wait_ge(s, v)
                for k in range(KT):
                    if first_k:
                        first_k(k)
                    for w, m in ((wh, ah), (wh, al), (wl, ah)):
                        for h in range(2):
                            ins = mat(out[:, h], w[:, u, k], m[:, k, halves[h]],
                                      start=(k == 0 and w is wh and m is ah),
                                      stop=(k == KT - 1 and w is wl))
                ins.then_inc(mm, 1)

            pe.sem_inc(g_mm, AHEAD)
            pe.wait_ge(wf_in, 16)
            for k in range(KT):
                if k % 4 == 0:
                    pe.wait_ge(x_in[k // 4], 16)
                for h in range(2):
                    ins = mat(ps[0:RANK, 4 + h, 0:TH], wf_raw[:, k], x_raw[:, k, halves[h]],
                              start=(k == 0), stop=(k == KT - 1))
            ins.then_inc(f_mm, 1)

            def gla(h):
                q, k = z[:, 0], z[:, 1]
                pe.wait_ge(f_out, 1)
                pe.wait_ge(consts_in, 16 * 9)
                for i in range(2):
                    ins = mat(ps[:, 4 + i, 0:TH], gw[:, h], flr[:, halves[i]], start=True, stop=True)
                ins.then_inc(gz_mm, 1)
                pe.wait_ge(gz_ra, h + 1)
                pe.wait_ge(gz_rd, h + 1)
                pe.wait_ge(z_out, 6 * (h + 1))
                for c in range(NC):
                    for v in range(2):
                        col = (c % 2) * DV + v * P
                        ins = nc.tensor.transpose(ps[0:CH, 4 + c // 2, col:col + P],
                                                  z[:, 2 + v, c * CH:(c + 1) * CH], ident[:])
                ins.then_inc(vt_mm, 1)
                pe.wait_ge(vt_out, 2 * h + 1)
                for v in range(2):
                    ins = nc.tensor.transpose(ps[0:TS, 4, v * P:v * P + P], z[:, 2 + v, TP:T], ident[:])
                ins.then_inc(vt_mm, 1)
                for l in range(7):
                    b = 4 + 2 * (l % 2)
                    a, m = (ke[l % 2], qe[l % 2]) if l < 6 else (z[:, 1], z[:, 0])
                    if l < 6:
                        pe.wait_ge(qke, 6 * h + l + 1)
                    if l == 0:
                        pe.wait_ge(vt_out, 2 * h + 2)
                    if l >= 2:
                        pe.wait_ge(sc_out, 7 * h + l - 1)
                    for c, t0, n in chunks:
                        if c == NC and l == 0:
                            continue
                        bank, col = (b, c * CH) if c < NC else (b + 1, 0)
                        ins = mat(ps[0:n, bank, col:col + n], a[:, t0:t0 + n], m[:, t0:t0 + n],
                                  start=True, stop=True)
                    ins.then_inc(sc_mm, 1)
                pe.wait_ge(kd_s, h + 1)
                pe.wait_ge(sc_out, 7 * h + 7)
                for c, t0, n in chunks:
                    ins = nc.tensor.transpose(ps[0:n, 4 + c // 4, (c % 4) * P:(c % 4) * P + P],
                                              ke[0][:, t0:t0 + n], ident[:])
                ins.then_inc(kt_mm, 1)
                pe.wait_ge(kt_out, h + 1)
                for c in range(NC):
                    ins = mat(ps[:, 4 + c // 2, (c % 2) * DV:(c % 2 + 1) * DV], kdN[:, c], vN[:, c],
                              start=True, stop=True)
                ins.then_inc(p_mm, 1)
                pe.wait_ge(p_out, 2 * h + 1)
                mat(ps[:, 4, 0:DV], kdN[0:TS, NC], vN[0:TS, NC], start=True, stop=True).then_inc(p_mm, 1)
                pe.wait_ge(qb_s, h + 1)
                pe.wait_ge(p_out, 2 * h + 2)
                for v in range(2):
                    for c, t0, n in chunks:
                        o_ps = ps[:, 4 + v, t0:t0 + n] if c < NC else ps[:, 6, v * TS:(v + 1) * TS]
                        vs_ = slice(v * P, (v + 1) * P)
                        ins = mat(o_ps, vN[0:n, c, vs_], scT[0:n, c, 0:n], start=True, stop=(c == 0))
                        if c:
                            ins = mat(o_ps, state[:, c % NC, vs_], qe[1][:, t0:t0 + n], start=False, stop=True)
                ins.then_inc(o_mm, 1)
                pe.wait_ge(o_out, h + 1)
                for i in range(2):
                    for v in range(2):
                        ins = mat(ps[:, 4 + i, 0:TH], ones[:], ke[v][:, halves[i]], start=(v == 0), stop=(v == 1))
                ins.then_inc(rs_mm, 1)

            pe.wait_ge(x_lo, 4)
            pe.wait_ge(ones_set, 1)
            for h in range(HEADS):
                for j in range(6):
                    n = 6 * h + j
                    job(n % 2, n, xh, xh, xl, zr(n % 2), [(z_out, n - 1)] if n >= 2 else [])
                gla(h)

            with pe.Fori(0, CT) as c:
                job(0, c * 2 + A_CONV, xh, xh, xl, zr(0), [(z_out, NZ), (glu_s, c + 1)])
                job(1, c * 2 + (A_CONV + 1), xh, xh, xl, zr(1), [(sg_s, c + 1)])

            def mean_mm(s1, s2, wait, value, done):
                pe.wait_ge(wait, value)
                for j, s in enumerate((s1, s2)):
                    for i in range(2):
                        ins = mat(ps[:, 4 + 2 * j + i, 0:TH], ones[:], s[:, halves[i]], start=True, stop=True)
                ins.then_inc(done, 1)

            pe.wait_ge(head_out, HEADS)
            mean_mm(sum1, sum2, cst_s, 1, cmean_mm)

            def w_out_k(k):
                if k < CT:
                    pe.wait_ge(mix_s, k + 1)
            job(0, A_OUT, mh, mh, ml, zr(0), [(glu_s, CT + 1)], w_out_k)
            job(1, A_OUT + 1, mh, mh, ml, zr(1), [(sg_s, CT + 1)])
            with pe.Fori(1, NO // 2) as i:
                for u in range(2):
                    job(u, i * 2 + (A_OUT + u), mh, mh, ml, zr(u), [(r_s, i * 2 + (u - 1))])
            mean_mm(sum1, sum2, rst_s, 1, rmean_mm)

            def x2_k(k):
                pe.wait_ge(x2_s, k + 1)

            def q_job(u, n, first_k=None):
                job(u, n + A_Q, xh, xh, xl, zr(u), [(r_s, NO)] + ([] if first_k or isinstance(n, int) and n < 2 else [(q_out, n - 1)]),
                    first_k)

            def key_scores(u, n):
                pe.wait_ge(q_out, n + 1)
                if not (isinstance(n, int) and n < 2):
                    pe.wait_ge(s_out, n - 1)
                for tt in range(TT):
                    m = P if tt < 4 else TS
                    o_ps = ps[0:m, 4 + 2 * u, tt * P:tt * P + P] if tt < 4 else ps[0:m, 5 + 2 * u, 0:P]
                    key = skT[:, n] if isinstance(n, int) else skT[:, bass.ds(n, 1)].rearrange("p o c -> p (o c)")
                    ins = mat(o_ps, qT[:, u, tt * P:tt * P + m], key, start=True, stop=True)
                ins.then_inc(s_mm, 1)

            q_job(0, 0, x2_k)
            q_job(1, 1)
            pe.wait_ge(keys_in, 16)
            key_scores(0, 0)
            with pe.Fori(1, NQ // 2) as i:
                q_job(0, i * 2)
                key_scores(1, i * 2 - 1)
                q_job(1, i * 2 + 1)
                key_scores(0, i * 2)
            key_scores(1, NQ - 1)

            pe.wait_ge(picks_s, 1)
            pe.wait_ge(s_out, NQ)
            for a in range(3):
                for tt in range(TT):
                    m = P if tt < 4 else TS
                    src = picks[0:m, a, tt].rearrange("p h k -> p (h k)")
                    if a < 2:
                        dst = ps[:, 4 + 2 * a, tt * P:tt * P + m] if tt < 4 else ps[:, 5 + 2 * a, 0:m]
                    else:
                        dst = ps[:, 0, tt * P:tt * P + m] if tt < 4 else ps[:, 1, 0:m]
                    ins = nc.tensor.transpose(dst, src, ident[0:m, 0:m])
            ins.then_inc(pt_mm, 1)

            pe.wait_ge(pt_out, 1)
            with pe.Fori(0, T // 8) as i:
                for u in range(2):
                    pe.wait_ge(oneh, i * 2 + (u + 1))
                    pe.wait_ge(g_out, i * 2 + (u + 1))
                    for t in range(4):
                        ins = mat(ps[:, 4 + u, t * P:(t + 1) * P], oneB[:, u, t], oneA[:, u, t],
                                  start=True, stop=True)
                    ins.then_inc(g_mm, 1)

            pe.wait_ge(acc_set, 1)
            with pe.Fori(0, NG) as g:
                n0 = g * (2 * EG) + A_DENSE
                with pe.Fori(0, EG // 2) as i:
                    for u in range(2):
                        job(u, i * 2 + (n0 + u), xh, xh, xl, zr(u), [(h_out, g * EG + (i * 2 + (u + 1)))])
                with pe.Fori(0, EG // 2) as i:
                    for u in range(2):
                        n = i * 2 + (n0 + (EG + u))
                        pe.wait_ge(wlo, n + 1)
                        pe.wait_ge(w_s, g * EG + (EG + AHEAD))
                        for d in range(2):
                            pe.wait_ge(y_add, g * KT + (i * 4 + (2 * u + d + 1)))
                            for e in range(EG):
                                for w, m in ((wh, W0h), (wh, W0l), (wl, W0h)):
                                    for h in range(2):
                                        ins = mat(yr(d)[:, h], w[:, u, d * EG + e], m[:, e, halves[h]],
                                                  start=(e == 0 and w is wh and m is W0h),
                                                  stop=(e == EG - 1 and w is wl))
                            ins.then_inc(mm, 1)
            mean_mm(fsum1, fsum2, n2_st, 1, n2_mm)

        @block.scalar
        def _(a):
            C = Counts(a)
            go = nc.scalar.activation

            def hi(n, u, freed):
                a.wait_ge(w_in_s[u], n * 8 + (16 - 8 * u))
                if freed is not None:
                    a.wait_ge(mm, freed)
                go(wh[:, u], wraw[:, u], ACT.Copy).then_inc(whi, 1)

            a.sem_inc(g_out, AHEAD)
            a.sem_inc(h_out, AHEAD)
            a.sem_inc(sg_s, 1)
            for i in range(4):
                a.wait_ge(x_in[i], 16)
                go(xh[:, 4 * i:4 * i + 4], x_raw[:, 4 * i:4 * i + 4], ACT.Copy).then_inc(x_hi, 1)
            hi(0, 0, None)
            hi(1, 1, None)
            a.wait_ge(f_mm, 1)
            go(parts(flr[:]), ps[0:RANK, 4:6, 0:TH], ACT.Copy).then_inc(f_out, 1)
            a.wait_ge(consts_in, 16 * 9)

            def root(buf, n):
                a.wait_ge(inv_s, n + 1)
                go(buf[:], buf[:], ACT.Sqrt).then_inc(root_s, 1)

            def gla_state_in(h):
                a.dma_start(state[:, 0], gla_state[:, h]).then_inc(gs_in, 16)

            gla_state_in(0)

            def gla(h):
                a.wait_ge(gz_mm, h + 1)
                C.done(go(parts(qe[0][:]), yr(0), ACT.Abs, bias=gb[:, h:h + 1]), gz_ra)
                C.done(go(qe[0][:], qe[0][:], ACT.Exp, scale=-1.0), act)
                go(qe[0][:], qe[0][:], ACT.Ln, bias=1.0).then_inc(soft, 1)
                a.wait_ge(vt_mm, 2 * h + 1)
                go(vN[:, 0:NC].rearrange("p (b c) v -> p b (c v)", c=2), ps[0:CH, 4:8, :], ACT.Copy).then_inc(vt_out, 1)
                a.wait_ge(vt_mm, 2 * h + 2)
                go(vN[0:TS, NC], ps[0:TS, 4, 0:DV], ACT.Copy).then_inc(vt_out, 1)
                for l in range(6):
                    a.wait_ge(dist_s, 7 * h + l + 1)
                    n = TP if l == 0 else T
                    go(dist[l % 2][:, 0:n], dist[l % 2][:, 0:n], ACT.Exp, scale=1.0 / TAU).then_inc(decay_s, 1)
                a.wait_ge(sc_mm, 7 * h + 5)
                go(qe[0][:], bcum[:], ACT.Exp, scale=1.0 / TAU).then_inc(decay_s, 1)
                a.wait_ge(dist_s, 7 * h + 7)
                go(dist[0][:], dist[0][:], ACT.Exp, scale=1.0 / TAU).then_inc(decay_s, 1)
                a.wait_ge(kt_mm, h + 1)
                go(kdN[:, 0:NC].rearrange("p (b c) v -> p b (c v)", c=4), ps[0:CH, 4:6, :], ACT.Copy)
                go(kdN[0:TS, NC], ps[0:TS, 6, 0:P], ACT.Copy).then_inc(kt_out, 1)
                a.wait_ge(p_out, 2 * h + 2)
                a.dma_start(gla_p[:, h], state[:, NC]).then_inc(st_out, 16)
                a.dma_start(gla_s[:, h], s_new[:]).then_inc(st_out, 16)
                a.wait_ge(o_mm, h + 1)
                if h + 1 < HEADS:
                    gla_state_in(h + 1)
                for v in range(2):
                    go(z[:, 2 + v, 0:TP], ps[:, 4 + v, :], ACT.Copy)
                    go(ke[v][:, 0:TP], ps[:, 4 + v, :], ACT.Square)
                go(z[:, 2:4, TP:T], ps[:, 6, 0:2 * TS].rearrange("p (v t) -> p v t", v=2), ACT.Copy)
                for v in range(2):
                    ins = go(ke[v][:, TP:T], ps[:, 6, v * TS:(v + 1) * TS], ACT.Square)
                ins.then_inc(o_out, 1)
                root(qe[0], h)

            for h in range(HEADS):
                for j in range(6):
                    n = 6 * h + j
                    a.wait_ge(mm, n + 1)
                    if h:
                        a.wait_ge(head_out, h)
                    go(parts(z[:, j]), zr(n % 2), ACT.Silu if j >= 4 else ACT.Copy,
                       scale=DK ** -0.5 if j == 0 else 1.0).then_inc(z_out, 1)
                    hi(n + 2, n % 2, n + 1)
                gla(h)

            a.wait_ge(head_out, HEADS)
            a.dma_start(cst[:], conv_state).then_inc(cst_in, 16)
            with C.loop(CT, {}) as c:
                n0 = c * 2 + A_CONV
                a.wait_ge(mm, n0 + 1)
                hi(n0 + 2, 0, None)
                a.wait_ge(mm, n0 + 2)
                a.wait_ge(glu_s, c + 1)
                go(parts(sg[:]), zr(1), ACT.Sigmoid).then_inc(sg_s, 1)
                hi(n0 + 3, 1, None)
                a.wait_ge(yf_s, c + 1)
                a.wait_ge(csq_u, c + 1)
                go(sq[:], yf[:, bass.ds(c, 1)].rearrange("p o t -> p (o t)"), ACT.Square).then_inc(csq_s, 1)
            a.wait_ge(yf_s, CT)
            a.dma_start(conv_p, cpo[:, 0]).then_inc(cst_out, 16)
            a.dma_start(conv_s, cpo[:, 1]).then_inc(cst_out, 16)
            root(sum2, HEADS)
            for c in range(CT):
                a.wait_ge(ycn_s, c + 1)
                go(tmp[c % 2][:], tmp[c % 2][:], ACT.Silu).then_inc(ysilu_s, 1)

            with C.loop(NO // 2, {}) as i:
                for u in range(2):
                    n = i * 2 + u
                    a.wait_ge(mm, n + (A_OUT + 1))
                    hi(n + (A_OUT + 2), u, None)
                    a.wait_ge(r_s, n + 1)
                    a.wait_ge(rsq_u, n + 1)
                    go(sq[:], r1[:, bass.ds(n, 1)].rearrange("p o t -> p (o t)"), ACT.Square).then_inc(rsq_s, 1)

            root(sum2, HEADS + 1)
            a.wait_ge(sc_set, 1)

            def q_evict(u, n, hi_next):
                a.wait_ge(mm, n + (A_Q + 1))
                if not (isinstance(n, int) and n < 2):
                    a.wait_ge(s_mm, n - 1)
                go(parts(qT[:, u]), zr(u), ACT.Copy).then_inc(q_out, 1)
                if hi_next:
                    hi(n + (A_Q + 2), u, None)

            def score_evict(u, n):
                a.wait_ge(s_mm, n + 1)
                if not (isinstance(n, int) and n < 2):
                    a.wait_ge(topk_s, n - 1)
                go(sc[:, u, 0:4].rearrange("p q k -> p (q k)"), ps[:, 4 + 2 * u, :], ACT.Copy)
                go(sc[0:TS, u, 4], ps[0:TS, 5 + 2 * u, 0:P], ACT.Copy).then_inc(s_out, 1)

            q_evict(0, 0, True)
            q_evict(1, 1, True)
            score_evict(0, 0)
            with a.Fori(1, NQ // 2 - 1) as i:
                q_evict(0, i * 2, True)
                score_evict(1, i * 2 - 1)
                q_evict(1, i * 2 + 1, True)
                score_evict(0, i * 2)
            q_evict(0, NQ - 2, False)
            score_evict(1, NQ - 3)
            q_evict(1, NQ - 1, False)
            score_evict(0, NQ - 2)
            score_evict(1, NQ - 1)
            a.wait_ge(gd_s, 1)
            go(picks[:, 0], picks[:, 0], ACT.Exp).then_inc(ge_s, 1)
            a.wait_ge(pt_mm, 1)
            for j in range(3):
                b = 4 + 2 * j if j < 2 else 0
                go(picksT[:, j, 0:TP], ps[:, b, :], ACT.Copy)
                ins = go(picksT[:, j, TP:T], ps[:, b + 1, 0:TS], ACT.Copy)
            ins.then_inc(pt_out, 1)

            def g_chunk(c, v):
                if not isinstance(c, int) or c >= 2:
                    a.wait_ge(g_st[v], (c - v) * 8)
                for q in range(GC // 4):
                    a.wait_ge(g_mm, c * (GC // 4) + (q + 1 + AHEAD))
                    go(gst[:, v, :, 4 * q:4 * q + 4].rearrange("p i t -> p t i"),
                       ps[:, 4 + q % 2, :].rearrange("p (t i) -> p t i", t=4), ACT.Copy).then_inc(g_out, 1)
                a.wait_ge(g_out, c * (GC // 4) + (GC // 4 + AHEAD))
                dst = g_dram[c] if isinstance(c, int) else g_dram[bass.ds(c, 1)].rearrange("o j i t -> (o j) i t")
                a.dma_start(dst, gst[:, v]).then_inc(g_st[v], 16)

            for v in range(2):
                g_chunk(v, v)
            with a.Fori(1, NGC // 2) as i:
                for v in range(2):
                    g_chunk(i * 2 + v, v)
            g_chunk(NGC - 1, 0)

            with a.Fori(0, NG) as g:
                n0, m0 = g * (2 * EG) + A_DENSE, g * PER_G + A_DENSE
                for u in range(2):
                    hi(n0 + u, u, m0 - 1 + u)

                def gelu(i, u):
                    a.wait_ge(mm, i * 2 + (m0 + (u + 1)))
                    a.wait_ge(w_s, g * EG + (i * 2 + (u + 1)))
                    go(parts(hb[u][:]), zr(u), ACT.Gelu).then_inc(h_out, 1)

                with a.Fori(0, EG // 2 - 1) as i:
                    for u in range(2):
                        gelu(i, u)
                        hi(i * 2 + (n0 + (u + 2)), u, None)
                for u in range(2):
                    gelu(EG // 2 - 1, u)
                    hi(n0 + (EG + u), u, None)
                with a.Fori(0, EG // 2 - 1) as i:
                    for u in range(2):
                        hi(i * 2 + (n0 + (EG + u + 2)), u, i * 4 + (m0 + (EG + 2 * u + 2)))

            for k in range(KT):
                a.wait_ge(y_add, NG * KT + AHEAD)
                if k >= 2:
                    a.wait_ge(n2_used, k - 1)
                go(fsq[k % 2][:], acc[:, k], ACT.Square).then_inc(n2_sq, 1)
            root(fsum2, HEADS + 2)
            for k in range(0, KT, 4):
                a.wait_ge(n2_out, k + 4)
                a.dma_start(y_out[:, k:k + 4], acc[:, k:k + 4]).then_inc(y_st, 16)
            a.wait_ge(y_st, 16 * (KT // 4))
            a.wait_ge(st_out, 32 * HEADS)
            a.wait_ge(cst_out, 32)
            a.wait_ge(g_st[0], 16 * ((NGC + 1) // 2))
            a.wait_ge(g_st[1], 16 * (NGC // 2))

        @block.vector
        def _(v_):
            C = Counts(v_)
            tt_, ts_, stt_, cp = (nc.vector.tensor_tensor, nc.vector.tensor_scalar,
                                  nc.vector.scalar_tensor_tensor, nc.vector.tensor_copy)

            def one(ap):
                return ap.rearrange("p o t -> p (o t)")

            v_.sem_inc(y_add, AHEAD)
            v_.sem_inc(w_s, AHEAD)
            C.base[w_s.name] = C.base[y_add.name] = AHEAD
            for s in (glu_s, csq_u, rsq_u):
                v_.sem_inc(s, 1)
                C.base[s.name] = 1
            for i in range(4):
                s = slice(4 * i, 4 * i + 4)
                v_.wait_ge(x_hi, i + 1)
                C.inc(tt_(xl[:, s], x_raw[:, s], f(xh[:, s]), ALU.subtract), x_lo)
            v_.wait_ge(x_lo, 4)
            v_.wait_ge(f_mm, 1)
            C.done(nc.vector.memset(keep[:], 1.0), dve)
            nc.vector.memset(keep[:, 0:TP:CH], 0.0)
            nc.vector.memset(keep[:, TP:TP + 1], 0.0)
            C.done(nc.vector.memset(scT[:], 0.0), dve)
            v_.wait_ge(consts_in, 16 * 9)

            def blocks(ap, l):
                m = LEVELS[l]
                n = (TP if m == CH // 2 else T) // (2 * m)
                return ap[:, 0:n * 2 * m].rearrange("p (n two m) -> p n two m", two=2, m=m), n, m

            def gla(h):
                q, k = z[:, 0], z[:, 1]
                v_.wait_ge(gz_ra, h + 1)
                C.done(ts_(parts(bcum[:]), yr(0), gb[:, h:h + 1], 0.0, ALU.add, ALU.min), gz_rd)
                v_.wait_ge(soft, h + 1)
                C.done(tt_(ke[0][:], bcum[:], qe[0][:], ALU.subtract), dve)
                C.done(nc.vector.tensor_tensor_scan(bcum[:], keep[:], ke[0][:], 0.0, ALU.mult, ALU.add), dve)

                def distances(l):
                    b, n, m = blocks(bcum, l)
                    d, _, _ = blocks(dist[l % 2], l)
                    mid = b[:, :, 0, m - 1:m].to_broadcast([P, n, m])
                    tt_(d[:, :, 0], mid, b[:, :, 0], ALU.subtract)
                    C.done(tt_(d[:, :, 1], b[:, :, 1], mid, ALU.subtract), dist_s)

                def take_scores(l):
                    v_.wait_ge(sc_mm, 7 * h + l + 1)
                    b = 4 + 2 * (l % 2)
                    m8 = masks[:, l:l + 1].to_broadcast([CH, NC, CH])
                    src = ps[0:CH, b, :].rearrange("p (c t) -> p c t", c=NC)
                    if l == 0:
                        C.done(tt_(scT[:, 0:NC], src, m8, ALU.mult), sc_out)
                        return
                    tt_(stmp[:, 0:NC], src, m8, ALU.mult)
                    dst = scT if l == 1 else stmp
                    C.done(tt_(dst[0:TS, NC, 0:TS], ps[0:TS, b + 1, 0:TS], masks[0:TS, l, 0:TS], ALU.mult), sc_out)
                    ins = tt_(scT[:, 0:NC], scT[:, 0:NC], stmp[:, 0:NC], ALU.add)
                    if l > 1:
                        ins = tt_(scT[0:TS, NC, 0:TS], scT[0:TS, NC, 0:TS], stmp[0:TS, NC, 0:TS], ALU.add)
                    C.done(ins, dve)

                distances(0)
                v_.wait_ge(z_out, 6 * h + 2)
                for l in range(6):
                    if l < 5:
                        distances(l + 1)
                    v_.wait_ge(decay_s, 8 * h + l + 1)
                    if l >= 2:
                        take_scores(l - 2)
                    n = TP if l == 0 else T
                    tt_(qe[l % 2][:, 0:n], q[:, 0:n], dist[l % 2][:, 0:n], ALU.mult)
                    C.done(tt_(ke[l % 2][:, 0:n], k[:, 0:n], dist[l % 2][:, 0:n], ALU.mult), qke)
                end = bcum[:, 0:TP].rearrange("p (c t) -> p c t", c=NC)
                tt_(dist[0][:, 0:TP].rearrange("p (c t) -> p c t", c=NC),
                    end[:, :, CH - 1:CH].to_broadcast([P, NC, CH]), end, ALU.subtract)
                C.done(tt_(dist[0][:, TP:T], bcum[:, T - 1:T].to_broadcast([P, TS]), bcum[:, TP:T], ALU.subtract),
                       dist_s)
                take_scores(4)
                take_scores(5)
                v_.wait_ge(decay_s, 8 * h + 7)
                C.done(tt_(qe[1][:], q, qe[0][:], ALU.mult), qb_s)
                take_scores(6)
                v_.wait_ge(decay_s, 8 * h + 8)
                C.done(tt_(ke[0][:], k, dist[0][:], ALU.mult), kd_s)
                v_.wait_ge(p_mm, 2 * h + 1)
                v_.wait_ge(st_out, 32 * h)
                C.done(cp(state[:, 1], ps[:, 4, 0:DV]), dve)
                for c in range(1, NC):
                    e = c * CH + CH - 1
                    C.done(stt_(state[:, c + 1], state[:, c], qe[0][:, e:e + 1],
                                ps[:, 4 + c // 2, (c % 2) * DV:(c % 2 + 1) * DV], ALU.mult, ALU.add),
                           p_out if c == NC - 1 else dve)
                v_.wait_ge(gs_in, 16 * (h + 1))
                v_.wait_ge(p_mm, 2 * h + 2)
                C.done(stt_(s_new[:], state[:, 0], qe[0][:, T - 1:T], ps[:, 4, 0:DV], ALU.mult, ALU.add), p_out)
                v_.wait_ge(rs_mm, h + 1)
                C.done(ts_(parts(qe[0][:]), yr(0), 1.0 / DV, EPS, ALU.mult, ALU.add), dve)
                C.done(nc.vector.reciprocal(qe[0][:], qe[0][:]), inv_s)
                v_.wait_ge(root_s, h + 1)
                for v in range(2):
                    C.done(stt_(z[:, 2 + v], z[:, 2 + v], ng[:, 2 * h + v:2 * h + v + 1], qe[0][:],
                                ALU.mult, ALU.mult), dve)
                v_.wait_ge(z_out, 6 * h + 6)
                for v in range(2):
                    j = CT + 2 * h + v
                    C.done(tt_(z[:, 2 + v], z[:, 2 + v], z[:, 4 + v], ALU.mult), dve)
                    C.done(cp(mh[:, j], z[:, 2 + v]), dve)
                    C.done(tt_(ml[:, j], z[:, 2 + v], f(mh[:, j]), ALU.subtract), head_out if v else dve)

            for h in range(HEADS):
                gla(h)

            v_.wait_ge(cst_in, 16)
            v_.wait_ge(st_out, 32 * HEADS)
            nc.vector.memset(ext[:, 0:NPAD], 0.0)
            nc.vector.memset(sum1[:], 0.0)
            C.done(nc.vector.memset(sum2[:], 0.0), dve)
            e_state, e_sample = NPAD + TP, NPAD + TP + NPAD
            with C.loop(CT, {dve: CW + 2, glu_s: 1, yf_s: 1, csq_u: 1}) as c:
                v_.wait_ge(mm, c * 2 + (A_CONV + 1))
                v_.wait_ge(sg_s, c + 2)
                cc = bass.ds(c, 1)
                tt_(ext[:, NPAD:NPAD + TH], ps[:, 0, 0:TH], sg[:, 0:TH], ALU.mult)
                tt_(ext[:, NPAD + TH:e_state], ps[:, 1, 0:TP - TH], sg[:, TH:TP], ALU.mult)
                C.done(tt_(ext[:, e_sample:EXT], ps[:, 1, TP - TH:TH], sg[:, TP:T], ALU.mult), glu_s)
                C.done(cp(ext[:, e_state:e_sample], one(cst[:, cc])), dve)
                cp(one(cpo[:, 0, cc]), ext[:, TP:TP + NPAD])
                C.done(cp(one(cpo[:, 1, cc]), ext[:, EXT - NPAD:EXT]), dve)
                C.done(ts_(yb[:], ext[:, 0:YL], one(cwt[:, cc, 0:1]), one(cvec[:, 0:1, cc]), ALU.mult, ALU.add), dve)
                for w in range(1, CW - 1):
                    C.done(stt_(yb[:], ext[:, w:w + YL], one(cwt[:, cc, w:w + 1]), yb[:], ALU.mult, ALU.add), dve)
                w = CW - 1
                stt_(one(yf[:, cc, 0:TP]), ext[:, w:w + TP], one(cwt[:, cc, w:w + 1]), yb[:, 0:TP], ALU.mult, ALU.add)
                C.done(stt_(one(yf[:, cc, TP:T]), ext[:, e_sample:EXT], one(cwt[:, cc, w:w + 1]), yb[:, e_state:YL],
                            ALU.mult, ALU.add), yf_s)
                C.done(tt_(sum1[:], sum1[:], one(yf[:, cc]), ALU.add), dve)
                v_.wait_ge(csq_s, c + 1)
                C.done(tt_(sum2[:], sum2[:], sq[:], ALU.add), csq_u)
            v_.sem_inc(cst_s, 1)

            def norm_stats(n, s1, s2, t):
                C.done(ts_(parts(s1[:]), yr(0), 1.0 / n, None, ALU.mult), dve)
                C.done(tt_(t[:], s1[:], s1[:], ALU.mult), dve)
                C.done(stt_(parts(s2[:]), yr(1), 1.0 / n, parts(t[:]), ALU.mult, ALU.subtract), dve)
                C.done(ts_(s2[:], s2[:], 0.0, EPS, ALU.max, ALU.add), dve)
                C.done(nc.vector.reciprocal(s2[:], s2[:]), inv_s)
                v_.wait_ge(root_s, C.base[inv_s.name])

            v_.wait_ge(cmean_mm, 1)
            norm_stats(CONV, sum1, sum2, tmp[0])
            v_.wait_ge(cst_out, 32)

            def mix_out(c):
                t = tmp[c % 2]
                v_.wait_ge(ysilu_s, c + 1)
                C.done(cp(mh[:, c], t[:]), dve)
                C.done(tt_(ml[:, c], t[:], f(mh[:, c]), ALU.subtract), mix_s)

            for c in range(CT):
                t = tmp[c % 2]
                C.done(tt_(t[:], yf[:, c], sum1[:], ALU.subtract), dve)
                C.done(tt_(t[:], t[:], sum2[:], ALU.mult), dve)
                C.done(ts_(t[:], t[:], cvec[:, 1, c:c + 1], cvec[:, 2, c:c + 1], ALU.mult, ALU.add), ycn_s)
                if c:
                    mix_out(c - 1)
            mix_out(CT - 1)

            nc.vector.memset(sum1[:], 0.0)
            C.done(nc.vector.memset(sum2[:], 0.0), dve)
            with C.loop(NO // 2, {dve: 4, r_s: 2, rsq_u: 2}) as i:
                for u in range(2):
                    n = bass.ds(i * 2 + u, 1)
                    v_.wait_ge(mm, i * 2 + (A_OUT + u + 1))
                    C.done(stt_(parts(one(r1[:, n])), parts(one(f(xh[:, n]))), ALPHA, zr(u), ALU.mult, ALU.add), dve)
                    C.done(stt_(one(r1[:, n]), one(f(xl[:, n])), ALPHA, one(r1[:, n]), ALU.mult, ALU.add), r_s)
                    C.done(tt_(sum1[:], sum1[:], one(r1[:, n]), ALU.add), dve)
                    v_.wait_ge(rsq_s, i * 2 + (u + 1))
                    C.done(tt_(sum2[:], sum2[:], sq[:], ALU.add), rsq_u)
            v_.sem_inc(rst_s, 1)
            C.done(nc.vector.memset(sc[:], 0.0), sc_set)
            v_.wait_ge(rmean_mm, 1)
            norm_stats(D, sum1, sum2, tmp[0])
            for k in range(KT):
                t = tmp[k % 2]
                C.done(tt_(t[:], r1[:, k], sum1[:], ALU.subtract), dve)
                C.done(tt_(t[:], t[:], sum2[:], ALU.mult), dve)
                C.done(ts_(t[:], t[:], lvec[:, 0, k:k + 1], lvec[:, 1, k:k + 1], ALU.mult, ALU.add), dve)
                C.done(cp(xh[:, k], t[:]), dve)
                C.done(tt_(xl[:, k], t[:], f(xh[:, k]), ALU.subtract), x2_s)

            LOWEST = -3.0e38

            def top16(vals, work, best, num, used):
                for tt in range(TT):
                    ins = nc.vector.max(best[:, tt, 0:8], vals[:, tt])
                C.done(ins, dve)
                for tt in range(TT):
                    nc.vector.max_index(num[:, tt, 0:8], best[:, tt, 0:8], vals[:, tt])
                    ins = nc.vector.match_replace(work[:, tt], best[:, tt, 0:8], vals[:, tt], LOWEST)
                C.done(ins, used)
                for tt in range(TT):
                    ins = nc.vector.max(best[:, tt, 8:16], work[:, tt])
                C.done(ins, dve)
                for tt in range(TT):
                    ins = nc.vector.max_index(num[:, tt, 8:16], best[:, tt, 8:16], work[:, tt])
                C.done(ins, dve)

            for h in range(PH):
                for p in range(2):
                    v_.wait_ge(s_out, 2 * h + p + 1)
                    top16(sc[:, p], scw, sv[:, p], si[:, p], topk_s)
                C.done(cp(sif[:], si[:]), dve)
                s4 = [P, TT, 16, 16]
                C.done(tt_(cand[:].rearrange("p t (a b) -> p t a b", a=16),
                           sv[:, 0].unsqueeze(3).to_broadcast(s4), sv[:, 1].unsqueeze(2).to_broadcast(s4), ALU.add), dve)
                top16(cand, candw, bs, pos, dve)
                cp(picks[:, 0, :, h], bs[:])
                ts_(pab[:, 0], pos[:], 4, None, ALU.logical_shift_right)
                C.done(ts_(pab[:, 1], pos[:], 15, None, ALU.bitwise_and), dve)
                C.done(cp(pabf[:], pab[:]), dve)
                flat = [P, TT * 16, 16]
                oh3 = oh[:].rearrange("p t k a -> p (t k) a")
                for p in range(2):
                    at_ = pabf[:, p].rearrange("p t k -> p (t k)").unsqueeze(2).to_broadcast(flat)
                    C.done(tt_(oh3, at_, iota[:, 0:16].unsqueeze(1).to_broadcast(flat), ALU.is_equal), dve)
                    C.done(tt_(oh[:], oh[:], sif[:, p].unsqueeze(2).to_broadcast(s4), ALU.mult), dve)
                    C.done(nc.vector.tensor_reduce(picks[:, 1 + p, :, h], oh[:], AX, ALU.add), dve)

            g2 = picks[:, 0].rearrange("p t h k -> p (t h) k")
            C.done(cp(gsum[:], g2[:, :, 0]), dve)
            gs_b = gsum[:].unsqueeze(2).to_broadcast([P, TT * PH, 16])
            C.done(tt_(g2, g2, gs_b, ALU.subtract), gd_s)
            v_.wait_ge(ge_s, 1)
            C.done(nc.vector.tensor_reduce(gsum[:], g2, AX, ALU.add), dve)
            C.done(nc.vector.reciprocal(gsum[:], gsum[:]), dve)
            C.done(tt_(g2, g2, gs_b, ALU.mult), picks_s)

            v_.wait_ge(pt_out, 1)
            with C.loop(T // 8, {oneh: 2}) as i:
                for u in range(2):
                    v_.wait_ge(g_mm, i * 2 + (u + 1))
                    for t in range(4):
                        tok = bass.ds(i * 8 + (4 * u + t), 1)
                        ts_(oneA[:, u, t], iota[:], picksT[:, 1, tok], picksT[:, 0, tok], ALU.is_equal, ALU.mult)
                        ins = ts_(oneB[:, u, t], iota[:], picksT[:, 2, tok], None, ALU.is_equal)
                    C.inc(ins, oneh)

            v_.wait_ge(g_mm, T // 4 + AHEAD)
            with C.loop(KT, {dve: 2}) as k:
                kk = bass.ds(k, 1)
                C.done(ts_(one(acc[:, kk]), one(f(xh[:, kk])), ALPHA, None, ALU.mult), dve)
                C.done(stt_(one(acc[:, kk]), one(f(xl[:, kk])), ALPHA, one(acc[:, kk]), ALU.mult, ALU.add), dve)
            v_.sem_inc(acc_set, 1)
            v_.wait_ge(g_st[0], 16 * ((NGC + 1) // 2))
            v_.wait_ge(g_st[1], 16 * (NGC // 2))
            with C.loop(NG, {dve: 2 * EG, w_s: EG, y_add: KT}) as g:
                with C.loop(EG // 2, {dve: 4, w_s: 2}) as i:
                    for u in range(2):
                        e = bass.ds(i * 2 + u, 1)
                        v_.wait_ge(g_in, g * 16 + 16)
                        v_.wait_ge(h_out, g * EG + (i * 2 + (u + 1 + AHEAD)))
                        gate = gt[:, :, e].rearrange("p c o t -> p c (o t)")
                        h3 = hb[u][:].rearrange("p (c t) -> p c t", c=NGC)
                        C.done(tt_(h3, h3, gate, ALU.mult), dve)
                        C.done(cp(one(W0h[:, e]), hb[u][:]), dve)
                        C.done(tt_(one(W0l[:, e]), hb[u][:], one(f(W0h[:, e])), ALU.subtract), w_s)
                with C.loop(EG // 2, {y_add: 4}) as i:
                    for u in range(2):
                        for d in range(2):
                            v_.wait_ge(mm, g * PER_G + (i * 4 + (A_DENSE + EG + 2 * u + d + 1)))
                            dd = bass.ds(i * 4 + (2 * u + d), 1)
                            a_ = parts(one(acc[:, dd]))
                            C.done(tt_(a_, a_, yr(d), ALU.add), y_add)

            nc.vector.memset(fsum1[:], 0.0)
            C.done(nc.vector.memset(fsum2[:], 0.0), dve)
            for k in range(KT):
                C.done(tt_(fsum1[:], fsum1[:], acc[:, k], ALU.add), dve)
                v_.wait_ge(n2_sq, k + 1)
                C.done(tt_(fsum2[:], fsum2[:], fsq[k % 2][:], ALU.add), n2_used)
            v_.sem_inc(n2_st, 1)
            v_.wait_ge(n2_mm, 1)
            norm_stats(D, fsum1, fsum2, fsq[0])
            for k in range(KT):
                C.done(tt_(acc[:, k], acc[:, k], fsum1[:], ALU.subtract), dve)
                C.done(tt_(acc[:, k], acc[:, k], fsum2[:], ALU.mult), dve)
                C.done(ts_(acc[:, k], acc[:, k], lvec[:, 2, k:k + 1], lvec[:, 3, k:k + 1], ALU.mult, ALU.add), n2_out)


def _tiles(w, cols):
    n = w.shape[1] // cols
    return np.ascontiguousarray(w.reshape(-1, P, n, cols).transpose(2, 1, 0, 3))


def _by_feature(a):
    return np.ascontiguousarray(a.T.reshape(-1, P, a.shape[0]).transpose(1, 0, 2))


def _level_masks():
    s, t = np.arange(CH)[:, None], np.arange(CH)[None, :]
    m = [((s // l) % 2 == 0) & (t // l == s // l + 1) for l in LEVELS] + [s == t]
    return np.ascontiguousarray(np.stack(m, 1).astype(np.float32))


def kernel(x_prompt, x_sample, state_conv, state_gla, w_in, conv_w, conv_b, conv_ln_g, conv_ln_b,
           gla_gate_w, gla_gate_b, gla_norm_g, w_out, ln1_g, ln1_b, peer_w_query, peer_sub_keys,
           peer_u, peer_v, ln2_g, ln2_b):
    import concourse.bacc as bacc
    from concourse.bass_utils import run_bass_kernel_spmd

    w_in = np.asarray(w_in)[0]
    QK, V = HEADS * DK, HEADS * DV
    o = np.cumsum([0, CONV, CONV, QK, QK, V, V])
    part = {n: _tiles(w_in[:, o[i]:o[i + 1]], P) for i, n in enumerate(["val", "gate", "q", "k", "v", "g"])}
    order = []
    for h in range(HEADS):
        order += [part["q"][h], part["k"][h], part["v"][2 * h], part["v"][2 * h + 1],
                  part["g"][2 * h], part["g"][2 * h + 1]]
    for c in range(CT):
        order += [part["val"][c], part["gate"][c]]

    def vec(a):
        return np.asarray(a)[0].reshape(-1, P).T

    pv = np.asarray(peer_v)[0].reshape(NG, EG, P, EG, 2, P).transpose(0, 3, 2, 4, 1, 5)
    ins = {
        "xT": _by_feature(np.concatenate([np.asarray(x_prompt)[0], np.asarray(x_sample)[0]], 0)),
        "w_in": np.stack(order),
        "w_f": _tiles(w_in[:, o[6]:], RANK)[0],
        "w_out": _tiles(np.asarray(w_out)[0], P),
        "w_q": _tiles(np.asarray(peer_w_query)[0], P),
        "u_t": np.ascontiguousarray(np.asarray(peer_u)[0].reshape(NKEY, P, KT, P).transpose(0, 3, 2, 1)),
        "v_t": np.ascontiguousarray(pv).reshape(NG * EG, P, KT, P),
        "conv_state": np.ascontiguousarray(np.asarray(state_conv)[0, 0].T.reshape(CT, P, NPAD).transpose(1, 0, 2)),
        "conv_w": np.ascontiguousarray(np.asarray(conv_w)[0].T.reshape(CT, P, CW).transpose(1, 0, 2)),
        "conv_vec": np.ascontiguousarray(np.stack([vec(conv_b), vec(conv_ln_g), vec(conv_ln_b)], 1)),
        "gla_state": np.ascontiguousarray(np.asarray(state_gla)[0, 0].transpose(1, 0, 2)),
        "gate_w": np.ascontiguousarray(np.asarray(gla_gate_w)[0].reshape(RANK, HEADS, P)),
        "gate_b": np.ascontiguousarray(vec(gla_gate_b)),
        "norm_g": np.ascontiguousarray(vec(gla_norm_g)),
        "ln_vec": np.ascontiguousarray(np.stack([vec(ln1_g), vec(ln1_b), vec(ln2_g), vec(ln2_b)], 1)),
        "sub_keys": np.ascontiguousarray(
            np.asarray(peer_sub_keys)[0].reshape(2 * PH, NKEY, P).transpose(2, 0, 1)),
        "ident": np.eye(P, dtype=np.float32),
        "iota": np.ascontiguousarray(np.broadcast_to(np.arange(P, dtype=np.float32), (P, P))),
        "masks": _level_masks(),
    }
    outs = {"y": (P, KT, T), "conv_p": (P, CT, NPAD), "conv_s": (P, CT, NPAD),
            "gla_p": (P, HEADS, DV), "gla_s": (P, HEADS, DV)}
    nc = bacc.Bacc("TRN2", target_bir_lowering=False, num_devices=1)
    args = [nc.dram_tensor("in_" + n, a.shape, F32, kind="ExternalInput").ap() for n, a in ins.items()]
    args += [nc.dram_tensor("out_" + n, s, F32, kind="ExternalOutput").ap() for n, s in outs.items()]
    args.append(nc.dram_tensor("g_scratch", (NGC, P, P, GC), F32, kind="Internal").ap())
    program(nc, *args)
    r = run_bass_kernel_spmd(nc, [{"in_" + n: a for n, a in ins.items()}], core_ids=[0]).results[0]
    y = np.asarray(r["out_y"]).transpose(2, 1, 0).reshape(T, D)

    def rows(a):
        return np.ascontiguousarray(np.asarray(a).transpose(2, 1, 0).reshape(1, 1, NPAD, CONV))

    def states(a):
        return np.ascontiguousarray(np.asarray(a).transpose(1, 0, 2))[None, None]

    return (np.ascontiguousarray(y[None, :TP]), np.ascontiguousarray(y[None, TP:]),
            rows(r["out_conv_p"]), states(r["out_gla_p"]), rows(r["out_conv_s"]), states(r["out_gla_s"]))
```

```python
from contextlib import ExitStack

import numpy as np

import concourse.bass as bass
from concourse import mybir
from concourse.alu_op_type import AluOpType as ALU

F32 = mybir.dt.float32
F32R = mybir.dt.float32r
U32 = mybir.dt.uint32
I32 = mybir.dt.int32
ACT = mybir.ActivationFunctionType
AX = mybir.AxisListType.X

P = 128
TP, TS = 512, 32
T = TP + TS
TH = T // 2
D = 2048
KT = D // P
CONV, CW = 1024, 31
CT = CONV // P
NPAD = CW - 1
EXT = NPAD + TP + NPAD + TS
YL = EXT - NPAD
HEADS, DK, DV, RANK = 4, 128, 256, 16
TAU = 16.0
CH = 64
NC = TP // CH
PH, NKEY, TOPK = 8, 128, 16
TT = 5
EG = 8
NG = NKEY // EG
GC = 32
NGC = T // GC
EPS = 1e-5
ALPHA = 2.0 ** 0.25
AHEAD = 2
LEVELS = (32, 16, 8, 4, 2, 1)


class Counts:

    def __init__(self, eng):
        self.eng, self.base, self.loops = eng, {}, []

    def value(self, sem):
        v = self.base.get(sem.name, 0)
        for reg, per in self.loops:
            if per.get(sem.name, 0):
                v = reg * per[sem.name] + v
        return v

    def inc(self, ins, sem):
        ins.then_inc(sem, 1)
        self.base[sem.name] = self.base.get(sem.name, 0) + 1

    def done(self, ins, sem):
        self.inc(ins, sem)
        self.eng.wait_ge(sem, self.value(sem))

    def lag(self, ins, sem):
        self.inc(ins, sem)
        self.eng.wait_ge(sem, self.value(sem) - 1)

    def loop(self, n, per):
        return _Loop(self, n, per)


class _Loop:
    def __init__(self, c, n, per):
        self.c, self.n, self.per = c, n, {s.name: k for s, k in per.items()}

    def __enter__(self):
        self.fori = self.c.eng.Fori(0, self.n)
        reg = self.fori.__enter__()
        self.before = dict(self.c.base)
        self.c.loops.append((reg, self.per))
        return reg

    def __exit__(self, *e):
        self.c.loops.pop()
        if e[0] is None:
            for name in set(self.c.base) | set(self.per):
                got = self.c.base.get(name, 0) - self.before.get(name, 0)
                assert got == self.per.get(name, 0), (name, got, self.per.get(name, 0))
                self.c.base[name] = self.before.get(name, 0) + self.n * got
        return self.fori.__exit__(*e)


def program(nc, xT, w_in, w_f, w_out, w_q, u_t, v_t, conv_state, conv_w, conv_vec, gla_state,
            gate_w, gate_b, norm_g, ln_vec, sub_keys, ident_in, iota_in, masks_in,
            y_out, conv_p, conv_s, gla_p, gla_s, g_dram, h_dram):
    ctx = ExitStack()
    with ctx:
        lo0 = -(-nc.sbuf_base // 32) * 32

        def at(name, shape, dt, off):
            return nc.alloc_sbuf_tensor_at(name, shape, dt, offset=lo0 + off)

        def sem(name):
            return ctx.enter_context(nc.semaphore(name))

        ROW = T * 4
        X0, X1 = 0, KT * ROW
        M0, M1 = 2 * KT * ROW, 3 * KT * ROW
        R0 = 4 * KT * ROW
        TILE = KT * P * 4
        C0 = R0 + 6 * TILE
        S0 = C0 + 2656
        xh = at("xh", [P, KT, T], F32R, X0)
        xl = at("xl", [P, KT, T], F32R, X1)
        r1 = at("r1", [P, KT, T], F32, X0)
        mh = at("mh", [P, KT, T], F32R, M0)
        ml = at("ml", [P, KT, T], F32R, M1)
        x_raw = at("x_raw", [P, KT, T], F32, M0)
        wraw = at("wraw", [P, 2, KT, P], F32, R0)
        wh = at("wh", [P, 2, KT, P], F32R, R0 + 2 * TILE)
        wl = at("wl", [P, 2, KT, P], F32R, R0 + 4 * TILE)
        ident = at("ident", [P, P], F32, C0)
        ones = at("ones", [P, P], F32, C0 + 512)
        iota = at("iota", [P, P], F32, C0 + 1024)
        cvec = at("cvec", [P, 3, CT], F32, C0 + 1536)
        gb = at("gb", [P, HEADS], F32, C0 + 1632)
        ng = at("ng", [P, HEADS * 2], F32, C0 + 1664)
        lvec = at("lvec", [P, 4, KT], F32, C0 + 1696)
        wf_raw = at("wf_raw", [P, KT, RANK], F32, M1)
        z = at("z", [P, 6, T], F32, M0)
        bcum = at("bcum", [P, T], F32, M0 + 6 * ROW)
        keep = at("keep", [P, T], F32, M0 + 7 * ROW)
        state = at("state", [P, NC + 1, DV], F32, M1)
        kdN = at("kdN", [CH, NC + 1, P], F32, M1 + 9216)
        dist0 = at("dist0", [P, T], F32, M1 + 9216 + 4608)
        qe = [at(f"qe{u}", [P, T], F32, M0 + (14 + u) * ROW) for u in range(2)]
        ke = [at(f"ke{u}", [P, T], F32, M1 + (14 + u) * ROW) for u in range(2)]
        masks = at("masks", [CH, 7, CH], F32, S0)
        gw = at("gw", [RANK, HEADS, P], F32, S0 + 1792)
        flr = at("flr", [RANK, T], F32, S0 + 3840)
        vN = at("vN", [CH, NC + 1, DV], F32, S0 + 6016)
        scT = at("scT", [CH, NC + 1, CH], F32, S0 + 15232)
        dist1 = at("dist1", [P, T], F32, S0 + 17536)
        s_new = at("s_new", [P, DV], F32, S0 + 19712)
        cwt = at("cwt", [P, CT, CW], F32, S0 + 20768)
        dist = [dist0, dist1]
        stmp = at("stmp", [CH, NC + 1, CH], F32, M1 + 9216)
        cst = at("cst", [P, CT, NPAD], F32, M0)
        cpo = at("cpo", [P, 2, CT, NPAD], F32, M0 + 960)
        ext = at("ext", [P, EXT], F32, S0)
        sg = at("sg", [P, T], F32, S0 + 4864)
        yb = [at("yb0", [P, YL], F32, S0 + 7040), at("yb1", [P, YL], F32, S0 + 15872)]
        sum1 = at("sum1", [P, T], F32, S0 + 9344)
        sum2 = at("sum2", [P, T], F32, S0 + 11520)
        sq = at("sq", [P, T], F32, S0 + 13696)
        yf = at("yf", [P, CT, T], F32, M1)
        tmp = [at(f"tmp{u}", [P, T], F32, S0 + 15872 + u * ROW) for u in range(2)]
        qT = at("qT", [P, 2, T], F32, M0)
        skT = at("skT", [P, 2 * PH, P], F32, M0 + 2 * ROW)
        o = M1
        sc = at("sc", [P, 2, TT, P], F32, o); o += 2 * TT * P * 4
        scw = at("scw", [P, TT, P], F32, o); o += TT * P * 4
        cand = at("cand", [P, TT, 256], F32, o); o += TT * 1024
        candw = at("candw", [P, TT, 256], F32, o); o += TT * 1024
        oh = at("oh", [P, TT, 16, 16], F32, o); o += TT * 1024
        sv = at("sv", [P, 2, TT, 16], F32, o); o += 640
        si = at("si", [P, 2, TT, 16], U32, o); o += 640
        sif = at("sif", [P, 2, TT, 16], F32, o); o += 640
        bs = at("bs", [P, TT, 16], F32, o); o += 320
        pos = at("pos", [P, TT, 16], U32, o); o += 320
        pab = at("pab", [P, 2, TT, 16], U32, o); o += 640
        pabf = at("pabf", [P, 2, TT, 16], F32, o); o += 640
        assert o <= M1 + KT * ROW, o - M1
        picks = at("picks", [P, 3, TT, PH, 16], F32, S0)
        gsum = at("gsum", [P, TT * PH], F32, S0 + 7680)
        picksT = at("picksT", [P, 3, T], F32, S0 + 7840)
        gate_h = at("gate_h", [P, T], F32R, S0 + 14368)
        gate_l = at("gate_l", [P, T], F32R, S0 + 14368 + ROW)
        hb = at("hb", [P, 2, 2, T], F32, M0)
        gst = at("gst", [P, P, GC], F32, M0 + 4 * ROW)
        OH = 2 * 4 * P * 4
        oneAh = at("oneAh", [P, 2, 4, P], F32R, M1)
        oneAl = at("oneAl", [P, 2, 4, P], F32R, M1 + OH)
        oneB = at("oneB", [P, 2, 4, P], F32R, M1 + 2 * OH)
        Wh = [at(f"Wh{v}", [P, EG, T], F32R, X0 + v * KT * ROW) for v in range(2)]
        Wl = [at(f"Wl{v}", [P, EG, T], F32R, X0 + v * KT * ROW + EG * ROW) for v in range(2)]
        acc = at("acc", [P, KT, T], F32, M1)
        gt = at("gt", [P, NGC, EG, GC], F32, S0)
        hg = at("hg", [P, EG, T], F32, M0 + 4 * ROW)
        wt = [at(f"wt{v}", [P, T], F32, S0 + EG * ROW + v * ROW) for v in range(2)]
        fsum1 = at("fsum1", [P, T], F32, M0)
        fsum2 = at("fsum2", [P, T], F32, M0 + ROW)
        fsq = [at(f"fsq{u}", [P, T], F32, M0 + (2 + u) * ROW) for u in range(2)]

        ps = ctx.enter_context(nc.psum_tensor("ps", [P, 8, 512], F32))

        x_in = [sem(f"x_in{i}") for i in range(4)]
        consts_in, wf_in, keys_in = sem("consts_in"), sem("wf_in"), sem("sub_keys_in")
        w_in_s = [sem("w_slot0_in"), sem("w_slot1_in")]
        whi, wlo = sem("w_hi_split"), sem("w_lo_split")
        mm = sem("tile_mm_done")
        x_hi, x_lo = sem("x_hi_split"), sem("x_lo_split")
        f_mm, f_out, z_out, ones_set = sem("f_mm"), sem("f_out"), sem("z_out"), sem("ones_set")
        dve, act = sem("dve_step"), sem("act_step")
        gz_mm, soft, gz_ra, gz_rd = sem("gate_mm"), sem("softplus"), sem("gate_read_act"), sem("gate_read_dve")
        vt_mm, vt_out, kt_mm, kt_out = sem("v_turned"), sem("v_out"), sem("k_turned"), sem("k_out")
        dist_s, decay_s, qke, sc_mm, sc_out = (
            sem("distances"), sem("decays"), sem("qk_decayed"), sem("score_mm"), sem("score_out"))
        qb_s, kd_s, p_mm, p_out, o_mm, o_out, rs_mm, head_out = (
            sem("q_from_start"), sem("k_to_end"), sem("kv_mm"), sem("states"), sem("o_mm"), sem("o_out"),
            sem("rms_mm"), sem("head_done"))
        gs_in, st_out = sem("gla_state_in"), sem("gla_state_out")
        cst_in, cst_out = sem("conv_state_in"), sem("conv_state_out")
        sg_s, glu_s, yf_s, csq_s, csq_u, cst_s, cmean_mm, ycn_s, ysilu_s, mix_s = (
            sem("gate_sigmoid"), sem("glu_done"), sem("conv_done"), sem("conv_square"), sem("conv_square_used"),
            sem("conv_sums"), sem("conv_mean_mm"), sem("conv_normed"), sem("conv_silu"), sem("mix_ready"))
        r_s, rsq_s, rsq_u, rst_s, rmean_mm, x2_s, sc_set = (
            sem("residual_ready"), sem("residual_square"), sem("residual_square_used"), sem("norm1_sums"),
            sem("norm1_mean_mm"), sem("x2_ready"), sem("score_pad_set"))
        inv_s, root_s = sem("inverse_variance"), sem("inverse_deviation")
        q_out, s_mm, s_out, topk_s, gd_s, ge_s, picks_s, pt_mm, pt_out = (
            sem("q_out"), sem("key_scores"), sem("key_scores_out"), sem("head_picked"), sem("gate_diff"),
            sem("gate_exp"), sem("picks_ready"), sem("picks_turned"), sem("picks_turned_out"))
        oneh, g_mm, g_out = sem("one_hots"), sem("g_mm"), sem("g_out")
        g_st, h_st = sem("g_stored"), [sem("h_stored0"), sem("h_stored1")]
        g_in, h_in = sem("g_group_in"), sem("h_group_in")
        h_out, w_s, y_add, acc_set = sem("gelu_out"), sem("w_ready"), sem("y_added"), sem("acc_set")
        n2_sq, n2_used, n2_st, n2_mm, n2_out, y_st = (
            sem("norm2_square"), sem("norm2_square_used"), sem("norm2_sums"), sem("norm2_mean_mm"),
            sem("norm2_out"), sem("y_stored"))

        NZ, NCV, NO, NQ = 6 * HEADS, 2 * CT, KT, 2 * PH
        A_CONV, A_OUT, A_Q, A_U = NZ, NZ + NCV, NZ + NCV + NO, NZ + NCV + NO + NQ
        A_V = A_U + NKEY
        U_A, U_B = 3, NGC
        U_C = NKEY // 4 - U_A - U_B

        halves = [slice(h * TH, (h + 1) * TH) for h in range(2)]
        chunks = [(c, c * CH, CH) for c in range(NC)] + [(NC, TP, TS)]

        def parts(a):
            return a.rearrange("p (h t) -> p h t", h=2)

        def zr(u):
            return ps[:, 2 * u:2 * u + 2, 0:TH]

        def yr(u):
            return ps[:, 4 + 2 * u:6 + 2 * u, 0:TH]

        def f(ap):
            return ap.bitcast(F32)

        block = ctx.enter_context(nc.Block())

        @block.sync
        def _(sp):
            def load(dst, src, s):
                sp.dma_start(dst, src).then_inc(s, 16)

            def tile(src, u):
                load(wraw[:, u], src, w_in_s[u])

            def pairs(w):
                return w.rearrange("(n u) p k c -> n u p k c", u=2)

            load(x_raw[:, 0:4], xT[:, 0:4], x_in[0])
            load(wf_raw[:], w_f, wf_in)
            tile(pairs(w_in)[0, 0], 0)
            for i in range(1, 4):
                load(x_raw[:, 4 * i:4 * i + 4], xT[:, 4 * i:4 * i + 4], x_in[i])
            tile(pairs(w_in)[0, 1], 1)
            for dst, src in ((ident, ident_in), (iota, iota_in), (cvec, conv_vec), (gb, gate_b), (ng, norm_g),
                             (lvec, ln_vec), (masks, masks_in), (gw, gate_w), (cwt, conv_w)):
                load(dst[:], src, consts_in)

            def stream(src, n0, i0, i1):
                s = pairs(src)
                with sp.Fori(0, i1 - i0) as i:
                    for u in range(2):
                        sp.wait_ge(wlo, i * 2 + (n0 + u - 1))
                        tile(s[bass.ds(i + i0, 1), u].rearrange("o p k c -> (o p) k c"), u)

            stream(w_in, 2, 1, (NZ + NCV) // 2)
            stream(w_out, A_OUT, 0, NO // 2)
            s = pairs(w_q)
            for u in range(2):
                sp.wait_ge(wlo, A_Q + u - 1)
                tile(s[0, u], u)
            sp.wait_ge(mm, A_Q)
            load(skT[:], sub_keys, keys_in)
            stream(w_q, A_Q + 2, 1, NQ // 2)
            stream(u_t, A_U, 0, NKEY // 2)
            gsrc = g_dram.rearrange("c j (g e) t -> g j c (e t)", e=EG)
            hsrc = h_dram.rearrange("(g n) p u t -> g p n (u t)", n=EG // 2)
            vs = v_t.rearrange("(g n u) p k c -> g n u p k c", u=2, n=EG // 2)

            def group_in(g):
                for dst, src, q in ((gt[:].rearrange("p c e t -> p c (e t)"), gsrc, g_in),
                                    (hg[:].rearrange("p (n u) t -> p n (u t)", u=2), hsrc, h_in)):
                    a = src[g] if isinstance(g, int) else src[bass.ds(g, 1)].rearrange("o p n q -> (o p) n q")
                    load(dst, a, q)

            def v_pairs(g, i0, i1):
                with sp.Fori(i0, i1) as i:
                    for u in range(2):
                        sp.wait_ge(wlo, (g * EG + (A_V - 1 + u)) + i * 2)
                        t = vs[bass.ds(g, 1), bass.ds(i, 1), u]
                        tile(t.rearrange("o q p k c -> (o q p) k c"), u)

            sp.wait_ge(g_st, 16 * NGC)
            for v in range(2):
                sp.wait_ge(h_st[v], 16 * (EG // 4))
            group_in(0)
            with sp.Fori(0, NG - 1) as g:
                v_pairs(g, 0, EG // 4)
                sp.wait_ge(w_s, g * EG + EG)
                for v in range(2):
                    sp.wait_ge(h_st[v], 16 * (NKEY // 4))
                group_in(g + 1)
                v_pairs(g, EG // 4, EG // 2)
            with sp.Fori(NG - 1, NG) as g:
                v_pairs(g, 0, EG // 2)

        @block.gpsimd
        def _(pool):
            nc.gpsimd.memset(ones[:], 1.0).then_inc(ones_set, 1)

            def lo(n, u, freed):
                pool.wait_ge(whi, n + 1)
                if freed is not None:
                    pool.wait_ge(mm, freed)
                nc.gpsimd.tensor_tensor(wl[:, u], wraw[:, u], f(wh[:, u]), ALU.subtract).then_inc(wlo, 1)

            for u in range(2):
                lo(u, u, None)
            with pool.Fori(1, A_V // 2 + 1) as i:
                for u in range(2):
                    lo(i * 2 + u, u, i * 2 + (u - 1))
            with pool.Fori(1, NKEY // 2) as i:
                for u in range(2):
                    lo(i * 2 + (A_V + u), u, i * 4 + (A_V + 2 * u - 2))

        @block.tensor
        def _(pe):
            mat = nc.tensor.matmul

            def job(u, n, a, ah, al, out, waits, first_k=None):
                pe.wait_ge(wlo, n + 1)
                for s, v in waits:
                    pe.wait_ge(s, v)
                for k in range(KT):
                    if first_k:
                        first_k(k)
                    for w, m in ((wh, ah), (wh, al), (wl, ah)):
                        for h in range(2):
                            ins = mat(out[:, h], w[:, u, k], m[:, k, halves[h]],
                                      start=(k == 0 and w is wh and m is ah),
                                      stop=(k == KT - 1 and w is wl))
                ins.then_inc(mm, 1)

            pe.sem_inc(g_mm, AHEAD)
            pe.wait_ge(wf_in, 16)
            for k in range(KT):
                if k % 4 == 0:
                    pe.wait_ge(x_in[k // 4], 16)
                for h in range(2):
                    ins = mat(ps[0:RANK, 4 + h, 0:TH], wf_raw[:, k], x_raw[:, k, halves[h]],
                              start=(k == 0), stop=(k == KT - 1))
            ins.then_inc(f_mm, 1)

            def gla(h):
                q, k = z[:, 0], z[:, 1]
                pe.wait_ge(f_out, 1)
                pe.wait_ge(consts_in, 16 * 9)
                for i in range(2):
                    ins = mat(ps[:, 4 + i, 0:TH], gw[:, h], flr[:, halves[i]], start=True, stop=True)
                ins.then_inc(gz_mm, 1)
                pe.wait_ge(gz_ra, h + 1)
                pe.wait_ge(gz_rd, h + 1)
                pe.wait_ge(z_out, 6 * (h + 1))
                for c in range(NC):
                    for v in range(2):
                        col = (c % 2) * DV + v * P
                        ins = nc.tensor.transpose(ps[0:CH, 4 + c // 2, col:col + P],
                                                  z[:, 2 + v, c * CH:(c + 1) * CH], ident[:])
                ins.then_inc(vt_mm, 1)
                pe.wait_ge(vt_out, 2 * h + 1)
                for v in range(2):
                    ins = nc.tensor.transpose(ps[0:TS, 4, v * P:v * P + P], z[:, 2 + v, TP:T], ident[:])
                ins.then_inc(vt_mm, 1)
                for l in range(7):
                    b = 4 + 2 * (l % 2)
                    a, m = (ke[l % 2], qe[l % 2]) if l < 6 else (z[:, 1], z[:, 0])
                    if l < 6:
                        pe.wait_ge(qke, 6 * h + l + 1)
                    if l == 0:
                        pe.wait_ge(vt_out, 2 * h + 2)
                    if l >= 2:
                        pe.wait_ge(sc_out, 7 * h + l - 1)
                    for c, t0, n in chunks:
                        if c == NC and l == 0:
                            continue
                        bank, col = (b, c * CH) if c < NC else (b + 1, 0)
                        ins = mat(ps[0:n, bank, col:col + n], a[:, t0:t0 + n], m[:, t0:t0 + n],
                                  start=True, stop=True)
                    ins.then_inc(sc_mm, 1)
                pe.wait_ge(kd_s, h + 1)
                pe.wait_ge(sc_out, 7 * h + 7)
                for c, t0, n in chunks:
                    ins = nc.tensor.transpose(ps[0:n, 4 + c // 4, (c % 4) * P:(c % 4) * P + P],
                                              ke[0][:, t0:t0 + n], ident[:])
                ins.then_inc(kt_mm, 1)
                pe.wait_ge(kt_out, h + 1)
                for c in range(NC):
                    ins = mat(ps[:, 4 + c // 2, (c % 2) * DV:(c % 2 + 1) * DV], kdN[:, c], vN[:, c],
                              start=True, stop=True)
                ins.then_inc(p_mm, 1)
                pe.wait_ge(p_out, 2 * h + 1)
                mat(ps[:, 4, 0:DV], kdN[0:TS, NC], vN[0:TS, NC], start=True, stop=True).then_inc(p_mm, 1)
                pe.wait_ge(qb_s, h + 1)
                pe.wait_ge(p_out, 2 * h + 2)
                for v in range(2):
                    for c, t0, n in chunks:
                        o_ps = ps[:, 4 + v, t0:t0 + n] if c < NC else ps[:, 6, v * TS:(v + 1) * TS]
                        vs_ = slice(v * P, (v + 1) * P)
                        ins = mat(o_ps, vN[0:n, c, vs_], scT[0:n, c, 0:n], start=True, stop=(c == 0))
                        if c:
                            ins = mat(o_ps, state[:, c % NC, vs_], qe[1][:, t0:t0 + n], start=False, stop=True)
                ins.then_inc(o_mm, 1)
                pe.wait_ge(o_out, h + 1)
                for i in range(2):
                    for v in range(2):
                        ins = mat(ps[:, 4 + i, 0:TH], ones[:], ke[v][:, halves[i]], start=(v == 0), stop=(v == 1))
                ins.then_inc(rs_mm, 1)

            pe.wait_ge(x_lo, 4)
            pe.wait_ge(ones_set, 1)
            for h in range(HEADS):
                for j in range(6):
                    n = 6 * h + j
                    job(n % 2, n, xh, xh, xl, zr(n % 2), [(z_out, n - 1)] if n >= 2 else [])
                gla(h)

            with pe.Fori(0, CT) as c:
                job(0, c * 2 + A_CONV, xh, xh, xl, zr(0), [(z_out, NZ), (glu_s, c + 1)])
                job(1, c * 2 + (A_CONV + 1), xh, xh, xl, zr(1), [(sg_s, c + 1)])

            def mean_mm(s1, s2, wait, value, done):
                pe.wait_ge(wait, value)
                for j, s in enumerate((s1, s2)):
                    for i in range(2):
                        ins = mat(ps[:, 4 + 2 * j + i, 0:TH], ones[:], s[:, halves[i]], start=True, stop=True)
                ins.then_inc(done, 1)

            pe.wait_ge(head_out, HEADS)
            mean_mm(sum1, sum2, cst_s, 1, cmean_mm)

            def w_out_k(k):
                if k < CT:
                    pe.wait_ge(mix_s, k + 1)
            job(0, A_OUT, mh, mh, ml, zr(0), [(glu_s, CT + 1)], w_out_k)
            job(1, A_OUT + 1, mh, mh, ml, zr(1), [(sg_s, CT + 1)])
            with pe.Fori(1, NO // 2) as i:
                for u in range(2):
                    job(u, i * 2 + (A_OUT + u), mh, mh, ml, zr(u), [(r_s, i * 2 + (u - 1))])
            mean_mm(sum1, sum2, rst_s, 1, rmean_mm)

            def x2_k(k):
                pe.wait_ge(x2_s, k + 1)

            def q_job(u, n, first_k=None):
                job(u, n + A_Q, xh, xh, xl, zr(u), [(r_s, NO)] + ([] if first_k or isinstance(n, int) and n < 2 else [(q_out, n - 1)]),
                    first_k)

            def key_scores(u, n):
                pe.wait_ge(q_out, n + 1)
                if not (isinstance(n, int) and n < 2):
                    pe.wait_ge(s_out, n - 1)
                for tt in range(TT):
                    m = P if tt < 4 else TS
                    o_ps = ps[0:m, 4 + 2 * u, tt * P:tt * P + P] if tt < 4 else ps[0:m, 5 + 2 * u, 0:P]
                    key = skT[:, n] if isinstance(n, int) else skT[:, bass.ds(n, 1)].rearrange("p o c -> p (o c)")
                    ins = mat(o_ps, qT[:, u, tt * P:tt * P + m], key, start=True, stop=True)
                ins.then_inc(s_mm, 1)

            q_job(0, 0, x2_k)
            q_job(1, 1)
            pe.wait_ge(keys_in, 16)
            key_scores(0, 0)
            with pe.Fori(1, NQ // 2) as i:
                q_job(0, i * 2)
                key_scores(1, i * 2 - 1)
                q_job(1, i * 2 + 1)
                key_scores(0, i * 2)
            key_scores(1, NQ - 1)

            def u_tile(n, u):
                job(u, n + A_U, xh, xh, xl, zr(u), [(h_out, n + 1)])

            def g_group(q, v, bank):
                pe.wait_ge(oneh, q + 1)
                pe.wait_ge(g_out, q + 1)
                for t in range(4):
                    o_ps = ps[:, bank, t * P:(t + 1) * P]
                    mat(o_ps, oneB[:, v, t], oneAh[:, v, t], start=True, stop=False)
                    ins = mat(o_ps, oneB[:, v, t], oneAl[:, v, t], start=False, stop=True)
                ins.then_inc(g_mm, 1)

            pe.wait_ge(q_out, NQ)
            with pe.Fori(0, U_A) as i:
                for w in range(4):
                    u_tile(i * 4 + w, w % 2)

            pe.wait_ge(picks_s, 1)
            pe.wait_ge(s_out, NQ)
            for a in range(3):
                for tt in range(TT):
                    m = P if tt < 4 else TS
                    src = picks[0:m, a, tt].rearrange("p h k -> p (h k)")
                    col = a * 4 * P + tt * P
                    dst = ps[:, 4 + a, tt * P:tt * P + m] if tt < 4 else ps[:, 7, a * TS:a * TS + m]
                    ins = nc.tensor.transpose(dst, src, ident[0:m, 0:m])
            ins.then_inc(pt_mm, 1)

            pe.wait_ge(pt_out, 1)
            with pe.Fori(0, U_B) as i:
                for w in range(4):
                    u_tile(i * 4 + (4 * U_A + w), w % 2)
                    for q in range(2):
                        g_group(i * 8 + (2 * w + q), q, 4 + (2 * w + q) % 4)
            with pe.Fori(0, U_C) as i:
                for w in range(4):
                    u_tile(i * 4 + (4 * (U_A + U_B) + w), w % 2)

            def v_group(g, v):
                with pe.Fori(0, EG // 2) as i:
                    for u in range(2):
                        n = g * EG + (A_V + u)
                        pe.wait_ge(wlo, (n + 1) + i * 2)
                        pe.wait_ge(w_s, g * EG + EG)
                        for d in range(2):
                            pe.wait_ge(y_add, g * KT + (i * 4 + (2 * u + d + 1)))
                            for e in range(EG):
                                for w, m in ((wh, Wh[v]), (wh, Wl[v]), (wl, Wh[v])):
                                    for h in range(2):
                                        ins = mat(yr(d)[:, h], w[:, u, d * EG + e], m[:, e, halves[h]],
                                                  start=(e == 0 and w is wh and m is Wh[v]),
                                                  stop=(e == EG - 1 and w is wl))
                            ins.then_inc(mm, 1)

            pe.wait_ge(acc_set, 1)
            with pe.Fori(0, NG // 2) as g:
                for v in range(2):
                    v_group(g * 2 + v, v)
            mean_mm(fsum1, fsum2, n2_st, 1, n2_mm)

        @block.scalar
        def _(a):
            C = Counts(a)
            go = nc.scalar.activation

            def hi(n, u, freed):
                a.wait_ge(w_in_s[u], n * 8 + (16 - 8 * u))
                if freed is not None:
                    a.wait_ge(mm, freed)
                go(wh[:, u], wraw[:, u], ACT.Copy).then_inc(whi, 1)

            a.sem_inc(g_out, 4)
            a.sem_inc(h_out, AHEAD)
            a.sem_inc(sg_s, 1)
            for i in range(4):
                a.wait_ge(x_in[i], 16)
                go(xh[:, 4 * i:4 * i + 4], x_raw[:, 4 * i:4 * i + 4], ACT.Copy).then_inc(x_hi, 1)
            hi(0, 0, None)
            hi(1, 1, None)
            a.wait_ge(f_mm, 1)
            go(parts(flr[:]), ps[0:RANK, 4:6, 0:TH], ACT.Copy).then_inc(f_out, 1)
            a.wait_ge(consts_in, 16 * 9)

            def root(buf, n):
                a.wait_ge(inv_s, n + 1)
                go(buf[:], buf[:], ACT.Sqrt).then_inc(root_s, 1)

            def gla_state_in(h):
                a.dma_start(state[:, 0], gla_state[:, h]).then_inc(gs_in, 16)

            gla_state_in(0)

            def gla(h):
                a.wait_ge(gz_mm, h + 1)
                C.done(go(parts(qe[0][:]), yr(0), ACT.Abs, bias=gb[:, h:h + 1]), gz_ra)
                C.done(go(qe[0][:], qe[0][:], ACT.Exp, scale=-1.0), act)
                go(qe[0][:], qe[0][:], ACT.Ln, bias=1.0).then_inc(soft, 1)
                a.wait_ge(vt_mm, 2 * h + 1)
                go(vN[:, 0:NC].rearrange("p (b c) v -> p b (c v)", c=2), ps[0:CH, 4:8, :], ACT.Copy).then_inc(vt_out, 1)
                a.wait_ge(vt_mm, 2 * h + 2)
                go(vN[0:TS, NC], ps[0:TS, 4, 0:DV], ACT.Copy).then_inc(vt_out, 1)
                for l in range(6):
                    a.wait_ge(dist_s, 7 * h + l + 1)
                    n = TP if l == 0 else T
                    go(dist[l % 2][:, 0:n], dist[l % 2][:, 0:n], ACT.Exp, scale=1.0 / TAU).then_inc(decay_s, 1)
                a.wait_ge(sc_mm, 7 * h + 5)
                go(qe[0][:], bcum[:], ACT.Exp, scale=1.0 / TAU).then_inc(decay_s, 1)
                a.wait_ge(dist_s, 7 * h + 7)
                go(dist[0][:], dist[0][:], ACT.Exp, scale=1.0 / TAU).then_inc(decay_s, 1)
                a.wait_ge(kt_mm, h + 1)
                go(kdN[:, 0:NC].rearrange("p (b c) v -> p b (c v)", c=4), ps[0:CH, 4:6, :], ACT.Copy)
                go(kdN[0:TS, NC], ps[0:TS, 6, 0:P], ACT.Copy).then_inc(kt_out, 1)
                a.wait_ge(p_out, 2 * h + 2)
                a.dma_start(gla_p[:, h], state[:, NC]).then_inc(st_out, 16)
                a.dma_start(gla_s[:, h], s_new[:]).then_inc(st_out, 16)
                a.wait_ge(o_mm, h + 1)
                if h + 1 < HEADS:
                    gla_state_in(h + 1)
                for v in range(2):
                    go(z[:, 2 + v, 0:TP], ps[:, 4 + v, :], ACT.Copy)
                    go(ke[v][:, 0:TP], ps[:, 4 + v, :], ACT.Square)
                go(z[:, 2:4, TP:T], ps[:, 6, 0:2 * TS].rearrange("p (v t) -> p v t", v=2), ACT.Copy)
                for v in range(2):
                    ins = go(ke[v][:, TP:T], ps[:, 6, v * TS:(v + 1) * TS], ACT.Square)
                ins.then_inc(o_out, 1)
                root(qe[0], h)

            for h in range(HEADS):
                for j in range(6):
                    n = 6 * h + j
                    a.wait_ge(mm, n + 1)
                    if h:
                        a.wait_ge(head_out, h)
                    go(parts(z[:, j]), zr(n % 2), ACT.Silu if j >= 4 else ACT.Copy,
                       scale=DK ** -0.5 if j == 0 else 1.0).then_inc(z_out, 1)
                    hi(n + 2, n % 2, n + 1)
                gla(h)

            a.wait_ge(head_out, HEADS)
            a.dma_start(cst[:], conv_state).then_inc(cst_in, 16)
            with C.loop(CT, {}) as c:
                n0 = c * 2 + A_CONV
                a.wait_ge(mm, n0 + 1)
                hi(n0 + 2, 0, None)
                a.wait_ge(mm, n0 + 2)
                a.wait_ge(glu_s, c + 1)
                go(parts(sg[:]), zr(1), ACT.Sigmoid).then_inc(sg_s, 1)
                hi(n0 + 3, 1, None)
                a.wait_ge(yf_s, c + 1)
                a.wait_ge(csq_u, c + 1)
                go(sq[:], yf[:, bass.ds(c, 1)].rearrange("p o t -> p (o t)"), ACT.Square).then_inc(csq_s, 1)
            a.wait_ge(yf_s, CT)
            a.dma_start(conv_p, cpo[:, 0]).then_inc(cst_out, 16)
            a.dma_start(conv_s, cpo[:, 1]).then_inc(cst_out, 16)
            root(sum2, HEADS)
            for c in range(CT):
                a.wait_ge(ycn_s, c + 1)
                go(tmp[c % 2][:], tmp[c % 2][:], ACT.Silu).then_inc(ysilu_s, 1)

            with C.loop(NO // 2, {}) as i:
                for u in range(2):
                    n = i * 2 + u
                    a.wait_ge(mm, n + (A_OUT + 1))
                    hi(n + (A_OUT + 2), u, None)
                    a.wait_ge(r_s, n + 1)
                    a.wait_ge(rsq_u, n + 1)
                    go(sq[:], r1[:, bass.ds(n, 1)].rearrange("p o t -> p (o t)"), ACT.Square).then_inc(rsq_s, 1)

            root(sum2, HEADS + 1)
            a.wait_ge(sc_set, 1)

            def q_evict(u, n, hi_next):
                a.wait_ge(mm, n + (A_Q + 1))
                if not (isinstance(n, int) and n < 2):
                    a.wait_ge(s_mm, n - 1)
                go(parts(qT[:, u]), zr(u), ACT.Copy).then_inc(q_out, 1)
                if hi_next:
                    hi(n + (A_Q + 2), u, None)

            def score_evict(u, n):
                a.wait_ge(s_mm, n + 1)
                if not (isinstance(n, int) and n < 2):
                    a.wait_ge(topk_s, n - 1)
                go(sc[:, u, 0:4].rearrange("p q k -> p (q k)"), ps[:, 4 + 2 * u, :], ACT.Copy)
                go(sc[0:TS, u, 4], ps[0:TS, 5 + 2 * u, 0:P], ACT.Copy).then_inc(s_out, 1)

            q_evict(0, 0, True)
            q_evict(1, 1, True)
            score_evict(0, 0)
            with a.Fori(1, NQ // 2) as i:
                q_evict(0, i * 2, True)
                score_evict(1, i * 2 - 1)
                q_evict(1, i * 2 + 1, True)
                score_evict(0, i * 2)
            score_evict(1, NQ - 1)

            def u_tile(n, w, first):
                a.wait_ge(mm, n + (A_U + 1))
                if w % 2 == 0 and not first:
                    a.wait_ge(h_st[w // 2], (n - w) * 4)
                C.done(go(parts(hb[:, w // 2, w % 2]), zr(w % 2), ACT.Gelu), h_out)
                hi(n + (A_U + 2), w % 2, None)

            def h_store(i, w):
                d = h_dram[bass.ds(i * 2 + w // 2, 1)] if not isinstance(i, int) else h_dram[2 * i + w // 2:2 * i + w // 2 + 1]
                a.dma_start(d.rearrange("o p u t -> (o p) u t"), hb[:, w // 2]).then_inc(h_st[w // 2], 16)

            def u_four(i, first=False):
                for w in range(4):
                    u_tile(i * 4 + w, w, first)
                    if w % 2:
                        h_store(i, w)

            C.base[h_out.name] = AHEAD
            u_four(0, True)
            with C.loop(U_A - 1, {h_out: 4}) as i:
                u_four(i + 1)
            a.wait_ge(gd_s, 1)
            go(picks[:, 0], picks[:, 0], ACT.Exp).then_inc(ge_s, 1)
            a.wait_ge(pt_mm, 1)
            for j in range(3):
                go(picksT[:, j, 0:TP], ps[:, 4 + j, :], ACT.Copy)
            go(picksT[:, :, TP:T], ps[:, 7, 0:3 * TS].rearrange("p (a t) -> p a t", a=3), ACT.Copy).then_inc(pt_out, 1)

            def g_evict(c, q, first):
                a.wait_ge(g_mm, c * 8 + (q + 1 + AHEAD))
                if q == 0 and not first:
                    a.wait_ge(g_st, c * 16)
                C.done(go(gst[:, :, 4 * q:4 * q + 4].rearrange("p i t -> p t i"),
                          ps[:, 4 + q % 4, :].rearrange("p (t i) -> p t i", t=4), ACT.Copy), g_out)

            def u_and_g(c, first=False):
                for w in range(4):
                    u_tile((c + U_A) * 4 + w, w, False)
                    if w % 2:
                        h_store(c + U_A, w)
                    for q in range(2):
                        g_evict(c, 2 * w + q, first)
                d = g_dram[bass.ds(c, 1)].rearrange("o j i t -> (o j) i t") if not isinstance(c, int) else g_dram[c]
                a.dma_start(d, gst[:]).then_inc(g_st, 16)

            C.base[g_out.name] = 4
            u_and_g(0, True)
            with C.loop(U_B - 1, {h_out: 4, g_out: 8}) as i:
                u_and_g(i + 1)
            with C.loop(U_C, {h_out: 4}) as i:
                u_four(i + (U_A + U_B))
            with a.Fori(0, NKEY // 2 - 1) as i:
                for u in range(2):
                    hi(i * 2 + (A_V + u + 2), u, i * 4 + (A_V + 2 * u + 2))

            for k in range(KT):
                a.wait_ge(y_add, NG * KT + AHEAD)
                if k >= 2:
                    a.wait_ge(n2_used, k - 1)
                go(fsq[k % 2][:], acc[:, k], ACT.Square).then_inc(n2_sq, 1)
            root(fsum2, HEADS + 2)
            for k in range(0, KT, 4):
                a.wait_ge(n2_out, k + 4)
                a.dma_start(y_out[:, k:k + 4], acc[:, k:k + 4]).then_inc(y_st, 16)
            a.wait_ge(y_st, 16 * (KT // 4))
            a.wait_ge(st_out, 32 * HEADS)
            a.wait_ge(cst_out, 32)
            a.wait_ge(g_st, 16 * NGC)
            for v in range(2):
                a.wait_ge(h_st[v], 16 * (NKEY // 4))

        @block.vector
        def _(v_):
            C = Counts(v_)
            tt_, ts_, stt_, cp = (nc.vector.tensor_tensor, nc.vector.tensor_scalar,
                                  nc.vector.scalar_tensor_tensor, nc.vector.tensor_copy)

            def one(ap):
                return ap.rearrange("p o t -> p (o t)")

            v_.sem_inc(y_add, AHEAD)
            C.base[y_add.name] = AHEAD
            for s in (glu_s, csq_u, rsq_u):
                v_.sem_inc(s, 1)
                C.base[s.name] = 1
            for i in range(4):
                s = slice(4 * i, 4 * i + 4)
                v_.wait_ge(x_hi, i + 1)
                C.inc(tt_(xl[:, s], x_raw[:, s], f(xh[:, s]), ALU.subtract), x_lo)
            v_.wait_ge(x_lo, 4)
            v_.wait_ge(f_mm, 1)
            C.done(nc.vector.memset(keep[:], 1.0), dve)
            nc.vector.memset(keep[:, 0:TP:CH], 0.0)
            nc.vector.memset(keep[:, TP:TP + 1], 0.0)
            C.done(nc.vector.memset(scT[:], 0.0), dve)
            v_.wait_ge(consts_in, 16 * 9)

            def blocks(ap, l):
                m = LEVELS[l]
                n = (TP if m == CH // 2 else T) // (2 * m)
                return ap[:, 0:n * 2 * m].rearrange("p (n two m) -> p n two m", two=2, m=m), n, m

            def gla(h):
                q, k = z[:, 0], z[:, 1]
                v_.wait_ge(gz_ra, h + 1)
                C.done(ts_(parts(bcum[:]), yr(0), gb[:, h:h + 1], 0.0, ALU.add, ALU.min), gz_rd)
                v_.wait_ge(soft, h + 1)
                C.done(tt_(ke[0][:], bcum[:], qe[0][:], ALU.subtract), dve)
                C.done(nc.vector.tensor_tensor_scan(bcum[:], keep[:], ke[0][:], 0.0, ALU.mult, ALU.add), dve)

                def distances(l):
                    b, n, m = blocks(bcum, l)
                    d, _, _ = blocks(dist[l % 2], l)
                    mid = b[:, :, 0, m - 1:m].to_broadcast([P, n, m])
                    tt_(d[:, :, 0], mid, b[:, :, 0], ALU.subtract)
                    C.done(tt_(d[:, :, 1], b[:, :, 1], mid, ALU.subtract), dist_s)

                def take_scores(l):
                    v_.wait_ge(sc_mm, 7 * h + l + 1)
                    b = 4 + 2 * (l % 2)
                    m8 = masks[:, l:l + 1].to_broadcast([CH, NC, CH])
                    src = ps[0:CH, b, :].rearrange("p (c t) -> p c t", c=NC)
                    if l == 0:
                        C.done(tt_(scT[:, 0:NC], src, m8, ALU.mult), sc_out)
                        return
                    tt_(stmp[:, 0:NC], src, m8, ALU.mult)
                    dst = scT if l == 1 else stmp
                    C.done(tt_(dst[0:TS, NC, 0:TS], ps[0:TS, b + 1, 0:TS], masks[0:TS, l, 0:TS], ALU.mult), sc_out)
                    ins = tt_(scT[:, 0:NC], scT[:, 0:NC], stmp[:, 0:NC], ALU.add)
                    if l > 1:
                        ins = tt_(scT[0:TS, NC, 0:TS], scT[0:TS, NC, 0:TS], stmp[0:TS, NC, 0:TS], ALU.add)
                    C.done(ins, dve)

                distances(0)
                v_.wait_ge(z_out, 6 * h + 2)
                for l in range(6):
                    if l < 5:
                        distances(l + 1)
                    v_.wait_ge(decay_s, 8 * h + l + 1)
                    if l >= 2:
                        take_scores(l - 2)
                    n = TP if l == 0 else T
                    tt_(qe[l % 2][:, 0:n], q[:, 0:n], dist[l % 2][:, 0:n], ALU.mult)
                    C.done(tt_(ke[l % 2][:, 0:n], k[:, 0:n], dist[l % 2][:, 0:n], ALU.mult), qke)
                end = bcum[:, 0:TP].rearrange("p (c t) -> p c t", c=NC)
                tt_(dist[0][:, 0:TP].rearrange("p (c t) -> p c t", c=NC),
                    end[:, :, CH - 1:CH].to_broadcast([P, NC, CH]), end, ALU.subtract)
                C.done(tt_(dist[0][:, TP:T], bcum[:, T - 1:T].to_broadcast([P, TS]), bcum[:, TP:T], ALU.subtract),
                       dist_s)
                take_scores(4)
                take_scores(5)
                v_.wait_ge(decay_s, 8 * h + 7)
                C.done(tt_(qe[1][:], q, qe[0][:], ALU.mult), qb_s)
                take_scores(6)
                v_.wait_ge(decay_s, 8 * h + 8)
                C.done(tt_(ke[0][:], k, dist[0][:], ALU.mult), kd_s)
                v_.wait_ge(p_mm, 2 * h + 1)
                v_.wait_ge(st_out, 32 * h)
                C.done(cp(state[:, 1], ps[:, 4, 0:DV]), dve)
                for c in range(1, NC):
                    e = c * CH + CH - 1
                    C.done(stt_(state[:, c + 1], state[:, c], qe[0][:, e:e + 1],
                                ps[:, 4 + c // 2, (c % 2) * DV:(c % 2 + 1) * DV], ALU.mult, ALU.add),
                           p_out if c == NC - 1 else dve)
                v_.wait_ge(gs_in, 16 * (h + 1))
                v_.wait_ge(p_mm, 2 * h + 2)
                C.done(stt_(s_new[:], state[:, 0], qe[0][:, T - 1:T], ps[:, 4, 0:DV], ALU.mult, ALU.add), p_out)
                v_.wait_ge(rs_mm, h + 1)
                C.done(ts_(parts(qe[0][:]), yr(0), 1.0 / DV, EPS, ALU.mult, ALU.add), dve)
                C.done(nc.vector.reciprocal(qe[0][:], qe[0][:]), inv_s)
                v_.wait_ge(root_s, h + 1)
                for v in range(2):
                    C.done(stt_(z[:, 2 + v], z[:, 2 + v], ng[:, 2 * h + v:2 * h + v + 1], qe[0][:],
                                ALU.mult, ALU.mult), dve)
                v_.wait_ge(z_out, 6 * h + 6)
                for v in range(2):
                    j = CT + 2 * h + v
                    C.done(tt_(z[:, 2 + v], z[:, 2 + v], z[:, 4 + v], ALU.mult), dve)
                    C.done(cp(mh[:, j], z[:, 2 + v]), dve)
                    C.done(tt_(ml[:, j], z[:, 2 + v], f(mh[:, j]), ALU.subtract), head_out if v else dve)

            for h in range(HEADS):
                gla(h)

            v_.wait_ge(cst_in, 16)
            v_.wait_ge(st_out, 32 * HEADS)
            nc.vector.memset(ext[:, 0:NPAD], 0.0)
            nc.vector.memset(sum1[:], 0.0)
            C.done(nc.vector.memset(sum2[:], 0.0), dve)
            e_state, e_sample = NPAD + TP, NPAD + TP + NPAD
            with C.loop(CT, {dve: CW + 3, glu_s: 1, yf_s: 1, csq_u: 1}) as c:
                v_.wait_ge(mm, c * 2 + (A_CONV + 1))
                v_.wait_ge(sg_s, c + 2)
                cc = bass.ds(c, 1)
                tt_(ext[:, NPAD:NPAD + TH], ps[:, 0, 0:TH], sg[:, 0:TH], ALU.mult)
                tt_(ext[:, NPAD + TH:e_state], ps[:, 1, 0:TP - TH], sg[:, TH:TP], ALU.mult)
                C.done(tt_(ext[:, e_sample:EXT], ps[:, 1, TP - TH:TH], sg[:, TP:T], ALU.mult), glu_s)
                C.done(cp(ext[:, e_state:e_sample], one(cst[:, cc])), dve)
                cp(one(cpo[:, 0, cc]), ext[:, TP:TP + NPAD])
                C.done(cp(one(cpo[:, 1, cc]), ext[:, EXT - NPAD:EXT]), dve)
                C.lag(ts_(yb[0][:], ext[:, 0:YL], one(cwt[:, cc, 0:1]), one(cvec[:, 0:1, cc]), ALU.mult, ALU.add), dve)
                C.lag(ts_(yb[1][:], ext[:, 1:1 + YL], one(cwt[:, cc, 1:2]), None, ALU.mult), dve)
                for w in range(2, CW):
                    y_ = yb[w % 2]
                    C.lag(stt_(y_[:], ext[:, w:w + YL], one(cwt[:, cc, w:w + 1]), y_[:], ALU.mult, ALU.add), dve)
                v_.wait_ge(dve, C.value(dve))
                tt_(one(yf[:, cc, 0:TP]), yb[0][:, 0:TP], yb[1][:, 0:TP], ALU.add)
                C.done(tt_(one(yf[:, cc, TP:T]), yb[0][:, e_state:YL], yb[1][:, e_state:YL], ALU.add), yf_s)
                C.done(tt_(sum1[:], sum1[:], one(yf[:, cc]), ALU.add), dve)
                v_.wait_ge(csq_s, c + 1)
                C.done(tt_(sum2[:], sum2[:], sq[:], ALU.add), csq_u)
            v_.sem_inc(cst_s, 1)

            def norm_stats(n, s1, s2, t):
                C.done(ts_(parts(s1[:]), yr(0), 1.0 / n, None, ALU.mult), dve)
                C.done(tt_(t[:], s1[:], s1[:], ALU.mult), dve)
                C.done(stt_(parts(s2[:]), yr(1), 1.0 / n, parts(t[:]), ALU.mult, ALU.subtract), dve)
                C.done(ts_(s2[:], s2[:], 0.0, EPS, ALU.max, ALU.add), dve)
                C.done(nc.vector.reciprocal(s2[:], s2[:]), inv_s)
                v_.wait_ge(root_s, C.base[inv_s.name])

            v_.wait_ge(cmean_mm, 1)
            norm_stats(CONV, sum1, sum2, tmp[0])
            v_.wait_ge(cst_out, 32)

            def mix_out(c):
                t = tmp[c % 2]
                v_.wait_ge(ysilu_s, c + 1)
                C.done(cp(mh[:, c], t[:]), dve)
                C.done(tt_(ml[:, c], t[:], f(mh[:, c]), ALU.subtract), mix_s)

            for c in range(CT):
                t = tmp[c % 2]
                C.done(tt_(t[:], yf[:, c], sum1[:], ALU.subtract), dve)
                C.done(tt_(t[:], t[:], sum2[:], ALU.mult), dve)
                C.done(ts_(t[:], t[:], cvec[:, 1, c:c + 1], cvec[:, 2, c:c + 1], ALU.mult, ALU.add), ycn_s)
                if c:
                    mix_out(c - 1)
            mix_out(CT - 1)

            nc.vector.memset(sum1[:], 0.0)
            C.done(nc.vector.memset(sum2[:], 0.0), dve)
            with C.loop(NO // 2, {dve: 4, r_s: 2, rsq_u: 2}) as i:
                for u in range(2):
                    n = bass.ds(i * 2 + u, 1)
                    v_.wait_ge(mm, i * 2 + (A_OUT + u + 1))
                    C.done(stt_(parts(one(r1[:, n])), parts(one(f(xh[:, n]))), ALPHA, zr(u), ALU.mult, ALU.add), dve)
                    C.done(stt_(one(r1[:, n]), one(f(xl[:, n])), ALPHA, one(r1[:, n]), ALU.mult, ALU.add), r_s)
                    C.done(tt_(sum1[:], sum1[:], one(r1[:, n]), ALU.add), dve)
                    v_.wait_ge(rsq_s, i * 2 + (u + 1))
                    C.done(tt_(sum2[:], sum2[:], sq[:], ALU.add), rsq_u)
            v_.sem_inc(rst_s, 1)
            C.done(nc.vector.memset(sc[:], 0.0), sc_set)
            v_.wait_ge(rmean_mm, 1)
            norm_stats(D, sum1, sum2, tmp[0])
            for k0 in range(0, KT, 2):
                ks = [(k0, tmp[0]), (k0 + 1, tmp[1])]
                for k, t in ks:
                    C.lag(tt_(t[:], r1[:, k], sum1[:], ALU.subtract), dve)
                for k, t in ks:
                    C.lag(tt_(t[:], t[:], sum2[:], ALU.mult), dve)
                for k, t in ks:
                    C.lag(ts_(t[:], t[:], lvec[:, 0, k:k + 1], lvec[:, 1, k:k + 1], ALU.mult, ALU.add), dve)
                for k, t in ks:
                    C.lag(cp(xh[:, k], t[:]), dve)
                v_.wait_ge(dve, C.value(dve))
                for k, t in ks:
                    ins = tt_(xl[:, k], t[:], f(xh[:, k]), ALU.subtract)
                    C.inc(ins, x2_s)
                v_.wait_ge(x2_s, C.value(x2_s))

            LOWEST = -3.0e38

            def top16(vals, work, best, num, used):
                for tt in range(TT):
                    ins = nc.vector.max(best[:, tt, 0:8], vals[:, tt])
                C.done(ins, dve)
                for tt in range(TT):
                    nc.vector.max_index(num[:, tt, 0:8], best[:, tt, 0:8], vals[:, tt])
                    ins = nc.vector.match_replace(work[:, tt], best[:, tt, 0:8], vals[:, tt], LOWEST)
                C.done(ins, used)
                for tt in range(TT):
                    ins = nc.vector.max(best[:, tt, 8:16], work[:, tt])
                C.done(ins, dve)
                for tt in range(TT):
                    ins = nc.vector.max_index(num[:, tt, 8:16], best[:, tt, 8:16], work[:, tt])
                C.done(ins, dve)

            for h in range(PH):
                for p in range(2):
                    v_.wait_ge(s_out, 2 * h + p + 1)
                    top16(sc[:, p], scw, sv[:, p], si[:, p], topk_s)
                C.done(cp(sif[:], si[:]), dve)
                s4 = [P, TT, 16, 16]
                C.done(tt_(cand[:].rearrange("p t (a b) -> p t a b", a=16),
                           sv[:, 0].unsqueeze(3).to_broadcast(s4), sv[:, 1].unsqueeze(2).to_broadcast(s4), ALU.add), dve)
                top16(cand, candw, bs, pos, dve)
                cp(picks[:, 0, :, h], bs[:])
                ts_(pab[:, 0], pos[:], 4, None, ALU.logical_shift_right)
                C.done(ts_(pab[:, 1], pos[:], 15, None, ALU.bitwise_and), dve)
                C.done(cp(pabf[:], pab[:]), dve)
                flat = [P, TT * 16, 16]
                oh3 = oh[:].rearrange("p t k a -> p (t k) a")
                for p in range(2):
                    at_ = pabf[:, p].rearrange("p t k -> p (t k)").unsqueeze(2).to_broadcast(flat)
                    C.done(tt_(oh3, at_, iota[:, 0:16].unsqueeze(1).to_broadcast(flat), ALU.is_equal), dve)
                    C.done(tt_(oh[:], oh[:], sif[:, p].unsqueeze(2).to_broadcast(s4), ALU.mult), dve)
                    C.done(nc.vector.tensor_reduce(picks[:, 1 + p, :, h], oh[:], AX, ALU.add), dve)

            g2 = picks[:, 0].rearrange("p t h k -> p (t h) k")
            C.done(cp(gsum[:], g2[:, :, 0]), dve)
            gs_b = gsum[:].unsqueeze(2).to_broadcast([P, TT * PH, 16])
            C.done(tt_(g2, g2, gs_b, ALU.subtract), gd_s)
            v_.wait_ge(ge_s, 1)
            C.done(nc.vector.tensor_reduce(gsum[:], g2, AX, ALU.add), dve)
            C.done(nc.vector.reciprocal(gsum[:], gsum[:]), dve)
            C.done(tt_(g2, g2, gs_b, ALU.mult), picks_s)

            v_.wait_ge(pt_out, 1)
            C.done(cp(gate_h[:], picksT[:, 0]), dve)
            C.done(tt_(gate_l[:], picksT[:, 0], f(gate_h[:]), ALU.subtract), dve)
            with C.loop(T // 8, {oneh: 2}) as i:
                for u in range(2):
                    v_.wait_ge(g_mm, i * 2 + (u + 1))
                    for t in range(4):
                        tok = bass.ds(i * 8 + (4 * u + t), 1)
                        ts_(oneAh[:, u, t], iota[:], picksT[:, 1, tok], f(gate_h[:, tok]), ALU.is_equal, ALU.mult)
                        ts_(oneAl[:, u, t], iota[:], picksT[:, 1, tok], f(gate_l[:, tok]), ALU.is_equal, ALU.mult)
                        ins = ts_(oneB[:, u, t], iota[:], picksT[:, 2, tok], None, ALU.is_equal)
                    C.inc(ins, oneh)

            v_.wait_ge(g_mm, T // 4 + AHEAD)
            with C.loop(KT, {dve: 2}) as k:
                kk = bass.ds(k, 1)
                C.done(ts_(one(acc[:, kk]), one(f(xh[:, kk])), ALPHA, None, ALU.mult), dve)
                C.done(stt_(one(acc[:, kk]), one(f(xl[:, kk])), ALPHA, one(acc[:, kk]), ALU.mult, ALU.add), dve)
            v_.sem_inc(acc_set, 1)

            def make_w(g, v, es):
                for j, e in enumerate(es):
                    v_.wait_ge(g_in, g * 16 + 16)
                    v_.wait_ge(h_in, g * 16 + 16)
                    gate = gt[:, :, e].rearrange("p c o t -> p c (o t)")
                    hh = one(hg[:, e]).rearrange("p (c t) -> p c t", c=NGC)
                    C.lag(tt_(wt[j][:].rearrange("p (c t) -> p c t", c=NGC), hh, gate, ALU.mult), dve)
                for j, e in enumerate(es):
                    C.lag(cp(one(Wh[v][:, e]), wt[j][:]), dve)
                v_.wait_ge(dve, C.value(dve))
                for j, e in enumerate(es):
                    C.inc(tt_(one(Wl[v][:, e]), wt[j][:], one(f(Wh[v][:, e])), ALU.subtract), w_s)
                v_.wait_ge(w_s, C.value(w_s))

            def add_y(g, i, u):
                for d in range(2):
                    v_.wait_ge(mm, (g * KT + (A_V + 2 * u + d + 1)) + i * 4)
                    dd = bass.ds(i * 4 + (2 * u + d), 1)
                    a_ = parts(one(acc[:, dd]))
                    C.done(tt_(a_, a_, yr(d), ALU.add), y_add)

            v_.wait_ge(mm, A_V)
            with C.loop(EG // 2, {dve: 4, w_s: 2}) as i:
                make_w(0, 0, [bass.ds(i * 2 + j, 1) for j in range(2)])

            def v_group(g, v, more):
                with C.loop(EG // 4, {y_add: 4}) as i:
                    for u in range(2):
                        add_y(g, i, u)
                with C.loop(EG // 4, {y_add: 4, dve: 8 * more, w_s: 4 * more}) as i:
                    for u in range(2):
                        if more:
                            make_w(g + 1, 1 - v, [bass.ds(i * 4 + (2 * u + j), 1) for j in range(2)])
                        add_y(g, i + EG // 4, u)

            with C.loop(NG // 2 - 1, {y_add: 2 * KT, dve: 32, w_s: 2 * EG}) as g:
                for v in range(2):
                    v_group(g * 2 + v, v, True)
            v_group(NG - 2, 0, True)
            v_group(NG - 1, 1, False)

            nc.vector.memset(fsum1[:], 0.0)
            C.done(nc.vector.memset(fsum2[:], 0.0), dve)
            for k in range(KT):
                C.done(tt_(fsum1[:], fsum1[:], acc[:, k], ALU.add), dve)
                v_.wait_ge(n2_sq, k + 1)
                C.done(tt_(fsum2[:], fsum2[:], fsq[k % 2][:], ALU.add), n2_used)
            v_.sem_inc(n2_st, 1)
            v_.wait_ge(n2_mm, 1)
            norm_stats(D, fsum1, fsum2, fsq[0])
            for k in range(KT):
                C.done(tt_(acc[:, k], acc[:, k], fsum1[:], ALU.subtract), dve)
                C.done(tt_(acc[:, k], acc[:, k], fsum2[:], ALU.mult), dve)
                C.done(ts_(acc[:, k], acc[:, k], lvec[:, 2, k:k + 1], lvec[:, 3, k:k + 1], ALU.mult, ALU.add), n2_out)


def _tiles(w, cols):
    n = w.shape[1] // cols
    return np.ascontiguousarray(w.reshape(-1, P, n, cols).transpose(2, 1, 0, 3))


def _by_feature(a):
    return np.ascontiguousarray(a.T.reshape(-1, P, a.shape[0]).transpose(1, 0, 2))


def _level_masks():
    s, t = np.arange(CH)[:, None], np.arange(CH)[None, :]
    m = [((s // l) % 2 == 0) & (t // l == s // l + 1) for l in LEVELS] + [s == t]
    return np.ascontiguousarray(np.stack(m, 1).astype(np.float32))


def kernel(x_prompt, x_sample, state_conv, state_gla, w_in, conv_w, conv_b, conv_ln_g, conv_ln_b,
           gla_gate_w, gla_gate_b, gla_norm_g, w_out, ln1_g, ln1_b, peer_w_query, peer_sub_keys,
           peer_u, peer_v, ln2_g, ln2_b):
    import concourse.bacc as bacc
    from concourse.bass_utils import run_bass_kernel_spmd

    w_in = np.asarray(w_in)[0]
    QK, V = HEADS * DK, HEADS * DV
    o = np.cumsum([0, CONV, CONV, QK, QK, V, V])
    part = {n: _tiles(w_in[:, o[i]:o[i + 1]], P) for i, n in enumerate(["val", "gate", "q", "k", "v", "g"])}
    order = []
    for h in range(HEADS):
        order += [part["q"][h], part["k"][h], part["v"][2 * h], part["v"][2 * h + 1],
                  part["g"][2 * h], part["g"][2 * h + 1]]
    for c in range(CT):
        order += [part["val"][c], part["gate"][c]]

    def vec(a):
        return np.asarray(a)[0].reshape(-1, P).T

    pv = np.asarray(peer_v)[0].reshape(NG, EG, P, EG, 2, P).transpose(0, 3, 2, 4, 1, 5)
    ins = {
        "xT": _by_feature(np.concatenate([np.asarray(x_prompt)[0], np.asarray(x_sample)[0]], 0)),
        "w_in": np.stack(order),
        "w_f": _tiles(w_in[:, o[6]:], RANK)[0],
        "w_out": _tiles(np.asarray(w_out)[0], P),
        "w_q": _tiles(np.asarray(peer_w_query)[0], P),
        "u_t": np.ascontiguousarray(np.asarray(peer_u)[0].reshape(NKEY, P, KT, P).transpose(0, 3, 2, 1)),
        "v_t": np.ascontiguousarray(pv).reshape(NG * EG, P, KT, P),
        "conv_state": np.ascontiguousarray(np.asarray(state_conv)[0, 0].T.reshape(CT, P, NPAD).transpose(1, 0, 2)),
        "conv_w": np.ascontiguousarray(np.asarray(conv_w)[0].T.reshape(CT, P, CW).transpose(1, 0, 2)),
        "conv_vec": np.ascontiguousarray(np.stack([vec(conv_b), vec(conv_ln_g), vec(conv_ln_b)], 1)),
        "gla_state": np.ascontiguousarray(np.asarray(state_gla)[0, 0].transpose(1, 0, 2)),
        "gate_w": np.ascontiguousarray(np.asarray(gla_gate_w)[0].reshape(RANK, HEADS, P)),
        "gate_b": np.ascontiguousarray(vec(gla_gate_b)),
        "norm_g": np.ascontiguousarray(vec(gla_norm_g)),
        "ln_vec": np.ascontiguousarray(np.stack([vec(ln1_g), vec(ln1_b), vec(ln2_g), vec(ln2_b)], 1)),
        "sub_keys": np.ascontiguousarray(
            np.asarray(peer_sub_keys)[0].reshape(2 * PH, NKEY, P).transpose(2, 0, 1)),
        "ident": np.eye(P, dtype=np.float32),
        "iota": np.ascontiguousarray(np.broadcast_to(np.arange(P, dtype=np.float32), (P, P))),
        "masks": _level_masks(),
    }
    outs = {"y": (P, KT, T), "conv_p": (P, CT, NPAD), "conv_s": (P, CT, NPAD),
            "gla_p": (P, HEADS, DV), "gla_s": (P, HEADS, DV)}
    nc = bacc.Bacc("TRN2", target_bir_lowering=False, num_devices=1)
    args = [nc.dram_tensor("in_" + n, a.shape, F32, kind="ExternalInput").ap() for n, a in ins.items()]
    args += [nc.dram_tensor("out_" + n, s, F32, kind="ExternalOutput").ap() for n, s in outs.items()]
    args.append(nc.dram_tensor("g_scratch", (NGC, P, P, GC), F32, kind="Internal").ap())
    args.append(nc.dram_tensor("h_scratch", (NKEY // 2, P, 2, T), F32, kind="Internal").ap())
    program(nc, *args)
    r = run_bass_kernel_spmd(nc, [{"in_" + n: a for n, a in ins.items()}], core_ids=[0]).results[0]
    y = np.asarray(r["out_y"]).transpose(2, 1, 0).reshape(T, D)

    def rows(a):
        return np.ascontiguousarray(np.asarray(a).transpose(2, 1, 0).reshape(1, 1, NPAD, CONV))

    def states(a):
        return np.ascontiguousarray(np.asarray(a).transpose(1, 0, 2))[None, None]

    return (np.ascontiguousarray(y[None, :TP]), np.ascontiguousarray(y[None, TP:]),
            rows(r["out_conv_p"]), states(r["out_gla_p"]), rows(r["out_conv_s"]), states(r["out_gla_s"]))
```

```python
from contextlib import ExitStack

import numpy as np

import concourse.bass as bass
from concourse import mybir
from concourse.alu_op_type import AluOpType as ALU

F32 = mybir.dt.float32
F32R = mybir.dt.float32r
BF16 = mybir.dt.bfloat16
U32 = mybir.dt.uint32
I32 = mybir.dt.int32
ACT = mybir.ActivationFunctionType
AX = mybir.AxisListType.X

P = 128
TP, TS = 512, 32
T = TP + TS
TH = T // 2
D = 2048
KT = D // P
CONV, CW = 1024, 31
CT = CONV // P
NPAD = CW - 1
EXT = NPAD + TP + NPAD + TS
YL = EXT - NPAD
HEADS, DK, DV, RANK = 4, 128, 256, 16
TAU = 16.0
CH = 64
NC = TP // CH
PH, NKEY, TOPK = 8, 128, 16
TT = 5
EG = 8
NG = NKEY // EG
GC = 32
NGC = T // GC
EPS = 1e-5
ALPHA = 2.0 ** 0.25
AHEAD = 2
LEVELS = (32, 16, 8, 4, 2, 1)


class Counts:

    def __init__(self, eng):
        self.eng, self.base, self.loops = eng, {}, []

    def value(self, sem):
        v = self.base.get(sem.name, 0)
        for reg, per in self.loops:
            if per.get(sem.name, 0):
                v = reg * per[sem.name] + v
        return v

    def inc(self, ins, sem):
        ins.then_inc(sem, 1)
        self.base[sem.name] = self.base.get(sem.name, 0) + 1

    def done(self, ins, sem):
        self.inc(ins, sem)
        self.eng.wait_ge(sem, self.value(sem))

    def lag(self, ins, sem):
        self.inc(ins, sem)
        v = self.value(sem)
        if not (isinstance(v, int) and v <= 1):
            self.eng.wait_ge(sem, v - 1)

    def loop(self, n, per):
        return _Loop(self, n, per)


class _Loop:
    def __init__(self, c, n, per):
        self.c, self.n, self.per = c, n, {s.name: k for s, k in per.items()}

    def __enter__(self):
        self.fori = self.c.eng.Fori(0, self.n)
        reg = self.fori.__enter__()
        self.before = dict(self.c.base)
        self.c.loops.append((reg, self.per))
        return reg

    def __exit__(self, *e):
        self.c.loops.pop()
        if e[0] is None:
            for name in set(self.c.base) | set(self.per):
                got = self.c.base.get(name, 0) - self.before.get(name, 0)
                assert got == self.per.get(name, 0), (name, got, self.per.get(name, 0))
                self.c.base[name] = self.before.get(name, 0) + self.n * got
        return self.fori.__exit__(*e)


def program(nc, xT, w_in, w_f, w_out, w_q, u_t, v_t, conv_state, conv_w, conv_vec, gla_state,
            gate_w, gate_b, norm_g, ln_vec, sub_keys, ident_in, iota_in, masks_in,
            y_out, conv_p, conv_s, gla_p, gla_s, g_dram, h_dram, yf_dram, hf_dram):
    ctx = ExitStack()
    with ctx:
        lo0 = -(-nc.sbuf_base // 32) * 32

        def at(name, shape, dt, off):
            return nc.alloc_sbuf_tensor_at(name, shape, dt, offset=lo0 + off)

        def sem(name):
            return ctx.enter_context(nc.semaphore(name))

        ROW = T * 4
        X0, X1 = 0, KT * ROW
        M0, M1 = 2 * KT * ROW, 3 * KT * ROW
        R0 = 4 * KT * ROW
        TILE = KT * P * 4
        C0 = R0 + 6 * TILE
        S0 = C0 + 2656
        xh = at("xh", [P, KT, T], F32R, X0)
        xl = at("xl", [P, KT, T], F32R, X1)
        r1 = at("r1", [P, KT, T], F32, X0)
        mh = at("mh", [P, KT, T], F32R, M0)
        ml = at("ml", [P, KT, T], F32R, M1)
        x_raw = at("x_raw", [P, KT, T], F32, M0)
        wraw = at("wraw", [P, 2, KT, P], F32, R0)
        wh = at("wh", [P, 2, KT, P], F32R, R0 + 2 * TILE)
        wl = at("wl", [P, 2, KT, P], F32R, R0 + 4 * TILE)
        ident = at("ident", [P, P], F32, C0)
        ones = at("ones", [P, P], F32, C0 + 512)
        iota = at("iota", [P, P], F32, C0 + 1024)
        cvec = at("cvec", [P, 3, CT], F32, C0 + 1536)
        gb = at("gb", [P, HEADS], F32, C0 + 1632)
        ng = at("ng", [P, HEADS * 2], F32, C0 + 1664)
        lvec = at("lvec", [P, 4, KT], F32, C0 + 1696)
        wf_raw = at("wf_raw", [P, KT, RANK], F32, M1)
        z = at("z", [P, 6, T], F32, M0)
        bcum = at("bcum", [P, T], F32, M0 + 6 * ROW)
        keep = at("keep", [P, T], F32, M0 + 7 * ROW)
        state = at("state", [P, NC + 1, DV], F32, M1)
        kdN = at("kdN", [CH, NC + 1, P], F32, M1 + 9216)
        dist0 = at("dist0", [P, T], F32, M1 + 9216 + 4608)
        qe = [at(f"qe{u}", [P, T], F32, M0 + (14 + u) * ROW) for u in range(2)]
        ke = [at(f"ke{u}", [P, T], F32, M1 + (14 + u) * ROW) for u in range(2)]
        masks = at("masks", [CH, 7, CH], F32, S0)
        gw = at("gw", [RANK, HEADS, P], F32, S0 + 1792)
        flr = at("flr", [RANK, T], F32, S0 + 3840)
        vN = at("vN", [CH, NC + 1, DV], F32, S0 + 6016)
        scT = at("scT", [CH, NC + 1, CH], F32, S0 + 15232)
        dist1 = at("dist1", [P, T], F32, S0 + 17536)
        s_new = at("s_new", [P, DV], F32, S0 + 19712)
        cwt = at("cwt", [P, CT, CW], F32, S0 + 20768)
        dist = [dist0, dist1]
        stmp = at("stmp", [CH, NC + 1, CH], F32, M1 + 9216)
        hf = at("hf", [P, CT, T], F32, M1 + CT * ROW)
        E0 = M0 + CT * ROW
        ext = at("ext", [P, 2, EXT], F32, E0)
        csum1 = at("csum1", [P, T], F32, E0 + 2 * EXT * 4)
        csum2 = at("csum2", [P, T], F32, E0 + 2 * EXT * 4 + ROW)
        E1 = E0 + 2 * EXT * 4 + 2 * ROW
        cst = at("cst", [P, CT, NPAD], F32, E1)
        cpo = at("cpo", [P, 2, CT, NPAD], F32, E1 + CT * NPAD * 4)
        assert E1 + 3 * CT * NPAD * 4 <= M0 + 14 * ROW
        F0 = M1 + CT * ROW
        yb = [at("yb0", [P, YL], F32, F0), at("yb1", [P, YL], F32, F0 + 2304)]
        yfb = at("yfb", [P, 2, T], F32, F0 + 4608)
        csq = at("csq", [P, T], F32, F0 + 8960)
        yf = at("yf", [P, CT, T], F32, M1)
        sum1 = at("sum1", [P, T], F32, S0 + 9344)
        sum2 = at("sum2", [P, T], F32, S0 + 11520)
        sq = at("sq", [P, T], F32, S0 + 13696)
        tmp = [at(f"tmp{u}", [P, T], F32, S0 + 15872 + u * ROW) for u in range(2)]
        x2t = [at(f"x2t{u}", [P, T], F32, S0 + u * ROW) for u in range(4)]
        SC = 4
        qT = at("qT", [P, 2, T], F32, M0)
        skT = at("skT", [P, 2 * PH, P], F32, M0 + 2 * ROW)
        o = M1
        sc = at("sc", [P, SC, TT, P], F32, o); o += SC * TT * P * 4
        scw = at("scw", [P, TT, P], F32, o); o += TT * P * 4
        cand = at("cand", [P, TT, 256], F32, o); o += TT * 1024
        candw = at("candw", [P, TT, 256], F32, o); o += TT * 1024
        oh = at("oh", [P, TT, 16, 16], F32, o); o += TT * 1024
        sv = at("sv", [P, 2, TT, 16], F32, o); o += 640
        si = at("si", [P, 2, TT, 16], U32, o); o += 640
        sif = at("sif", [P, 2, TT, 16], F32, o); o += 640
        bs = at("bs", [P, TT, 16], F32, o); o += 320
        pos = at("pos", [P, TT, 16], U32, o); o += 320
        pab = at("pab", [P, 2, TT, 16], U32, o); o += 640
        pabf = at("pabf", [P, 2, TT, 16], F32, o); o += 640
        assert o <= M1 + KT * ROW, o - M1
        picks = at("picks", [P, 3, TT, PH, 16], F32, S0)
        gsum = at("gsum", [P, TT * PH], F32, S0 + 7680)
        picksT = at("picksT", [P, 3, T], F32, S0 + 7840)
        gate_p = [at(f"gate_p{a}", [P, T], F32, S0 + 14368 + a * ROW) for a in range(3)]
        hb = at("hb", [P, 2, 2, T], F32, M0)
        OH = 2 * 4 * P * 2
        gst = [at("gst0", [P, P, GC], F32, M0 + 4 * ROW), at("gst1", [P, P, GC], F32, M1 + 4 * OH)]
        part = at("part", [P, T], BF16, M1 + 4 * OH + P * GC * 4)
        oneA = [at(f"oneA{a}", [P, 2, 4, P], BF16, M1 + a * OH) for a in range(3)]
        oneB = at("oneB", [P, 2, 4, P], BF16, M1 + 3 * OH)
        Wh = [at(f"Wh{v}", [P, EG, T], F32R, X0 + v * KT * ROW) for v in range(2)]
        Wl = [at(f"Wl{v}", [P, EG, T], F32R, X0 + v * KT * ROW + EG * ROW) for v in range(2)]
        acc = at("acc", [P, KT, T], F32, M1)
        gt = at("gt", [P, NGC, EG, GC], F32, S0)
        hg = at("hg", [P, EG, T], F32, M0 + 4 * ROW)
        wt = [at(f"wt{v}", [P, T], F32, S0 + EG * ROW + v * ROW) for v in range(2)]
        fsum1 = at("fsum1", [P, T], F32, M0)
        fsum2 = at("fsum2", [P, T], F32, M0 + ROW)
        fsq = [at(f"fsq{u}", [P, T], F32, M0 + (2 + u) * ROW) for u in range(2)]

        ps = ctx.enter_context(nc.psum_tensor("ps", [P, 8, 512], F32))

        x_in = [sem(f"x_in{i}") for i in range(4)]
        consts_in, wf_in, keys_in = sem("consts_in"), sem("wf_in"), sem("sub_keys_in")
        w_in_s = [sem("w_slot0_in"), sem("w_slot1_in")]
        whi, wlo = sem("w_hi_split"), sem("w_lo_split")
        mm = sem("tile_mm_done")
        x_hi, x_lo = sem("x_hi_split"), sem("x_lo_split")
        f_mm, f_out, z_out, ones_set = sem("f_mm"), sem("f_out"), sem("z_out"), sem("ones_set")
        dve, act = sem("dve_step"), sem("act_step")
        gz_mm, soft, gz_ra, gz_rd = sem("gate_mm"), sem("softplus"), sem("gate_read_act"), sem("gate_read_dve")
        vt_mm, vt_out, kt_mm, kt_out = sem("v_turned"), sem("v_out"), sem("k_turned"), sem("k_out")
        dist_s, decay_s, qke, sc_mm, sc_out = (
            sem("distances"), sem("decays"), sem("qk_decayed"), sem("score_mm"), sem("score_out"))
        qb_s, kd_s, p_mm, p_out, o_mm, o_out, rs_mm, head_out = (
            sem("q_from_start"), sem("k_to_end"), sem("kv_mm"), sem("states"), sem("o_mm"), sem("o_out"),
            sem("rms_mm"), sem("head_done"))
        gs_in, st_out = sem("gla_state_in"), sem("gla_state_out")
        cst_in, cst_out = sem("conv_state_in"), sem("conv_state_out")
        sg_s, glu_s, yf_s, csq_s, csq_u, yf_st, cst_s, cmean_mm, stat_s, ycn_s, ysilu_s, mixh_s, mix_s, mixc_s = (
            sem("gate_sigmoid"), sem("glu_done"), sem("conv_done"), sem("conv_square"),
            sem("conv_square_used"), sem("conv_stored"),
            sem("conv_sums"), sem("conv_mean_mm"), sem("conv_stats_moved"), sem("conv_normed"),
            sem("conv_silu"), sem("mix_hi"), sem("head_mix_ready"),
            sem("conv_mix_ready"))
        tap_s, hf_st, hf_in = sem("conv_tap"), sem("head_stored"), sem("heads_back")
        yf_in = [sem("conv_back0"), sem("conv_back1")]
        r_s, rsq_s, rsq_u, rst_s, rmean_mm, x2n_s, x2a_s, x2h_s, x2_s, sc_set = (
            sem("residual_ready"), sem("residual_square"), sem("residual_square_used"), sem("norm1_sums"),
            sem("norm1_mean_mm"), sem("x2_normed"), sem("x2_scaled"), sem("x2_hi"), sem("x2_ready"),
            sem("score_pad_set"))
        inv_s, root_s = sem("inverse_variance"), sem("inverse_deviation")
        q_out, s_mm, s_out, topk_s, gd_s, ge_s, picks_s, pt_mm, pt_out = (
            sem("q_out"), sem("key_scores"), sem("key_scores_out"), sem("head_picked"), sem("gate_diff"),
            sem("gate_exp"), sem("picks_ready"), sem("picks_turned"), sem("picks_turned_out"))
        oneh, g_mm, g_out = sem("one_hots"), sem("g_mm"), sem("g_out")
        g_st, h_st = [sem("g_stored0"), sem("g_stored1")], [sem("h_stored0"), sem("h_stored1")]
        g_in, h_in = sem("g_group_in"), sem("h_group_in")
        h_out, w_s, y_add, acc_set = sem("gelu_out"), sem("w_ready"), sem("y_added"), sem("acc_set")
        wp_s, wh_s = sem("w_product"), sem("w_hi")
        n2_sq, n2_used, n2_st, n2_mm, n2_dve, n2_pool, n2_out, y_st = (
            sem("norm2_square"), sem("norm2_square_used"), sem("norm2_sums"), sem("norm2_mean_mm"),
            sem("norm2_by_dve"), sem("norm2_by_pool"), sem("norm2_out"), sem("y_stored"))
        POOL_K = range(2, KT, 3)

        NZ, NCV, NO, NQ = 6 * HEADS, 2 * CT, KT, 2 * PH
        A_OUT, A_Q, A_U = NZ + NCV, NZ + NCV + NO, NZ + NCV + NO + NQ
        BLK = 10
        assert BLK * HEADS == A_OUT and 2 * HEADS == CT
        A_V = A_U + NKEY
        U_A, U_B = 4, NGC
        U_C = NKEY // 4 - U_A - U_B

        halves = [slice(h * TH, (h + 1) * TH) for h in range(2)]
        e_state, e_sample = NPAD + TP, NPAD + TP + NPAD

        def n_conv(c):
            return BLK * (c // 2) + 2 * (c % 2)

        def n_head(h, j):
            return BLK * h + 4 + j

        chunks = [(c, c * CH, CH) for c in range(NC)] + [(NC, TP, TS)]

        def parts(a):
            return a.rearrange("p (h t) -> p h t", h=2)

        def zr(u):
            return ps[:, 2 * u:2 * u + 2, 0:TH]

        def yr(u):
            return ps[:, 4 + 2 * u:6 + 2 * u, 0:TH]

        def f(ap):
            return ap.bitcast(F32)

        block = ctx.enter_context(nc.Block())

        @block.sync
        def _(sp):
            def load(dst, src, s):
                sp.dma_start(dst, src).then_inc(s, 16)

            def tile(src, u):
                load(wraw[:, u], src, w_in_s[u])

            def pairs(w):
                return w.rearrange("(n u) p k c -> n u p k c", u=2)

            load(x_raw[:, 0:4], xT[:, 0:4], x_in[0])
            load(wf_raw[:], w_f, wf_in)
            tile(pairs(w_in)[0, 0], 0)
            for i in range(1, 4):
                load(x_raw[:, 4 * i:4 * i + 4], xT[:, 4 * i:4 * i + 4], x_in[i])
            tile(pairs(w_in)[0, 1], 1)
            for dst, src in ((ident, ident_in), (iota, iota_in), (cvec, conv_vec), (gb, gate_b), (ng, norm_g),
                             (lvec, ln_vec), (masks, masks_in), (gw, gate_w), (cwt, conv_w)):
                load(dst[:], src, consts_in)

            def stream(src, n0, i0, i1):
                s = pairs(src)
                with sp.Fori(0, i1 - i0) as i:
                    for u in range(2):
                        sp.wait_ge(wlo, i * 2 + (n0 + u - 1))
                        tile(s[bass.ds(i + i0, 1), u].rearrange("o p k c -> (o p) k c"), u)

            stream(w_in, 2, 1, (NZ + NCV) // 2)
            stream(w_out, A_OUT, 0, NO // 2)
            s = pairs(w_q)
            for u in range(2):
                sp.wait_ge(wlo, A_Q + u - 1)
                tile(s[0, u], u)
            sp.wait_ge(mm, A_Q)
            load(skT[:], sub_keys, keys_in)
            stream(w_q, A_Q + 2, 1, NQ // 2)
            stream(u_t, A_U, 0, NKEY // 2)
            gsrc = g_dram.rearrange("c j (g e) t -> g j c (e t)", e=EG)
            hsrc = h_dram.rearrange("(g n) p u t -> g p n (u t)", n=EG // 2)
            vs = v_t.rearrange("(g n u) p k c -> g n u p k c", u=2, n=EG // 2)

            def group_in(g):
                for dst, src, q in ((gt[:].rearrange("p c e t -> p c (e t)"), gsrc, g_in),
                                    (hg[:].rearrange("p (n u) t -> p n (u t)", u=2), hsrc, h_in)):
                    a = src[g] if isinstance(g, int) else src[bass.ds(g, 1)].rearrange("o p n q -> (o p) n q")
                    load(dst, a, q)

            def v_pairs(g, i0, i1):
                with sp.Fori(i0, i1) as i:
                    for u in range(2):
                        sp.wait_ge(wlo, (g * EG + (A_V - 1 + u)) + i * 2)
                        t = vs[bass.ds(g, 1), bass.ds(i, 1), u]
                        tile(t.rearrange("o q p k c -> (o q p) k c"), u)

            for v in range(2):
                sp.wait_ge(g_st[v], 16 * (NGC // 2 + 1))
            for v in range(2):
                sp.wait_ge(h_st[v], 16 * (EG // 4))
            group_in(0)
            with sp.Fori(0, NG - 1) as g:
                v_pairs(g, 0, EG // 4)
                sp.wait_ge(w_s, g * EG + EG)
                for v in range(2):
                    sp.wait_ge(h_st[v], 16 * (NKEY // 4))
                group_in(g + 1)
                v_pairs(g, EG // 4, EG // 2)
            with sp.Fori(NG - 1, NG) as g:
                v_pairs(g, 0, EG // 2)
            for k in range(0, KT, 2):
                sp.wait_ge(n2_out, k + 2)
                sp.dma_start(y_out[:, k:k + 2], acc[:, k:k + 2]).then_inc(y_st, 16)
            sp.wait_ge(y_st, 16 * (KT // 2))

        @block.gpsimd
        def _(pool):
            nc.gpsimd.memset(ones[:], 1.0).then_inc(ones_set, 1)

            def lo(n, u, freed):
                pool.wait_ge(whi, n + 1)
                if freed is not None:
                    pool.wait_ge(mm, freed)
                nc.gpsimd.tensor_tensor(wl[:, u], wraw[:, u], f(wh[:, u]), ALU.subtract).then_inc(wlo, 1)

            for u in range(2):
                lo(u, u, None)
            def lo_pairs(i0, i1):
                with pool.Fori(i0, i1) as i:
                    for u in range(2):
                        lo(i * 2 + u, u, i * 2 + (u - 1))

            lo_pairs(1, A_OUT // 2 + 1)
            for c in range(CT):
                pool.wait_ge(mixh_s, c + 3)
                nc.gpsimd.tensor_tensor(ml[:, c], yf[:, c], f(mh[:, c]), ALU.subtract).then_inc(mixc_s, 1)
            lo_pairs(A_OUT // 2 + 1, A_Q // 2 + 1)
            for k in range(KT):
                pool.wait_ge(x2h_s, k + 1)
                nc.gpsimd.tensor_tensor(xl[:, k], x2t[k % 4][:], f(xh[:, k]), ALU.subtract).then_inc(x2_s, 1)
            lo_pairs(A_Q // 2 + 1, A_V // 2 + 1)
            with pool.Fori(1, NKEY // 2) as i:
                for u in range(2):
                    lo(i * 2 + (A_V + u), u, i * 4 + (A_V + 2 * u - 2))
            pool.wait_ge(root_s, HEADS + 3)
            for i, k in enumerate(POOL_K):
                nc.gpsimd.tensor_tensor(acc[:, k], acc[:, k], fsum1[:], ALU.subtract).then_inc(n2_pool, 1)
                pool.wait_ge(n2_pool, 2 * i + 1)
                nc.gpsimd.tensor_tensor(acc[:, k], acc[:, k], fsum2[:], ALU.mult).then_inc(n2_pool, 1)

        @block.tensor
        def _(pe):
            mat = nc.tensor.matmul

            def job(u, n, ah, al, out, waits, first_k=None, ks=range(KT), begin=True, end=True):
                if begin:
                    pe.wait_ge(wlo, n + 1)
                    for s, v in waits:
                        pe.wait_ge(s, v)
                for k in ks:
                    if first_k:
                        first_k(k)
                    for w, m in ((wh, ah), (wh, al), (wl, ah)):
                        for h in range(2):
                            ins = mat(out[:, h], w[:, u, k], m[:, k, halves[h]],
                                      start=(begin and k == ks[0] and w is wh and m is ah),
                                      stop=(end and k == ks[-1] and w is wl))
                if end:
                    ins.then_inc(mm, 1)

            pe.sem_inc(g_mm, AHEAD)
            pe.wait_ge(wf_in, 16)
            for k in range(KT):
                if k % 4 == 0:
                    pe.wait_ge(x_in[k // 4], 16)
                for h in range(2):
                    ins = mat(ps[0:RANK, 4 + h, 0:TH], wf_raw[:, k], x_raw[:, k, halves[h]],
                              start=(k == 0), stop=(k == KT - 1))
            ins.then_inc(f_mm, 1)

            def mean_mm(s1, s2, b, wait, value, done):
                pe.wait_ge(wait, value)
                for j, s in enumerate((s1, s2)):
                    for i in range(2):
                        ins = mat(ps[:, b + 2 * j + i, 0:TH], ones[:], s[:, halves[i]], start=True, stop=True)
                ins.then_inc(done, 1)

            def conv_waits(c, gate):
                if c % 2:
                    return [(sg_s if gate else glu_s, c)]
                return [(z_out, 3 * c if gate else 3 * c - 1)] if c else []

            def conv_piece(h, i):
                if h + 1 == HEADS:
                    return
                c, gate, q = 2 * h + 2 + i // 8, i // 4 % 2, i % 4
                job(gate, n_conv(c) + gate, xh, xl, zr(gate), conv_waits(c, gate),
                    ks=range(4 * q, 4 * q + 4), begin=(q == 0), end=(q == 3))

            def head_job(h, j, **part):
                w = [(z_out, 6 * h + j - 1)] if j >= 2 else [((glu_s, sg_s)[j], 2 * h + 2)]
                job(j % 2, n_head(h, j), xh, xl, zr(j % 2), w, **part)

            def vg_pieces(h, i):
                j, q = 2 + i // 2, i % 2
                head_job(h, j, ks=range(8 * q, 8 * q + 8), begin=(q == 0), end=(q == 1))

            def gla(h):
                q, k = z[:, 0], z[:, 1]
                pe.wait_ge(f_out, 1)
                pe.wait_ge(consts_in, 16 * 9)
                if h:
                    pe.wait_ge(inv_s, h)
                for i in range(2):
                    ins = mat(ps[:, 4 + i, 0:TH], gw[:, h], flr[:, halves[i]], start=True, stop=True)
                ins.then_inc(gz_mm, 1)
                head_job(h, 1)
                vg_pieces(h, 0)
                for l in range(7):
                    b = 4 + 2 * (l % 2)
                    a, m = (ke[l % 2], qe[l % 2]) if l < 6 else (z[:, 1], z[:, 0])
                    if l < 6:
                        pe.wait_ge(qke, 6 * h + l + 1)
                    if l == 0:
                        pe.wait_ge(gz_ra, h + 1)
                        pe.wait_ge(gz_rd, h + 1)
                    if l >= 2:
                        pe.wait_ge(sc_out, 7 * h + l - 1)
                    for c, t0, n in chunks:
                        if c == NC and l == 0:
                            continue
                        bank, col = (b, c * CH) if c < NC else (b + 1, 0)
                        ins = mat(ps[0:n, bank, col:col + n], a[:, t0:t0 + n], m[:, t0:t0 + n],
                                  start=True, stop=True)
                    ins.then_inc(sc_mm, 1)
                    vg_pieces(h, l + 1)
                pe.wait_ge(z_out, 6 * h + 4)
                pe.wait_ge(sc_out, 7 * h + 7)
                for c in range(NC):
                    for v in range(2):
                        col = (c % 2) * DV + v * P
                        ins = nc.tensor.transpose(ps[0:CH, 4 + c // 2, col:col + P],
                                                  z[:, 2 + v, c * CH:(c + 1) * CH], ident[:])
                ins.then_inc(vt_mm, 1)
                conv_piece(h, 0)
                pe.wait_ge(vt_out, 2 * h + 1)
                for v in range(2):
                    ins = nc.tensor.transpose(ps[0:TS, 4, v * P:v * P + P], z[:, 2 + v, TP:T], ident[:])
                ins.then_inc(vt_mm, 1)
                conv_piece(h, 1)
                pe.wait_ge(kd_s, h + 1)
                pe.wait_ge(vt_out, 2 * h + 2)
                for c, t0, n in chunks:
                    ins = nc.tensor.transpose(ps[0:n, 4 + c // 4, (c % 4) * P:(c % 4) * P + P],
                                              ke[0][:, t0:t0 + n], ident[:])
                ins.then_inc(kt_mm, 1)
                conv_piece(h, 2)
                pe.wait_ge(kt_out, h + 1)
                for c in range(NC):
                    ins = mat(ps[:, 4 + c // 2, (c % 2) * DV:(c % 2 + 1) * DV], kdN[:, c], vN[:, c],
                              start=True, stop=True)
                ins.then_inc(p_mm, 1)
                conv_piece(h, 3)
                pe.wait_ge(p_out, 2 * h + 1)
                mat(ps[:, 4, 0:DV], kdN[0:TS, NC], vN[0:TS, NC], start=True, stop=True).then_inc(p_mm, 1)
                conv_piece(h, 4)
                conv_piece(h, 5)
                pe.wait_ge(qb_s, h + 1)
                pe.wait_ge(p_out, 2 * h + 2)
                for v in range(2):
                    for c, t0, n in chunks:
                        o_ps = ps[:, 4 + v, t0:t0 + n] if c < NC else ps[:, 6, v * TS:(v + 1) * TS]
                        vs_ = slice(v * P, (v + 1) * P)
                        ins = mat(o_ps, vN[0:n, c, vs_], scT[0:n, c, 0:n], start=True, stop=(c == 0))
                        if c:
                            ins = mat(o_ps, state[:, c % NC, vs_], qe[1][:, t0:t0 + n], start=False, stop=True)
                ins.then_inc(o_mm, 1)
                conv_piece(h, 6)
                conv_piece(h, 7)
                if h == HEADS - 1:
                    pe.wait_ge(z_out, NZ)
                    mean_mm(csum1, csum2, 0, cst_s, 1, cmean_mm)
                pe.wait_ge(o_out, h + 1)
                for i in range(2):
                    for v in range(2):
                        ins = mat(ps[:, 4 + i, 0:TH], ones[:], ke[v][:, halves[i]], start=(v == 0), stop=(v == 1))
                ins.then_inc(rs_mm, 1)
                for i in range(8, 16):
                    conv_piece(h, i)

            pe.wait_ge(x_lo, 4)
            pe.wait_ge(ones_set, 1)
            for c in range(2):
                for gate in range(2):
                    job(gate, n_conv(c) + gate, xh, xl, zr(gate), conv_waits(c, gate))
            for h in range(HEADS):
                head_job(h, 0)
                gla(h)

            def w_out_k(k):
                if k >= CT:
                    pe.wait_ge(mix_s, 1 + (k >= 12))
                else:
                    pe.wait_ge(mixc_s, k + 1)
            for u in range(2):
                job(u, A_OUT + u, mh, ml, zr(u), [(stat_s, 1)], w_out_k, ks=range(CT, KT), end=False)
            for k in range(CT):
                for u in range(2):
                    job(u, A_OUT + u, mh, ml, zr(u), [], w_out_k, ks=range(k, k + 1), begin=False, end=(k == CT - 1))
            with pe.Fori(1, NO // 2) as i:
                for u in range(2):
                    job(u, i * 2 + (A_OUT + u), mh, ml, zr(u), [(r_s, i * 2 + (u - 1))])
            mean_mm(sum1, sum2, 4, rst_s, 1, rmean_mm)

            def x2_k(k):
                pe.wait_ge(x2_s, k + 1)

            def q_job(u, n):
                job(u, n + A_Q, xh, xl, zr(u), [(q_out, n - 1)])

            def key_scores(u, n):
                pe.wait_ge(q_out, n + 1)
                if not (isinstance(n, int) and n < 2):
                    pe.wait_ge(s_out, n - 1)
                for tt in range(TT):
                    m = P if tt < 4 else TS
                    o_ps = ps[0:m, 4 + 2 * u, tt * P:tt * P + P] if tt < 4 else ps[0:m, 5 + 2 * u, 0:P]
                    key = skT[:, n] if isinstance(n, int) else skT[:, bass.ds(n, 1)].rearrange("p o c -> p (o c)")
                    ins = mat(o_ps, qT[:, u, tt * P:tt * P + m], key, start=True, stop=True)
                ins.then_inc(s_mm, 1)

            for k in range(KT):
                for u in range(2):
                    job(u, A_Q + u, xh, xl, zr(u), [(r_s, NO)], x2_k, ks=range(k, k + 1), begin=(k == 0),
                        end=(k == KT - 1))
            pe.wait_ge(keys_in, 16)
            key_scores(0, 0)
            with pe.Fori(1, NQ // 2) as i:
                q_job(0, i * 2)
                key_scores(1, i * 2 - 1)
                q_job(1, i * 2 + 1)
                key_scores(0, i * 2)
            key_scores(1, NQ - 1)

            def u_tile(n, u):
                job(u, n + A_U, xh, xl, zr(u), [(h_out, n + 1)])

            def g_group(q, v, bank):
                pe.wait_ge(oneh, q + 1)
                pe.wait_ge(g_out, q + 1)
                for t in range(4):
                    o_ps = ps[:, bank, t * P:(t + 1) * P]
                    for a in range(3):
                        ins = mat(o_ps, oneB[:, v, t], oneA[a][:, v, t], start=(a == 0), stop=(a == 2))
                ins.then_inc(g_mm, 1)

            pe.wait_ge(q_out, NQ)
            with pe.Fori(0, U_A) as i:
                for w in range(4):
                    u_tile(i * 4 + w, w % 2)

            pe.wait_ge(picks_s, 1)
            pe.wait_ge(s_out, NQ)
            for a in range(3):
                for tt in range(TT):
                    m = P if tt < 4 else TS
                    src = picks[0:m, a, tt].rearrange("p h k -> p (h k)")
                    col = a * 4 * P + tt * P
                    dst = ps[:, 4 + a, tt * P:tt * P + m] if tt < 4 else ps[:, 7, a * TS:a * TS + m]
                    ins = nc.tensor.transpose(dst, src, ident[0:m, 0:m])
            ins.then_inc(pt_mm, 1)

            pe.wait_ge(pt_out, 1)
            with pe.Fori(0, U_B) as i:
                for w in range(4):
                    u_tile(i * 4 + (4 * U_A + w), w % 2)
                    for q in range(2):
                        g_group(i * 8 + (2 * w + q), q, 4 + (2 * w + q) % 4)
            with pe.Fori(0, U_C) as i:
                for w in range(4):
                    u_tile(i * 4 + (4 * (U_A + U_B) + w), w % 2)

            def v_products(v, u, d, e):
                for w, m in ((wh, Wh[v]), (wh, Wl[v]), (wl, Wh[v])):
                    for h in range(2):
                        ins = mat(yr(d)[:, h], w[:, u, d * EG + e], m[:, e, halves[h]],
                                  start=(e == 0 and w is wh and m is Wh[v]), stop=(e == EG - 1 and w is wl))
                return ins

            def v_tile(g, v, i, u):
                pe.wait_ge(wlo, (g * EG + (A_V + u + 1)) + i * 2)
                pe.wait_ge(w_s, g * EG + EG)
                for d in range(2):
                    pe.wait_ge(y_add, g * KT + (i * 4 + (2 * u + d + 1)))
                    for e in range(EG):
                        ins = v_products(v, u, d, e)
                    ins.then_inc(mm, 1)

            def v_group(g, v, i0=0):
                with pe.Fori(i0, EG // 2) as i:
                    for u in range(2):
                        v_tile(g, v, i, u)

            pe.wait_ge(acc_set, 1)
            pe.wait_ge(wlo, A_V + 1)
            pe.wait_ge(y_add, AHEAD)
            for e in range(EG):
                pe.wait_ge(w_s, e + 1)
                for d in range(2):
                    ins = v_products(0, 0, d, e)
                    if e == EG - 1:
                        ins.then_inc(mm, 1)
            v_tile(0, 0, 0, 1)
            v_group(0, 0, 1)
            v_group(1, 1)
            with pe.Fori(1, NG // 2) as g:
                for v in range(2):
                    v_group(g * 2 + v, v)
            mean_mm(fsum1, fsum2, 4, n2_st, 1, n2_mm)

        @block.scalar
        def _(a):
            C = Counts(a)
            go = nc.scalar.activation

            def hi(n, u, freed):
                a.wait_ge(w_in_s[u], n * 8 + (16 - 8 * u))
                if freed is not None:
                    a.wait_ge(mm, freed)
                go(wh[:, u], wraw[:, u], ACT.Copy).then_inc(whi, 1)

            a.sem_inc(g_out, 4)
            a.sem_inc(h_out, AHEAD)
            a.sem_inc(g_st[1], 16)
            for i in range(4):
                a.wait_ge(x_in[i], 16)
                go(xh[:, 4 * i:4 * i + 4], x_raw[:, 4 * i:4 * i + 4], ACT.Copy).then_inc(x_hi, 1)
            hi(0, 0, None)
            hi(1, 1, None)
            a.wait_ge(f_mm, 1)
            go(parts(flr[:]), ps[0:RANK, 4:6, 0:TH], ACT.Copy).then_inc(f_out, 1)
            a.wait_ge(consts_in, 16 * 9)

            def root(buf, n):
                a.wait_ge(inv_s, n + 1)
                go(buf[:], buf[:], ACT.Sqrt).then_inc(root_s, 1)

            def gla_state_in(h):
                a.dma_start(state[:, 0], gla_state[:, h]).then_inc(gs_in, 16)

            gla_state_in(0)

            a.wait_ge(x_lo, 4)
            a.dma_start(cst[:], conv_state).then_inc(cst_in, 16)

            def conv_value(c):
                n = n_conv(c)
                a.wait_ge(mm, n + 1)
                hi(n + 2, 0, None)

            def conv_gate(c):
                n, e = n_conv(c) + 1, c % 2
                a.wait_ge(mm, n + 1)
                if c >= 2:
                    a.wait_ge(yf_s, c - 1)
                go(ext[:, e, NPAD:NPAD + TH], ps[:, 2, 0:TH], ACT.Sigmoid)
                go(ext[:, e, NPAD + TH:e_state], ps[:, 3, 0:TP - TH], ACT.Sigmoid)
                go(ext[:, e, e_sample:EXT], ps[:, 3, TP - TH:TH], ACT.Sigmoid).then_inc(sg_s, 1)
                hi(n + 2, 1, None)

            def conv_square(c):
                a.wait_ge(yf_s, c + 1)
                a.dma_start(yf_dram[c], yfb[:, c % 2]).then_inc(yf_st, 16)
                if c:
                    a.wait_ge(csq_u, c)
                go(csq[:], yfb[:, c % 2], ACT.Square).then_inc(csq_s, 1)

            for c in range(2):
                conv_value(c)
                conv_gate(c)

            def evict(h, j):
                n = n_head(h, j)
                a.wait_ge(mm, n + 1)
                if h:
                    a.wait_ge(head_out, h)
                if h and j == 2:
                    a.wait_ge(hf_st, 16 * h)
                go(parts(z[:, j]), zr(j % 2), ACT.Silu if j >= 4 else ACT.Copy,
                   scale=DK ** -0.5 if j == 0 else 1.0).then_inc(z_out, 1)
                hi(n + 2, j % 2, n + 1)

            def decay(h, l):
                a.wait_ge(dist_s, 7 * h + l + 1)
                n = TP if l == 0 else T
                go(dist[l % 2][:, 0:n], dist[l % 2][:, 0:n], ACT.Exp, scale=1.0 / TAU).then_inc(decay_s, 1)

            def gla(h):
                nxt = 2 * h + 2 if h + 1 < HEADS else None
                if h:
                    a.wait_ge(head_out, h)
                    a.dma_start(hf_dram[:, 2 * h - 2:2 * h], z[:, 2:4]).then_inc(hf_st, 16)
                evict(h, 0)
                a.wait_ge(gz_mm, h + 1)
                C.done(go(parts(qe[0][:]), yr(0), ACT.Abs, bias=gb[:, h:h + 1]), gz_ra)
                C.done(go(qe[0][:], qe[0][:], ACT.Exp, scale=-1.0), act)
                go(qe[0][:], qe[0][:], ACT.Ln, bias=1.0).then_inc(soft, 1)
                conv_square(2 * h)
                decay(h, 0)
                decay(h, 1)
                evict(h, 1)
                decay(h, 2)
                evict(h, 2)
                decay(h, 3)
                decay(h, 4)
                evict(h, 3)
                decay(h, 5)
                a.wait_ge(sc_mm, 7 * h + 5)
                go(qe[0][:], bcum[:], ACT.Exp, scale=1.0 / TAU).then_inc(decay_s, 1)
                evict(h, 4)
                a.wait_ge(dist_s, 7 * h + 7)
                go(dist[0][:], dist[0][:], ACT.Exp, scale=1.0 / TAU).then_inc(decay_s, 1)
                evict(h, 5)
                a.wait_ge(vt_mm, 2 * h + 1)
                go(vN[:, 0:NC].rearrange("p (b c) v -> p b (c v)", c=2), ps[0:CH, 4:8, :], ACT.Copy).then_inc(vt_out, 1)
                a.wait_ge(vt_mm, 2 * h + 2)
                go(vN[0:TS, NC], ps[0:TS, 4, 0:DV], ACT.Copy).then_inc(vt_out, 1)
                a.wait_ge(kt_mm, h + 1)
                go(kdN[:, 0:NC].rearrange("p (b c) v -> p b (c v)", c=4), ps[0:CH, 4:6, :], ACT.Copy)
                go(kdN[0:TS, NC], ps[0:TS, 6, 0:P], ACT.Copy).then_inc(kt_out, 1)
                if nxt:
                    conv_value(nxt)
                a.wait_ge(p_out, 2 * h + 2)
                a.dma_start(gla_p[:, h], state[:, NC]).then_inc(st_out, 16)
                a.dma_start(gla_s[:, h], s_new[:]).then_inc(st_out, 16)
                conv_square(2 * h + 1)
                if not nxt:
                    a.dma_start(conv_p, cpo[:, 0]).then_inc(cst_out, 16)
                    a.dma_start(conv_s, cpo[:, 1]).then_inc(cst_out, 16)
                a.wait_ge(o_mm, h + 1)
                if h + 1 < HEADS:
                    gla_state_in(h + 1)
                for v in range(2):
                    go(z[:, 2 + v, 0:TP], ps[:, 4 + v, :], ACT.Copy)
                    go(ke[v][:, 0:TP], ps[:, 4 + v, :], ACT.Square)
                go(z[:, 2:4, TP:T], ps[:, 6, 0:2 * TS].rearrange("p (v t) -> p v t", v=2), ACT.Copy)
                for v in range(2):
                    ins = go(ke[v][:, TP:T], ps[:, 6, v * TS:(v + 1) * TS], ACT.Square)
                ins.then_inc(o_out, 1)
                if not nxt:
                    root(csum2, h)
                    a.wait_ge(yf_st, 16 * CT)
                    a.dma_start(hf[:, 0:CT - 2], hf_dram).then_inc(hf_in, 16)
                    a.wait_ge(st_out, 32 * HEADS)
                    for i in range(2):
                        r = slice(i * CT // 2, (i + 1) * CT // 2)
                        a.dma_start(yf[:, r], yf_dram[r].rearrange("c p t -> p c t")).then_inc(yf_in[i], 16)
                else:
                    conv_gate(nxt)
                root(qe[0], h if nxt else h + 1)
                if nxt:
                    conv_value(nxt + 1)
                    conv_gate(nxt + 1)

            for h in range(HEADS):
                gla(h)

            a.wait_ge(head_out, HEADS)
            a.wait_ge(cst_out, 32)
            a.wait_ge(stat_s, 1)
            for i in range(2):
                a.wait_ge(hf_in, 16)
                go(mh[:, CT + 4 * i:CT + 4 * i + 4], hf[:, 4 * i:4 * i + 4], ACT.Copy).then_inc(mixh_s, 1)
            for c in range(CT + 1):
                if c < CT:
                    a.wait_ge(ycn_s, c + 1)
                    go(yf[:, c], yf[:, c], ACT.Silu, scale=cvec[:, 1, c:c + 1],
                       bias=cvec[:, 2, c:c + 1]).then_inc(ysilu_s, 1)
                if c:
                    a.wait_ge(ysilu_s, c)
                    go(mh[:, c - 1], yf[:, c - 1], ACT.Copy).then_inc(mixh_s, 1)

            with C.loop(NO // 2, {}) as i:
                for u in range(2):
                    n = i * 2 + u
                    a.wait_ge(mm, n + (A_OUT + 1))
                    hi(n + (A_OUT + 2), u, None)
                    a.wait_ge(r_s, n + 1)
                    a.wait_ge(rsq_u, n + 1)
                    go(sq[:], r1[:, bass.ds(n, 1)].rearrange("p o t -> p (o t)"), ACT.Square).then_inc(rsq_s, 1)

            root(sum2, HEADS + 1)
            for k in range(KT + 1):
                if k < KT:
                    a.wait_ge(x2n_s, k + 1)
                    go(x2t[k % 4][:], x2t[k % 4][:], ACT.Identity, scale=lvec[:, 0, k:k + 1],
                       bias=lvec[:, 1, k:k + 1]).then_inc(x2a_s, 1)
                if k:
                    a.wait_ge(x2a_s, k)
                    go(xh[:, k - 1], x2t[(k - 1) % 4][:], ACT.Copy).then_inc(x2h_s, 1)
            a.wait_ge(sc_set, 1)

            def q_evict(u, n, hi_next):
                a.wait_ge(mm, n + (A_Q + 1))
                if not (isinstance(n, int) and n < 2):
                    a.wait_ge(s_mm, n - 1)
                go(parts(qT[:, u]), zr(u), ACT.Copy).then_inc(q_out, 1)
                if hi_next:
                    hi(n + (A_Q + 2), u, None)

            def score_evict(n, slot, first=False):
                a.wait_ge(s_mm, n + 1)
                if not first:
                    a.wait_ge(topk_s, n - (SC - 1))
                go(sc[:, slot, 0:4].rearrange("p q k -> p (q k)"), ps[:, 4 + 2 * (slot % 2), :], ACT.Copy)
                go(sc[0:TS, slot, 4], ps[0:TS, 5 + 2 * (slot % 2), 0:P], ACT.Copy).then_inc(s_out, 1)

            for n in range(SC):
                q_evict(n % 2, n, True)
                if n:
                    score_evict(n - 1, n - 1, True)
            with a.Fori(1, NQ // SC) as i:
                for j in range(SC):
                    q_evict(j % 2, i * SC + j, True)
                    score_evict(i * SC + (j - 1), (j - 1) % SC)
            score_evict(NQ - 1, SC - 1)

            def u_tile(n, w, first):
                a.wait_ge(mm, n + (A_U + 1))
                if w % 2 == 0 and not first:
                    a.wait_ge(h_st[w // 2], (n - w) * 4)
                C.done(go(parts(hb[:, w // 2, w % 2]), zr(w % 2), ACT.Gelu), h_out)
                hi(n + (A_U + 2), w % 2, None)

            def h_store(i, w):
                d = h_dram[bass.ds(i * 2 + w // 2, 1)] if not isinstance(i, int) else h_dram[2 * i + w // 2:2 * i + w // 2 + 1]
                a.dma_start(d.rearrange("o p u t -> (o p) u t"), hb[:, w // 2]).then_inc(h_st[w // 2], 16)

            def u_four(i, first=False):
                for w in range(4):
                    u_tile(i * 4 + w, w, first)
                    if w % 2:
                        h_store(i, w)

            C.base[h_out.name] = AHEAD
            u_four(0, True)
            with C.loop(U_A - 2, {h_out: 4}) as i:
                u_four(i + 1)
            a.wait_ge(gd_s, 1)
            go(picks[:, 0], picks[:, 0], ACT.Exp).then_inc(ge_s, 1)
            u_four(U_A - 1)
            a.wait_ge(pt_mm, 1)
            for j in range(3):
                go(picksT[:, j, 0:TP], ps[:, 4 + j, :], ACT.Copy)
            go(picksT[:, :, TP:T], ps[:, 7, 0:3 * TS].rearrange("p (a t) -> p a t", a=3), ACT.Copy).then_inc(pt_out, 1)

            def g_evict(c, b, q, stored):
                a.wait_ge(g_mm, c * 8 + (q + 1 + AHEAD))
                if q == 0 and stored is not None:
                    a.wait_ge(g_st[b], stored)
                C.done(go(gst[b][:, :, 4 * q:4 * q + 4].rearrange("p i t -> p t i"),
                          ps[:, 4 + q % 4, :].rearrange("p (t i) -> p t i", t=4), ACT.Copy), g_out)

            def u_and_g(c, b, stored=None):
                for w in range(4):
                    u_tile((c + U_A) * 4 + w, w, False)
                    if w % 2:
                        h_store(c + U_A, w)
                    for q in range(2):
                        g_evict(c, b, 2 * w + q, stored)
                d = g_dram[bass.ds(c, 1)].rearrange("o j i t -> (o j) i t") if not isinstance(c, int) else g_dram[c]
                a.dma_start(d, gst[b][:]).then_inc(g_st[b], 16)

            C.base[g_out.name] = 4
            u_and_g(0, 0)
            assert U_B % 2 == 1
            with C.loop(U_B // 2, {h_out: 8, g_out: 16}) as i:
                for b in (1, 0):
                    u_and_g(i * 2 + (2 - b), b, i * 16 + 16)
            with C.loop(U_C, {h_out: 4}) as i:
                u_four(i + (U_A + U_B))
            for e in range(EG):
                a.wait_ge(wp_s, e + 1)
                go(Wh[0][:, e], wt[e % 2][:], ACT.Copy).then_inc(wh_s, 1)
            with a.Fori(0, (NG - 1) * EG // 2) as i:
                for u in range(2):
                    hi(i * 2 + (A_V + u + 2), u, i * 4 + (A_V + 2 * u + 2))
            for m in range(EG):
                n = (NG - 1) * EG + m
                if m + 2 < EG:
                    hi(A_V + n + 2, m % 2, A_V + 2 * n + 2)
                for k in (2 * m, 2 * m + 1):
                    a.wait_ge(y_add, AHEAD + (NG - 1) * KT + k + 1)
                    if k >= 2:
                        a.wait_ge(n2_used, k - 1)
                    go(fsq[k % 2][:], acc[:, k], ACT.Square).then_inc(n2_sq, 1)
            root(fsum2, HEADS + 2)
            for k in range(KT):
                if k in POOL_K:
                    a.wait_ge(n2_pool, 2 * POOL_K.index(k) + 2)
                else:
                    a.wait_ge(n2_dve, k + 1 - len([j for j in POOL_K if j < k]))
                go(acc[:, k], acc[:, k], ACT.Identity, scale=lvec[:, 2, k:k + 1],
                   bias=lvec[:, 3, k:k + 1]).then_inc(n2_out, 1)
            a.wait_ge(y_st, 16 * (KT // 2))
            a.wait_ge(st_out, 32 * HEADS)
            a.wait_ge(cst_out, 32)
            for v in range(2):
                a.wait_ge(g_st[v], 16 * (NGC // 2 + 1))
            for v in range(2):
                a.wait_ge(h_st[v], 16 * (NKEY // 4))

        @block.vector
        def _(v_):
            C = Counts(v_)
            tt_, ts_, stt_, cp = (nc.vector.tensor_tensor, nc.vector.tensor_scalar,
                                  nc.vector.scalar_tensor_tensor, nc.vector.tensor_copy)

            def one(ap):
                return ap.rearrange("p o t -> p (o t)")

            v_.sem_inc(y_add, AHEAD)
            C.base[y_add.name] = AHEAD
            v_.sem_inc(rsq_u, 1)
            C.base[rsq_u.name] = 1
            for i in range(4):
                s = slice(4 * i, 4 * i + 4)
                v_.wait_ge(x_hi, i + 1)
                C.inc(tt_(xl[:, s], x_raw[:, s], f(xh[:, s]), ALU.subtract), x_lo)
            v_.wait_ge(x_lo, 4)
            v_.wait_ge(f_mm, 1)
            C.done(nc.vector.memset(keep[:], 1.0), dve)
            nc.vector.memset(keep[:, 0:TP:CH], 0.0)
            nc.vector.memset(keep[:, TP:TP + 1], 0.0)
            C.done(nc.vector.memset(scT[:], 0.0), dve)
            v_.wait_ge(consts_in, 16 * 9)

            def blocks(ap, l):
                m = LEVELS[l]
                n = (TP if m == CH // 2 else T) // (2 * m)
                return ap[:, 0:n * 2 * m].rearrange("p (n two m) -> p n two m", two=2, m=m), n, m

            def gla(h):
                q, k, c1 = z[:, 0], z[:, 1], 2 * h + 1
                v_.wait_ge(gz_ra, h + 1)
                C.done(ts_(parts(bcum[:]), yr(0), gb[:, h:h + 1], 0.0, ALU.add, ALU.min), gz_rd)
                conv_add_square(c1 - 1)
                conv_rows(c1)
                conv_taps(c1, 0, 4)
                v_.wait_ge(soft, h + 1)
                C.done(tt_(ke[0][:], bcum[:], qe[0][:], ALU.subtract), dve)
                C.done(nc.vector.tensor_tensor_scan(bcum[:], keep[:], ke[0][:], 0.0, ALU.mult, ALU.add), dve)

                def distances(l):
                    b, n, m = blocks(bcum, l)
                    d, _, _ = blocks(dist[l % 2], l)
                    mid = b[:, :, 0, m - 1:m].to_broadcast([P, n, m])
                    tt_(d[:, :, 0], mid, b[:, :, 0], ALU.subtract)
                    C.done(tt_(d[:, :, 1], b[:, :, 1], mid, ALU.subtract), dist_s)

                def take_scores(l):
                    v_.wait_ge(sc_mm, 7 * h + l + 1)
                    b = 4 + 2 * (l % 2)
                    m8 = masks[:, l:l + 1].to_broadcast([CH, NC, CH])
                    src = ps[0:CH, b, :].rearrange("p (c t) -> p c t", c=NC)
                    if l == 0:
                        C.done(tt_(scT[:, 0:NC], src, m8, ALU.mult), sc_out)
                        return
                    tt_(stmp[:, 0:NC], src, m8, ALU.mult)
                    dst = scT if l == 1 else stmp
                    C.done(tt_(dst[0:TS, NC, 0:TS], ps[0:TS, b + 1, 0:TS], masks[0:TS, l, 0:TS], ALU.mult), sc_out)
                    ins = tt_(scT[:, 0:NC], scT[:, 0:NC], stmp[:, 0:NC], ALU.add)
                    if l > 1:
                        ins = tt_(scT[0:TS, NC, 0:TS], scT[0:TS, NC, 0:TS], stmp[0:TS, NC, 0:TS], ALU.add)
                    C.done(ins, dve)

                distances(0)
                conv_taps(c1, 4, 6)
                for l in range(6):
                    if l < 5:
                        distances(l + 1)
                    conv_taps(c1, 6 + 2 * l, 8 + 2 * l)
                    v_.wait_ge(decay_s, 8 * h + l + 1)
                    if l >= 2:
                        take_scores(l - 2)
                    if l == 0:
                        v_.wait_ge(z_out, 6 * h + 2)
                    n = TP if l == 0 else T
                    tt_(qe[l % 2][:, 0:n], q[:, 0:n], dist[l % 2][:, 0:n], ALU.mult)
                    C.done(tt_(ke[l % 2][:, 0:n], k[:, 0:n], dist[l % 2][:, 0:n], ALU.mult), qke)
                end = bcum[:, 0:TP].rearrange("p (c t) -> p c t", c=NC)
                tt_(dist[0][:, 0:TP].rearrange("p (c t) -> p c t", c=NC),
                    end[:, :, CH - 1:CH].to_broadcast([P, NC, CH]), end, ALU.subtract)
                C.done(tt_(dist[0][:, TP:T], bcum[:, T - 1:T].to_broadcast([P, TS]), bcum[:, TP:T], ALU.subtract),
                       dist_s)
                conv_taps(c1, 18, 20)
                take_scores(4)
                conv_taps(c1, 20, 22)
                take_scores(5)
                v_.wait_ge(decay_s, 8 * h + 7)
                C.done(tt_(qe[1][:], q, qe[0][:], ALU.mult), qb_s)
                conv_taps(c1, 22, 24)
                take_scores(6)
                v_.wait_ge(decay_s, 8 * h + 8)
                C.done(tt_(ke[0][:], k, dist[0][:], ALU.mult), kd_s)
                conv_taps(c1, 24, CW)
                conv_end(c1)
                v_.wait_ge(p_mm, 2 * h + 1)
                v_.wait_ge(st_out, 32 * h)
                C.done(cp(state[:, 1], ps[:, 4, 0:DV]), dve)
                for c in range(1, NC):
                    e = c * CH + CH - 1
                    C.done(stt_(state[:, c + 1], state[:, c], qe[0][:, e:e + 1],
                                ps[:, 4 + c // 2, (c % 2) * DV:(c % 2 + 1) * DV], ALU.mult, ALU.add),
                           p_out if c == NC - 1 else dve)
                v_.wait_ge(gs_in, 16 * (h + 1))
                v_.wait_ge(p_mm, 2 * h + 2)
                C.done(stt_(s_new[:], state[:, 0], qe[0][:, T - 1:T], ps[:, 4, 0:DV], ALU.mult, ALU.add), p_out)
                conv_add_square(c1)
                if h == HEADS - 1:
                    v_.sem_inc(cst_s, 1)
                    v_.wait_ge(cmean_mm, 1)
                    norm_stats(CONV, csum1, csum2, csq, zr)
                else:
                    glu(c1 + 1)
                v_.wait_ge(rs_mm, h + 1)
                C.done(ts_(parts(qe[0][:]), yr(0), 1.0 / DV, EPS, ALU.mult, ALU.add), dve)
                C.done(nc.vector.reciprocal(qe[0][:], qe[0][:]), inv_s)
                v_.wait_ge(root_s, C.base[inv_s.name])
                for v in range(2):
                    C.done(stt_(z[:, 2 + v], z[:, 2 + v], ng[:, 2 * h + v:2 * h + v + 1], qe[0][:],
                                ALU.mult, ALU.mult), dve)
                v_.wait_ge(z_out, 6 * h + 6)
                for v in range(2):
                    j = 2 * h + v
                    to = hf[:, j] if h == HEADS - 1 else z[:, 2 + v]
                    C.done(tt_(to, z[:, 2 + v], z[:, 4 + v], ALU.mult), head_out if v else dve)

            def glu(c):
                e = c % 2
                v_.wait_ge(mm, n_conv(c) + 1)
                v_.wait_ge(sg_s, c + 1)
                for r, src in ((slice(NPAD, NPAD + TH), ps[:, 0, 0:TH]),
                               (slice(NPAD + TH, e_state), ps[:, 1, 0:TP - TH])):
                    tt_(ext[:, e, r], src, ext[:, e, r], ALU.mult)
                r = slice(e_sample, EXT)
                C.done(tt_(ext[:, e, r], ps[:, 1, TP - TH:TH], ext[:, e, r], ALU.mult), glu_s)

            def conv_rows(c):
                e = c % 2
                C.done(cp(ext[:, e, e_state:e_sample], cst[:, c]), dve)
                cp(cpo[:, 0, c], ext[:, e, TP:TP + NPAD])
                C.done(cp(cpo[:, 1, c], ext[:, e, EXT - NPAD:EXT]), dve)

            def conv_taps(c, w0, w1):
                for w in range(w0, w1):
                    y_, rows, tap = yb[w % 2], ext[:, c % 2, w:w + YL], cwt[:, c, w:w + 1]
                    if w == 0:
                        ins = ts_(y_[:], rows, tap, cvec[:, 0, c:c + 1], ALU.mult, ALU.add)
                    elif w == 1:
                        ins = ts_(y_[:], rows, tap, None, ALU.mult)
                    else:
                        ins = stt_(y_[:], rows, tap, y_[:], ALU.mult, ALU.add)
                    C.lag(ins, tap_s)

            def conv_end(c):
                e = c % 2
                if c and c % 2 == 0:
                    v_.wait_ge(yf_st, 16 * c)
                v_.wait_ge(tap_s, C.value(tap_s))
                tt_(yfb[:, e, 0:TP], yb[0][:, 0:TP], yb[1][:, 0:TP], ALU.add)
                C.done(tt_(yfb[:, e, TP:T], yb[0][:, e_state:YL], yb[1][:, e_state:YL], ALU.add), yf_s)
                C.done(tt_(csum1[:], csum1[:], yfb[:, e], ALU.add), dve)

            def conv_add_square(c):
                v_.wait_ge(csq_s, c + 1)
                C.done(tt_(csum2[:], csum2[:], csq[:], ALU.add), csq_u)

            def norm_stats(n, s1, s2, t, sums):
                C.done(ts_(parts(s1[:]), sums(0), 1.0 / n, None, ALU.mult), dve)
                C.done(tt_(t[:], s1[:], s1[:], ALU.mult), dve)
                C.done(stt_(parts(s2[:]), sums(1), 1.0 / n, parts(t[:]), ALU.mult, ALU.subtract), dve)
                C.done(ts_(s2[:], s2[:], 0.0, EPS, ALU.max, ALU.add), dve)
                C.done(nc.vector.reciprocal(s2[:], s2[:]), inv_s)
                v_.wait_ge(root_s, C.base[inv_s.name])

            v_.wait_ge(cst_in, 16)
            for e in range(2):
                nc.vector.memset(ext[:, e, 0:NPAD], 0.0)
            nc.vector.memset(csum1[:], 0.0)
            C.done(nc.vector.memset(csum2[:], 0.0), dve)
            glu(0)
            for h in range(HEADS):
                conv_rows(2 * h)
                conv_taps(2 * h, 0, CW // 2)
                glu(2 * h + 1)
                conv_taps(2 * h, CW // 2, CW)
                conv_end(2 * h)
                gla(h)

            cp(sum1[:], csum1[:])
            C.done(cp(sum2[:], csum2[:]), stat_s)
            for i in range(2):
                r = slice(CT + 4 * i, CT + 4 * i + 4)
                v_.wait_ge(mixh_s, i + 1)
                C.inc(tt_(ml[:, r], hf[:, 4 * i:4 * i + 4], f(mh[:, r]), ALU.subtract), mix_s)

            for c in range(0, CT, 2):
                v_.wait_ge(yf_in[c // (CT // 2)], 16)
                for d in range(2):
                    C.lag(tt_(yf[:, c + d], yf[:, c + d], sum1[:], ALU.subtract), dve)
                v_.wait_ge(dve, C.value(dve))
                for d in range(2):
                    C.inc(tt_(yf[:, c + d], yf[:, c + d], sum2[:], ALU.mult), ycn_s)
            v_.wait_ge(ycn_s, CT)
            v_.wait_ge(mix_s, 2)

            nc.vector.memset(sum1[:], 0.0)
            C.done(nc.vector.memset(sum2[:], 0.0), dve)
            with C.loop(NO // 2, {dve: 4, r_s: 2, rsq_u: 2}) as i:
                for u in range(2):
                    n = bass.ds(i * 2 + u, 1)
                    v_.wait_ge(mm, i * 2 + (A_OUT + u + 1))
                    C.done(stt_(parts(one(r1[:, n])), parts(one(f(xh[:, n]))), ALPHA, zr(u), ALU.mult, ALU.add), dve)
                    C.done(stt_(one(r1[:, n]), one(f(xl[:, n])), ALPHA, one(r1[:, n]), ALU.mult, ALU.add), r_s)
                    C.done(tt_(sum1[:], sum1[:], one(r1[:, n]), ALU.add), dve)
                    v_.wait_ge(rsq_s, i * 2 + (u + 1))
                    C.done(tt_(sum2[:], sum2[:], sq[:], ALU.add), rsq_u)
            v_.sem_inc(rst_s, 1)
            C.done(nc.vector.memset(sc[:], 0.0), sc_set)
            v_.wait_ge(rmean_mm, 1)
            norm_stats(D, sum1, sum2, tmp[0], yr)
            for k0 in range(0, KT, 2):
                for k in (k0, k0 + 1):
                    if k >= 4:
                        v_.wait_ge(x2_s, k - 3)
                    C.inc(tt_(x2t[k % 4][:], r1[:, k], sum1[:], ALU.subtract), dve)
                for k in (k0, k0 + 1):
                    v_.wait_ge(dve, C.value(dve) - (k == k0))
                    C.inc(tt_(x2t[k % 4][:], x2t[k % 4][:], sum2[:], ALU.mult), x2n_s)

            LOWEST = -3.0e38

            def top16(vals, work, best, num, used):
                for tt in range(TT):
                    ins = nc.vector.max(best[:, tt, 0:8], vals[:, tt])
                C.done(ins, dve)
                for tt in range(TT):
                    nc.vector.max_index(num[:, tt, 0:8], best[:, tt, 0:8], vals[:, tt])
                    ins = nc.vector.match_replace(work[:, tt], best[:, tt, 0:8], vals[:, tt], LOWEST)
                C.done(ins, used)
                for tt in range(TT):
                    ins = nc.vector.max(best[:, tt, 8:16], work[:, tt])
                C.done(ins, dve)
                for tt in range(TT):
                    ins = nc.vector.max_index(num[:, tt, 8:16], best[:, tt, 8:16], work[:, tt])
                C.done(ins, dve)

            for h in range(PH):
                for p in range(2):
                    v_.wait_ge(s_out, 2 * h + p + 1)
                    top16(sc[:, (2 * h + p) % SC], scw, sv[:, p], si[:, p], topk_s)
                C.done(cp(sif[:], si[:]), dve)
                s4 = [P, TT, 16, 16]
                C.done(tt_(cand[:].rearrange("p t (a b) -> p t a b", a=16),
                           sv[:, 0].unsqueeze(3).to_broadcast(s4), sv[:, 1].unsqueeze(2).to_broadcast(s4), ALU.add), dve)
                top16(cand, candw, bs, pos, dve)
                cp(picks[:, 0, :, h], bs[:])
                ts_(pab[:, 0], pos[:], 4, None, ALU.logical_shift_right)
                C.done(ts_(pab[:, 1], pos[:], 15, None, ALU.bitwise_and), dve)
                C.done(cp(pabf[:], pab[:]), dve)
                flat = [P, TT * 16, 16]
                oh3 = oh[:].rearrange("p t k a -> p (t k) a")
                for p in range(2):
                    at_ = pabf[:, p].rearrange("p t k -> p (t k)").unsqueeze(2).to_broadcast(flat)
                    C.done(tt_(oh3, at_, iota[:, 0:16].unsqueeze(1).to_broadcast(flat), ALU.is_equal), dve)
                    C.done(tt_(oh[:], oh[:], sif[:, p].unsqueeze(2).to_broadcast(s4), ALU.mult), dve)
                    C.done(nc.vector.tensor_reduce(picks[:, 1 + p, :, h], oh[:], AX, ALU.add), dve)

            g2 = picks[:, 0].rearrange("p t h k -> p (t h) k")
            C.done(cp(gsum[:], g2[:, :, 0]), dve)
            gs_b = gsum[:].unsqueeze(2).to_broadcast([P, TT * PH, 16])
            C.done(tt_(g2, g2, gs_b, ALU.subtract), gd_s)
            v_.wait_ge(ge_s, 1)
            C.done(nc.vector.tensor_reduce(gsum[:], g2, AX, ALU.add), dve)
            C.done(nc.vector.reciprocal(gsum[:], gsum[:]), dve)
            C.done(tt_(g2, g2, gs_b, ALU.mult), picks_s)

            v_.wait_ge(pt_out, 1)
            for a in range(2):
                C.done(cp(part[:], picksT[:, 0]), dve)
                C.done(cp(gate_p[a][:], part[:]), dve)
                out = gate_p[2][:] if a else picksT[:, 0]
                C.done(tt_(out, picksT[:, 0], gate_p[a][:], ALU.subtract), dve)
            with C.loop(T // 8, {oneh: 2}) as i:
                for u in range(2):
                    v_.wait_ge(g_mm, i * 2 + (u + 1))
                    for t in range(4):
                        tok = bass.ds(i * 8 + (4 * u + t), 1)
                        for a in range(3):
                            ts_(oneA[a][:, u, t], iota[:], picksT[:, 1, tok], gate_p[a][:, tok], ALU.is_equal, ALU.mult)
                        ins = ts_(oneB[:, u, t], iota[:], picksT[:, 2, tok], None, ALU.is_equal)
                    C.inc(ins, oneh)

            v_.wait_ge(g_mm, T // 4 + AHEAD)
            v_.wait_ge(g_st[1], 16 * (NGC // 2 + 1))
            with C.loop(KT, {dve: 2}) as k:
                kk = bass.ds(k, 1)
                C.done(ts_(one(acc[:, kk]), one(f(xh[:, kk])), ALPHA, None, ALU.mult), dve)
                C.done(stt_(one(acc[:, kk]), one(f(xl[:, kk])), ALPHA, one(acc[:, kk]), ALU.mult, ALU.add), dve)
            v_.sem_inc(acc_set, 1)

            def make_w(g, v, es):
                for j, e in enumerate(es):
                    v_.wait_ge(g_in, g * 16 + 16)
                    v_.wait_ge(h_in, g * 16 + 16)
                    gate = gt[:, :, e].rearrange("p c o t -> p c (o t)")
                    hh = one(hg[:, e]).rearrange("p (c t) -> p c t", c=NGC)
                    C.lag(tt_(wt[j][:].rearrange("p (c t) -> p c t", c=NGC), hh, gate, ALU.mult), dve)
                for j, e in enumerate(es):
                    C.lag(cp(one(Wh[v][:, e]), wt[j][:]), dve)
                v_.wait_ge(dve, C.value(dve))
                for j, e in enumerate(es):
                    C.inc(tt_(one(Wl[v][:, e]), wt[j][:], one(f(Wh[v][:, e])), ALU.subtract), w_s)
                v_.wait_ge(w_s, C.value(w_s))

            def add_y(g, i, u):
                for d in range(2):
                    v_.wait_ge(mm, (g * KT + (A_V + 2 * u + d + 1)) + i * 4)
                    dd = bass.ds(i * 4 + (2 * u + d), 1)
                    a_ = parts(one(acc[:, dd]))
                    C.done(tt_(a_, a_, yr(d), ALU.add), y_add)

            v_.wait_ge(mm, A_V)
            v_.wait_ge(g_in, 16)
            v_.wait_ge(h_in, 16)

            def w_lo(e):
                v_.wait_ge(wh_s, e + 1)
                C.inc(tt_(Wl[0][:, e], wt[e % 2][:], f(Wh[0][:, e]), ALU.subtract), w_s)

            for e in range(EG):
                if e >= 2:
                    v_.wait_ge(w_s, e - 1)
                C.inc(tt_(wt[e % 2][:].rearrange("p (c t) -> p c t", c=NGC),
                          hg[:, e].rearrange("p (c t) -> p c t", c=NGC), gt[:, :, e], ALU.mult), wp_s)
                if e:
                    w_lo(e - 1)
            w_lo(EG - 1)
            v_.wait_ge(w_s, EG)

            def v_group(g, v):
                with C.loop(EG // 4, {y_add: 4}) as i:
                    for u in range(2):
                        add_y(g, i, u)
                with C.loop(EG // 4, {y_add: 4, dve: 8, w_s: 4}) as i:
                    for u in range(2):
                        make_w(g + 1, 1 - v, [bass.ds(i * 4 + (2 * u + j), 1) for j in range(2)])
                        add_y(g, i + EG // 4, u)

            with C.loop(NG // 2 - 1, {y_add: 2 * KT, dve: 32, w_s: 2 * EG}) as g:
                for v in range(2):
                    v_group(g * 2 + v, v)
            v_group(NG - 2, 0)
            nc.vector.memset(fsum1[:], 0.0)
            C.done(nc.vector.memset(fsum2[:], 0.0), dve)
            for k in range(KT):
                v_.wait_ge(mm, A_V + (NG - 1) * KT + k + 1)
                a_ = parts(acc[:, k])
                C.done(tt_(a_, a_, yr(k % 2), ALU.add), y_add)
                C.done(tt_(fsum1[:], fsum1[:], acc[:, k], ALU.add), dve)
                v_.wait_ge(n2_sq, k + 1)
                C.done(tt_(fsum2[:], fsum2[:], fsq[k % 2][:], ALU.add), n2_used)
            v_.sem_inc(n2_st, 1)
            v_.wait_ge(n2_mm, 1)
            norm_stats(D, fsum1, fsum2, fsq[0], yr)
            for k in range(KT):
                if k not in POOL_K:
                    C.done(tt_(acc[:, k], acc[:, k], fsum1[:], ALU.subtract), dve)
                    C.inc(tt_(acc[:, k], acc[:, k], fsum2[:], ALU.mult), n2_dve)


def _tiles(w, cols):
    n = w.shape[1] // cols
    return np.ascontiguousarray(w.reshape(-1, P, n, cols).transpose(2, 1, 0, 3))


def _by_feature(a):
    return np.ascontiguousarray(a.T.reshape(-1, P, a.shape[0]).transpose(1, 0, 2))


def _level_masks():
    s, t = np.arange(CH)[:, None], np.arange(CH)[None, :]
    m = [((s // l) % 2 == 0) & (t // l == s // l + 1) for l in LEVELS] + [s == t]
    return np.ascontiguousarray(np.stack(m, 1).astype(np.float32))


def kernel(x_prompt, x_sample, state_conv, state_gla, w_in, conv_w, conv_b, conv_ln_g, conv_ln_b,
           gla_gate_w, gla_gate_b, gla_norm_g, w_out, ln1_g, ln1_b, peer_w_query, peer_sub_keys,
           peer_u, peer_v, ln2_g, ln2_b):
    import concourse.bacc as bacc
    from concourse.bass_utils import run_bass_kernel_spmd

    w_in = np.asarray(w_in)[0]
    QK, V = HEADS * DK, HEADS * DV
    o = np.cumsum([0, CONV, CONV, QK, QK, V, V])
    part = {n: _tiles(w_in[:, o[i]:o[i + 1]], P) for i, n in enumerate(["val", "gate", "q", "k", "v", "g"])}
    order = []
    for h in range(HEADS):
        for c in (2 * h, 2 * h + 1):
            order += [part["val"][c], part["gate"][c]]
        order += [part["q"][h], part["k"][h], part["v"][2 * h], part["v"][2 * h + 1],
                  part["g"][2 * h], part["g"][2 * h + 1]]

    def vec(a):
        return np.asarray(a)[0].reshape(-1, P).T

    pv = np.asarray(peer_v)[0].reshape(NG, EG, P, EG, 2, P).transpose(0, 3, 2, 4, 1, 5)
    ins = {
        "xT": _by_feature(np.concatenate([np.asarray(x_prompt)[0], np.asarray(x_sample)[0]], 0)),
        "w_in": np.stack(order),
        "w_f": _tiles(w_in[:, o[6]:], RANK)[0],
        "w_out": _tiles(np.asarray(w_out)[0], P),
        "w_q": _tiles(np.asarray(peer_w_query)[0], P),
        "u_t": np.ascontiguousarray(np.asarray(peer_u)[0].reshape(NKEY, P, KT, P).transpose(0, 3, 2, 1)),
        "v_t": np.ascontiguousarray(pv).reshape(NG * EG, P, KT, P),
        "conv_state": np.ascontiguousarray(np.asarray(state_conv)[0, 0].T.reshape(CT, P, NPAD).transpose(1, 0, 2)),
        "conv_w": np.ascontiguousarray(np.asarray(conv_w)[0].T.reshape(CT, P, CW).transpose(1, 0, 2)),
        "conv_vec": np.ascontiguousarray(np.stack([vec(conv_b), vec(conv_ln_g), vec(conv_ln_b)], 1)),
        "gla_state": np.ascontiguousarray(np.asarray(state_gla)[0, 0].transpose(1, 0, 2)),
        "gate_w": np.ascontiguousarray(np.asarray(gla_gate_w)[0].reshape(RANK, HEADS, P)),
        "gate_b": np.ascontiguousarray(vec(gla_gate_b)),
        "norm_g": np.ascontiguousarray(vec(gla_norm_g)),
        "ln_vec": np.ascontiguousarray(np.stack([vec(ln1_g), vec(ln1_b), vec(ln2_g), vec(ln2_b)], 1)),
        "sub_keys": np.ascontiguousarray(
            np.asarray(peer_sub_keys)[0].reshape(2 * PH, NKEY, P).transpose(2, 0, 1)),
        "ident": np.eye(P, dtype=np.float32),
        "iota": np.ascontiguousarray(np.broadcast_to(np.arange(P, dtype=np.float32), (P, P))),
        "masks": _level_masks(),
    }
    outs = {"y": (P, KT, T), "conv_p": (P, CT, NPAD), "conv_s": (P, CT, NPAD),
            "gla_p": (P, HEADS, DV), "gla_s": (P, HEADS, DV)}
    nc = bacc.Bacc("TRN2", target_bir_lowering=False, num_devices=1)
    args = [nc.dram_tensor("in_" + n, a.shape, F32, kind="ExternalInput").ap() for n, a in ins.items()]
    args += [nc.dram_tensor("out_" + n, s, F32, kind="ExternalOutput").ap() for n, s in outs.items()]
    args.append(nc.dram_tensor("g_scratch", (NGC, P, P, GC), F32, kind="Internal").ap())
    args.append(nc.dram_tensor("h_scratch", (NKEY // 2, P, 2, T), F32, kind="Internal").ap())
    args.append(nc.dram_tensor("conv_scratch", (CT, P, T), F32, kind="Internal").ap())
    args.append(nc.dram_tensor("head_scratch", (P, CT - 2, T), F32, kind="Internal").ap())
    program(nc, *args)
    r = run_bass_kernel_spmd(nc, [{"in_" + n: a for n, a in ins.items()}], core_ids=[0]).results[0]
    y = np.asarray(r["out_y"]).transpose(2, 1, 0).reshape(T, D)

    def rows(a):
        return np.ascontiguousarray(np.asarray(a).transpose(2, 1, 0).reshape(1, 1, NPAD, CONV))

    def states(a):
        return np.ascontiguousarray(np.asarray(a).transpose(1, 0, 2))[None, None]

    return (np.ascontiguousarray(y[None, :TP]), np.ascontiguousarray(y[None, TP:]),
            rows(r["out_conv_p"]), states(r["out_gla_p"]), rows(r["out_conv_s"]), states(r["out_gla_s"]))
```
